# Optimizing a Trainium2 kernel written in Bass

```python
import jax, jax.numpy as jnp
from jax import lax
import numpy as np
import math

D_MODEL = 2048
BATCH = 1
SEQ = 256
DEPTH = 2

N_EVEN = (DEPTH + 1) // 2
N_ODD = DEPTH // 2
N_MEM = 256
ROPE_THETA = 500000.0
ROT_FRAC = 4
EPS = 1e-6
Q_BLOCK = 128

MLA_HEADS = 8
MLA_Q_RANK = 512
MLA_KV_RANK = 256
MLA_NOPE = 128
MLA_ROPE = 64
MLA_V = 128
MOBA_HEADS = 8
MOBA_DH = 128
MOBA_BLOCK = 256
MOBA_TOPK = 3
MOBA_QCHUNK = 32
SWA_HEADS = 16
SWA_KV_HEADS = 2
SWA_DH = 64
SWA_WINDOW = 128
DIL_HEADS = 6
DIL_DH = 128
DIL_PATTERNS = ((128, 1), (512, 4), (2048, 16))
MEM_HEADS = 4
MEM_DH = 128

MEMQ_W = MEM_HEADS * MEM_DH
EVEN_VW = MLA_HEADS * MLA_V + MOBA_HEADS * MOBA_DH + MEMQ_W
EVEN_SPLITS = (MLA_Q_RANK, MLA_KV_RANK, MLA_ROPE, 3 * MOBA_HEADS * MOBA_DH, MEMQ_W, EVEN_VW)
EVEN_IN = sum(EVEN_SPLITS)
ODD_VW = SWA_HEADS * SWA_DH + DIL_HEADS * DIL_DH + MEMQ_W
ODD_SPLITS = ((SWA_HEADS + 2 * SWA_KV_HEADS) * SWA_DH, 3 * DIL_HEADS * DIL_DH, MEMQ_W, ODD_VW)
ODD_IN = sum(ODD_SPLITS)


def split_cols(h, sizes):
    return jnp.split(h, [int(i) for i in np.cumsum(sizes)[:-1]], axis=-1)

def rms_norm(x, g):
    xf = x.astype(jnp.float32)
    y = xf * lax.rsqrt(jnp.mean(xf * xf, axis=-1, keepdims=True) + EPS)
    return (y * g.astype(jnp.float32)).astype(x.dtype)

def apply_rope(x, rot_dim):
    S = x.shape[1]
    inv = 1.0 / (ROPE_THETA ** (jnp.arange(0, rot_dim, 2, dtype=jnp.float32) / rot_dim))
    ang = jnp.arange(S, dtype=jnp.float32)[:, None] * inv[None, :]
    c, s = jnp.cos(ang)[None, :, None, :], jnp.sin(ang)[None, :, None, :]
    xr = x[..., :rot_dim].astype(jnp.float32)
    x1, x2 = xr[..., : rot_dim // 2], xr[..., rot_dim // 2:]
    rot = jnp.concatenate([x1 * c - x2 * s, x1 * s + x2 * c], axis=-1).astype(x.dtype)
    return jnp.concatenate([rot, x[..., rot_dim:]], axis=-1)

def causal_attention_qblocks(q, k, v, scale):
    B, H, S, dq = q.shape
    nb = S // Q_BLOCK
    qb = q.reshape(B, H, nb, Q_BLOCK, dq).transpose(2, 0, 1, 3, 4)
    kpos = jnp.arange(S)

    def one(args):
        qi, n = args
        s = jnp.einsum('bhqd,bhkd->bhqk', qi, k).astype(jnp.float32) * scale
        qpos = n * Q_BLOCK + jnp.arange(Q_BLOCK)
        s = jnp.where(kpos[None, :] <= qpos[:, None], s, -jnp.inf)
        p = jax.nn.softmax(s, axis=-1).astype(v.dtype)
        return jnp.einsum('bhqk,bhkd->bhqd', p, v)

    o = lax.map(one, (qb, jnp.arange(nb)))
    return o.transpose(1, 2, 0, 3, 4).reshape(B, H, S, v.shape[-1])

def moba_attention(q, k, v):
    B, H, S, dh = q.shape
    L = MOBA_BLOCK
    nblk = -(-S // L)
    Sp = nblk * L
    pad = ((0, 0), (0, 0), (0, Sp - S), (0, 0))
    kb = jnp.pad(k, pad).reshape(B, H, nblk, L, dh)
    vb = jnp.pad(v, pad).reshape(B, H, nblk, L, dh)
    kmean = jnp.mean(kb.astype(jnp.float32), axis=3)
    topk = min(MOBA_TOPK, nblk - 1)
    scale = dh ** -0.5
    QC = MOBA_QCHUNK
    nc = S // QC
    qc = q.reshape(B, H, nc, QC, dh).transpose(2, 0, 1, 3, 4)
    offs = jnp.arange(L)
    gather = jax.vmap(jax.vmap(lambda t, i: t[i]))

    def one(args):
        qi, c = args
        blk = (c * QC) // L
        qpos = c * QC + jnp.arange(QC)
        k_own = lax.dynamic_index_in_dim(kb, blk, axis=2, keepdims=False)
        v_own = lax.dynamic_index_in_dim(vb, blk, axis=2, keepdims=False)
        s_own = jnp.einsum('bhqd,bhld->bhql', qi, k_own).astype(jnp.float32) * scale
        s_own = jnp.where((blk * L + offs)[None, :] <= qpos[:, None], s_own, -jnp.inf)
        if topk == 0:
            p = jax.nn.softmax(s_own, axis=-1).astype(v.dtype)
            return jnp.einsum('bhql,bhld->bhqd', p, v_own)
        gate = jnp.einsum('bhqd,bhnd->bhqn', qi.astype(jnp.float32), kmean)
        gate = jnp.where(jnp.arange(nblk) < blk, gate, -jnp.inf)
        _, idx = lax.top_k(gate, topk)
        valid = jnp.arange(topk) < blk
        kg = gather(kb, idx)
        vg = gather(vb, idx)
        s_sel = jnp.einsum('bhqd,bhqkld->bhqkl', qi, kg).astype(jnp.float32) * scale
        s_sel = jnp.where(valid[:, None], s_sel, -jnp.inf)
        s_all = jnp.concatenate([s_sel.reshape(B, H, QC, topk * L), s_own], axis=-1)
        p = jax.nn.softmax(s_all, axis=-1).astype(v.dtype)
        p_sel = p[..., : topk * L].reshape(B, H, QC, topk, L)
        return (jnp.einsum('bhqkl,bhqkld->bhqd', p_sel, vg)
                + jnp.einsum('bhql,bhld->bhqd', p[..., topk * L:], v_own))

    o = lax.map(one, (qc, jnp.arange(nc)))
    return o.transpose(1, 2, 0, 3, 4).reshape(B, H, S, dh)

def banded_attention(q, k, v, max_dist, scale):
    B, Hk, G, L, dh = q.shape
    QB = Q_BLOCK
    nb = -(-L // QB)
    Lp = nb * QB
    qp = jnp.pad(q, ((0, 0), (0, 0), (0, 0), (0, Lp - L), (0, 0))).reshape(B, Hk, G, nb, QB, dh)
    kp = jnp.pad(k, ((0, 0), (0, 0), (QB, Lp - L), (0, 0)))
    vp = jnp.pad(v, ((0, 0), (0, 0), (QB, Lp - L), (0, 0)))
    kband = jnp.concatenate([kp[:, :, :Lp].reshape(B, Hk, nb, QB, dh),
                             kp[:, :, QB:].reshape(B, Hk, nb, QB, dh)], axis=3)
    vband = jnp.concatenate([vp[:, :, :Lp].reshape(B, Hk, nb, QB, dh),
                             vp[:, :, QB:].reshape(B, Hk, nb, QB, dh)], axis=3)
    s = jnp.einsum('bkgnqd,bknsd->bkgnqs', qp, kband).astype(jnp.float32) * scale
    dist = QB + jnp.arange(QB)[:, None] - jnp.arange(2 * QB)[None, :]
    kpos = jnp.arange(nb)[:, None] * QB - QB + jnp.arange(2 * QB)[None, :]
    mask = ((dist >= 0) & (dist <= max_dist))[None] & (kpos >= 0)[:, None, :]
    s = jnp.where(mask, s, -jnp.inf)
    m = jnp.max(s, axis=-1, keepdims=True)
    p = jnp.exp(s - m)
    l = jnp.sum(p, axis=-1, keepdims=True)
    o = jnp.einsum('bkgnqs,bknsd->bkgnqd', (p / l).astype(v.dtype), vband)
    lse = (m + jnp.log(l))[..., 0]
    return (o.reshape(B, Hk, G, Lp, dh)[:, :, :, :L], lse.reshape(B, Hk, G, Lp)[:, :, :, :L])

def dilated_attention(q, k, v):
    B, S, H, dh = q.shape
    outs, lses = [], []
    for window, dil in DIL_PATTERNS:
        L = S // dil

        def to_sub(t):
            return t.reshape(B, L, dil, H, dh).transpose(0, 2, 3, 1, 4).reshape(B * dil, H, L, dh)

        o, lse = banded_attention(to_sub(q)[:, :, None], to_sub(k), to_sub(v), window // dil, dh ** -0.5)
        outs.append(o[:, :, 0].reshape(B, dil, H, L, dh).transpose(0, 3, 1, 2, 4).reshape(B, S, H, dh))
        lses.append(lse[:, :, 0].reshape(B, dil, H, L).transpose(0, 3, 1, 2).reshape(B, S, H))
    w = jax.nn.softmax(jnp.stack(lses, axis=0), axis=0)
    return jnp.sum(w[..., None] * jnp.stack(outs, axis=0).astype(jnp.float32), axis=0).astype(q.dtype)

def memory_attention(q_mem, mem, mem_norm_g, w_mem_kv):
    B, S, _ = q_mem.shape
    kv = (rms_norm(mem, mem_norm_g) @ w_mem_kv).reshape(B, -1, 2, MEM_HEADS, MEM_DH)
    q = q_mem.reshape(B, S, MEM_HEADS, MEM_DH)
    s = jnp.einsum('bshd,bmhd->bhsm', q, kv[:, :, 0]).astype(jnp.float32) * MEM_DH ** -0.5
    p = jax.nn.softmax(s, axis=-1).astype(q.dtype)
    return jnp.einsum('bhsm,bmhd->bshd', p, kv[:, :, 1]).reshape(B, S, MEMQ_W)

def even_layer(x, mem, norm_g, w_in, q_norm_g, w_uq, kv_norm_g, w_ukv, mem_norm_g, w_mem_kv, w_out):
    B, S, _ = x.shape
    h = rms_norm(x, norm_g) @ w_in
    c_q, c_kv, k_pe, qkv_b, q_mem, gate = split_cols(h, EVEN_SPLITS)
    q_a = (rms_norm(c_q, q_norm_g) @ w_uq).reshape(B, S, MLA_HEADS, MLA_NOPE + MLA_ROPE)
    q_a = jnp.concatenate([q_a[..., :MLA_NOPE], apply_rope(q_a[..., MLA_NOPE:], MLA_ROPE)], axis=-1)
    kv_a = (rms_norm(c_kv, kv_norm_g) @ w_ukv).reshape(B, S, MLA_HEADS, MLA_NOPE + MLA_V)
    k_pe = apply_rope(k_pe[:, :, None, :], MLA_ROPE)
    k_a = jnp.concatenate([kv_a[..., :MLA_NOPE],
                           jnp.broadcast_to(k_pe, (B, S, MLA_HEADS, MLA_ROPE))], axis=-1)
    v_a = kv_a[..., MLA_NOPE:]
    o_a = causal_attention_qblocks(q_a.transpose(0, 2, 1, 3), k_a.transpose(0, 2, 1, 3),
                                   v_a.transpose(0, 2, 1, 3), (MLA_NOPE + MLA_ROPE) ** -0.5)
    o_a = o_a.transpose(0, 2, 1, 3).reshape(B, S, MLA_HEADS * MLA_V)
    qkv_b = qkv_b.reshape(B, S, 3, MOBA_HEADS, MOBA_DH)
    rot = MOBA_DH // ROT_FRAC
    q_b = apply_rope(qkv_b[:, :, 0], rot).transpose(0, 2, 1, 3)
    k_b = apply_rope(qkv_b[:, :, 1], rot).transpose(0, 2, 1, 3)
    v_b = qkv_b[:, :, 2].transpose(0, 2, 1, 3)
    o_b = moba_attention(q_b, k_b, v_b).transpose(0, 2, 1, 3).reshape(B, S, MOBA_HEADS * MOBA_DH)
    o_m = memory_attention(q_mem, mem, mem_norm_g, w_mem_kv)
    y = jnp.concatenate([o_a, o_b.astype(o_a.dtype), o_m.astype(o_a.dtype)], axis=-1) * jax.nn.silu(gate)
    return x + (y @ w_out).astype(x.dtype)

def odd_layer(x, mem, norm_g, w_in, sinks, mem_norm_g, w_mem_kv, w_out):
    B, S, _ = x.shape
    h = rms_norm(x, norm_g) @ w_in
    qkv_c, qkv_d, q_mem, gate = split_cols(h, ODD_SPLITS)
    q_c, k_c, v_c = split_cols(qkv_c, (SWA_HEADS * SWA_DH, SWA_KV_HEADS * SWA_DH, SWA_KV_HEADS * SWA_DH))
    rot_c = SWA_DH // ROT_FRAC
    G = SWA_HEADS // SWA_KV_HEADS
    q_c = apply_rope(q_c.reshape(B, S, SWA_HEADS, SWA_DH), rot_c)
    k_c = apply_rope(k_c.reshape(B, S, SWA_KV_HEADS, SWA_DH), rot_c)
    v_c = v_c.reshape(B, S, SWA_KV_HEADS, SWA_DH)
    qg = q_c.reshape(B, S, SWA_KV_HEADS, G, SWA_DH).transpose(0, 2, 3, 1, 4)
    o_c, lse_c = banded_attention(qg, k_c.transpose(0, 2, 1, 3), v_c.transpose(0, 2, 1, 3),
                                  SWA_WINDOW - 1, SWA_DH ** -0.5)
    o_c = o_c.transpose(0, 3, 1, 2, 4).reshape(B, S, SWA_HEADS, SWA_DH)
    lse_c = lse_c.transpose(0, 3, 1, 2).reshape(B, S, SWA_HEADS)
    sink_w = jax.nn.sigmoid(lse_c - sinks.astype(jnp.float32))
    o_c = (o_c.astype(jnp.float32) * sink_w[..., None]).astype(x.dtype).reshape(B, S, SWA_HEADS * SWA_DH)
    qkv_d = qkv_d.reshape(B, S, 3, DIL_HEADS, DIL_DH)
    rot_d = DIL_DH // ROT_FRAC
    o_d = dilated_attention(apply_rope(qkv_d[:, :, 0], rot_d), apply_rope(qkv_d[:, :, 1], rot_d),
                            qkv_d[:, :, 2]).reshape(B, S, DIL_HEADS * DIL_DH)
    o_m = memory_attention(q_mem, mem, mem_norm_g, w_mem_kv)
    y = jnp.concatenate([o_c, o_d.astype(o_c.dtype), o_m.astype(o_c.dtype)], axis=-1) * jax.nn.silu(gate).astype(o_c.dtype)
    return x + (y @ w_out).astype(x.dtype)

def first_inputs(seed: int = 0) -> dict:
    key = jax.random.key(seed)
    ks = jax.random.split(key, 20)

    def dense(k, shape):
        return jax.random.normal(k, shape, jnp.float32) * shape[-2] ** -0.5

    def gain(k, shape):
        return 1.0 + 0.02 * jax.random.normal(k, shape, jnp.float32)

    return {
        "x": jax.random.normal(ks[0], (BATCH, SEQ, D_MODEL), jnp.float32),
        "mem": jax.random.normal(ks[1], (BATCH, N_MEM, D_MODEL), jnp.float32),
        "ev_norm_g": gain(ks[2], (N_EVEN, D_MODEL)),
        "ev_w_in": dense(ks[3], (N_EVEN, D_MODEL, EVEN_IN)),
        "ev_q_norm_g": gain(ks[4], (N_EVEN, MLA_Q_RANK)),
        "ev_w_uq": dense(ks[5], (N_EVEN, MLA_Q_RANK, MLA_HEADS * (MLA_NOPE + MLA_ROPE))),
        "ev_kv_norm_g": gain(ks[6], (N_EVEN, MLA_KV_RANK)),
        "ev_w_ukv": dense(ks[7], (N_EVEN, MLA_KV_RANK, MLA_HEADS * (MLA_NOPE + MLA_V))),
        "ev_mem_norm_g": gain(ks[8], (N_EVEN, D_MODEL)),
        "ev_w_mem_kv": dense(ks[9], (N_EVEN, D_MODEL, 2 * MEMQ_W)),
        "ev_w_out": dense(ks[10], (N_EVEN, EVEN_VW, D_MODEL)),
        "od_norm_g": gain(ks[11], (N_ODD, D_MODEL)),
        "od_w_in": dense(ks[12], (N_ODD, D_MODEL, ODD_IN)),
        "od_sinks": 0.5 * jax.random.normal(ks[13], (N_ODD, SWA_HEADS), jnp.float32),
        "od_mem_norm_g": gain(ks[14], (N_ODD, D_MODEL)),
        "od_w_mem_kv": dense(ks[15], (N_ODD, D_MODEL, 2 * MEMQ_W)),
        "od_w_out": dense(ks[16], (N_ODD, ODD_VW, D_MODEL)),
        "final_norm_g": gain(ks[17], (D_MODEL,)),
    }

def first_block(x, mem, ev_norm_g, ev_w_in, ev_q_norm_g, ev_w_uq, ev_kv_norm_g, ev_w_ukv,
              ev_mem_norm_g, ev_w_mem_kv, ev_w_out, od_norm_g, od_w_in, od_sinks,
              od_mem_norm_g, od_w_mem_kv, od_w_out, final_norm_g):
    for layer in range(DEPTH):
        i = layer // 2
        if layer % 2 == 0:
            x = even_layer(x, mem, ev_norm_g[i], ev_w_in[i], ev_q_norm_g[i], ev_w_uq[i],
                           ev_kv_norm_g[i], ev_w_ukv[i], ev_mem_norm_g[i], ev_w_mem_kv[i], ev_w_out[i])
        else:
            x = odd_layer(x, mem, od_norm_g[i], od_w_in[i], od_sinks[i], od_mem_norm_g[i],
                          od_w_mem_kv[i], od_w_out[i])
    return rms_norm(x, final_norm_g)


GRID_W = 64
CTX_LEN = 256
N_MIXERS = 2
N_LRU = (DEPTH + 1) // 2
N_ATT = DEPTH // 2
LRU_WIDTH = D_MODEL
LRU_BLOCKS = 16
LRU_BLOCK = LRU_WIDTH // LRU_BLOCKS
LRU_C = 8.0
CONV_W = 4
CONV_PAD = (2, 1)
ATT_HEAD_DIM = 64
ATT_HEADS = D_MODEL // (2 * ATT_HEAD_DIM)
ATT_V_DIM = 2 * ATT_HEAD_DIM
ATT_WIDTH = ATT_HEADS * ATT_V_DIM
ROPE_FREQS = ATT_HEAD_DIM // 4
ROPE_BASE = 10000.0


def rms_norm_2(x, g):
    xf = x.astype(jnp.float32)
    y = xf * lax.rsqrt(jnp.mean(xf * xf, axis=-1, keepdims=True) + EPS)
    return (y * g.astype(jnp.float32)).astype(x.dtype)

def dwconv(u, w, b):
    y = lax.conv_general_dilated(u, w[:, None, :], window_strides=(1,), padding=[CONV_PAD],
                                 dimension_numbers=("NWC", "WIO", "NWC"),
                                 feature_group_count=u.shape[-1])
    return y + b

def lru_coeffs(xc, gw, gb, lam):
    B_, L, _ = xc.shape
    xb = xc.reshape(B_, L, LRU_BLOCKS, LRU_BLOCK)
    gates = jax.nn.sigmoid((jnp.einsum("blnc,gncd->gblnd", xb, gw) + gb[:, None, None]).astype(jnp.float32))
    gates = gates.reshape(2, B_, L, LRU_WIDTH)
    r, i = gates[0], gates[1]
    log_a = -LRU_C * r * jax.nn.softplus(-lam.astype(jnp.float32))
    a = jnp.exp(log_a)
    b = jnp.sqrt(-jnp.expm1(2.0 * log_a)) * (i * xc.astype(jnp.float32))
    return a, b

def linear_scan(a, b, h0, reverse):
    def step(h, ab):
        at, bt = ab
        h = at * h + bt
        return h, h
    h_end, hs = lax.scan(step, h0, (jnp.swapaxes(a, 0, 1), jnp.swapaxes(b, 0, 1)), reverse=reverse)
    return h_end, jnp.swapaxes(hs, 0, 1)

def rglru_mixer(h_lat, h_ctx, w_in, conv_w, conv_b, gate_w, gate_b, lam, w_out, need_ctx_out):
    u_lat, g_lat = jnp.split(h_lat @ w_in, 2, axis=-1)
    u_ctx, g_ctx = jnp.split(h_ctx @ w_in, 2, axis=-1)
    xc_lat = dwconv(u_lat, conv_w, conv_b)
    xc_ctx = dwconv(u_ctx, conv_w, conv_b)
    h0 = jnp.zeros((h_lat.shape[0], LRU_WIDTH), jnp.float32)
    outs_lat, outs_ctx = [], []
    for d, rev in enumerate((False, True)):
        a_c, b_c = lru_coeffs(xc_ctx, gate_w[d], gate_b[d], lam[d])
        h_end, hs_ctx = linear_scan(a_c, b_c, h0, rev)
        a_l, b_l = lru_coeffs(xc_lat, gate_w[d], gate_b[d], lam[d])
        _, hs_lat = linear_scan(a_l, b_l, h_end, rev)
        outs_lat.append(hs_lat)
        outs_ctx.append(hs_ctx)
    y_lat = ((outs_lat[0] + outs_lat[1]).astype(h_lat.dtype) * jax.nn.silu(g_lat)) @ w_out
    y_ctx = None
    if need_ctx_out:
        y_ctx = ((outs_ctx[0] + outs_ctx[1]).astype(h_ctx.dtype) * jax.nn.silu(g_ctx)) @ w_out
    return y_lat, y_ctx

def axial_rope_tables(S):
    rows = S // GRID_W
    row = jnp.broadcast_to(jnp.arange(rows)[:, None], (rows, GRID_W)).reshape(S).astype(jnp.float32)
    col = jnp.broadcast_to(jnp.arange(GRID_W)[None, :], (rows, GRID_W)).reshape(S).astype(jnp.float32)
    inv = ROPE_BASE ** (-jnp.arange(ROPE_FREQS, dtype=jnp.float32) / ROPE_FREQS)
    ang = jnp.stack([row[:, None] * inv, col[:, None] * inv], axis=1)
    return jnp.cos(ang), jnp.sin(ang)

def apply_axial_rope(x, cos, sin):
    xs = x.astype(jnp.float32).reshape(x.shape[:-1] + (2, 2, ROPE_FREQS))
    x1, x2 = xs[..., 0, :], xs[..., 1, :]
    out = jnp.stack([x1 * cos - x2 * sin, x2 * cos + x1 * sin], axis=-2)
    return out.reshape(x.shape).astype(x.dtype)

def diff_attend(q, k, v, lam):
    s = jnp.einsum("bhcqd,bhckd->bhcqk", q, k).astype(jnp.float32)
    p = jax.nn.softmax(s, axis=-1)
    attn = p[:, :, 0] - lam * p[:, :, 1]
    return jnp.einsum("bhqk,bhkv->bhqv", attn.astype(v.dtype), v)

def diff_attn_mixer(h_lat, h_ctx, w_in, q_g, k_g, lam_vecs, subln_g, w_out, lam_init, cos, sin, need_ctx_out):
    def project(h):
        B_, L, _ = h.shape
        q, k, v, g = jnp.split(h @ w_in, 4, axis=-1)
        q = rms_norm_2(q.reshape(B_, L, ATT_HEADS, 2, ATT_HEAD_DIM), q_g).transpose(0, 2, 3, 1, 4)
        k = rms_norm_2(k.reshape(B_, L, ATT_HEADS, 2, ATT_HEAD_DIM), k_g).transpose(0, 2, 3, 1, 4)
        v = v.reshape(B_, L, ATT_HEADS, ATT_V_DIM).transpose(0, 2, 1, 3)
        return q * (ATT_HEAD_DIM ** -0.5), k, v, g

    def finish(o, g):
        B_, _, L, _ = o.shape
        o = rms_norm_2(o, subln_g) * (1.0 - lam_init)
        o = o.transpose(0, 2, 1, 3).reshape(B_, L, ATT_WIDTH)
        return (o * jax.nn.silu(g)) @ w_out

    lv = lam_vecs.astype(jnp.float32)
    lam = jnp.exp(jnp.sum(lv[0] * lv[1])) - jnp.exp(jnp.sum(lv[2] * lv[3])) + lam_init

    q_l, k_l, v_l, g_l = project(h_lat)
    q_c, k_c, v_c, g_c = project(h_ctx)
    q_l = apply_axial_rope(q_l, cos, sin)
    k_l = apply_axial_rope(k_l, cos, sin)
    k_all = jnp.concatenate([k_l, k_c], axis=3)
    v_all = jnp.concatenate([v_l, v_c], axis=2)

    B_, H, _, S, d = q_l.shape
    nblk = S // Q_BLOCK
    qb = jnp.moveaxis(q_l.reshape(B_, H, 2, nblk, Q_BLOCK, d), 3, 0)
    ob = lax.map(lambda qq: diff_attend(qq, k_all, v_all, lam), qb)
    o_l = jnp.moveaxis(ob, 0, 2).reshape(B_, H, S, ATT_V_DIM)
    y_lat = finish(o_l, g_l)
    y_ctx = None
    if need_ctx_out:
        y_ctx = finish(diff_attend(q_c, k_c, v_c, lam), g_c)
    return y_lat, y_ctx

def second_inputs(seed: int = 0) -> dict:
    key = jax.random.key(seed)
    ks = jax.random.split(key, 24)
    f32 = jnp.float32
    D, W = D_MODEL, LRU_WIDTH
    u = jax.random.uniform(ks[11], (N_LRU, 2, W), f32, 0.9, 0.999)
    a = u ** (1.0 / LRU_C)
    return {
        "x": jax.random.normal(ks[0], (BATCH, SEQ, D), f32),
        "c": jax.random.normal(ks[1], (BATCH, D), f32),
        "ctx": jax.random.normal(ks[2], (BATCH, CTX_LEN, D), f32),
        "c_ctx": jax.random.normal(ks[3], (D,), f32),
        "mod_w": jax.random.normal(ks[4], (DEPTH, D, 3 * D), f32) * (0.5 * D ** -0.5),
        "mod_b": jax.random.normal(ks[5], (DEPTH, 3 * D), f32) * 0.01,
        "norm_g": 1.0 + 0.1 * jax.random.normal(ks[6], (DEPTH, D), f32),
        "lru_w_in": jax.random.normal(ks[7], (N_LRU, D, 2 * W), f32) * D ** -0.5,
        "lru_conv_w": jax.random.normal(ks[8], (N_LRU, CONV_W, W), f32) * CONV_W ** -0.5,
        "lru_conv_b": jax.random.normal(ks[9], (N_LRU, W), f32) * 0.01,
        "lru_gate_w": jax.random.normal(ks[10], (N_LRU, 2, 2, LRU_BLOCKS, LRU_BLOCK, LRU_BLOCK), f32) * LRU_BLOCK ** -0.5,
        "lru_gate_b": jax.random.normal(ks[12], (N_LRU, 2, 2, LRU_BLOCKS, LRU_BLOCK), f32) * 0.01,
        "lru_lambda": jnp.log(a) - jnp.log1p(-a),
        "lru_w_out": jax.random.normal(ks[13], (N_LRU, W, D), f32) * W ** -0.5,
        "att_w_in": jax.random.normal(ks[14], (N_ATT, D, 4 * ATT_WIDTH), f32) * D ** -0.5,
        "att_q_norm": 1.0 + 0.1 * jax.random.normal(ks[15], (N_ATT, ATT_HEAD_DIM), f32),
        "att_k_norm": 1.0 + 0.1 * jax.random.normal(ks[16], (N_ATT, ATT_HEAD_DIM), f32),
        "att_lambda": 0.1 * jax.random.normal(ks[17], (N_ATT, 4, ATT_HEAD_DIM), f32),
        "att_subln": 1.0 + 0.1 * jax.random.normal(ks[18], (N_ATT, ATT_V_DIM), f32),
        "att_w_out": jax.random.normal(ks[19], (N_ATT, ATT_WIDTH, D), f32) * ATT_WIDTH ** -0.5,
    }

def second_block(x, c, ctx, c_ctx, mod_w, mod_b, norm_g, lru_w_in, lru_conv_w, lru_conv_b, lru_gate_w,
              lru_gate_b, lru_lambda, lru_w_out, att_w_in, att_q_norm, att_k_norm, att_lambda,
              att_subln, att_w_out):
    S = x.shape[1]
    cos, sin = axial_rope_tables(S)
    sc = jax.nn.silu(c)
    scc = jax.nn.silu(c_ctx)
    for i in range(DEPTH):
        need_ctx_out = i < DEPTH - 1
        shift, scale, gate = jnp.split(sc @ mod_w[i] + mod_b[i], 3, axis=-1)
        cshift, cscale, cgate = jnp.split(scc @ mod_w[i] + mod_b[i], 3, axis=-1)
        h_lat = rms_norm_2(x, norm_g[i]) * (1.0 + scale[:, None]) + shift[:, None]
        h_ctx = rms_norm_2(ctx, norm_g[i]) * (1.0 + cscale) + cshift
        j = i // N_MIXERS
        if i % N_MIXERS == 0:
            y_lat, y_ctx = rglru_mixer(h_lat, h_ctx, lru_w_in[j], lru_conv_w[j], lru_conv_b[j],
                                       lru_gate_w[j], lru_gate_b[j], lru_lambda[j], lru_w_out[j],
                                       need_ctx_out)
        else:
            lam_init = 0.8 - 0.6 * math.exp(-0.3 * i)
            y_lat, y_ctx = diff_attn_mixer(h_lat, h_ctx, att_w_in[j], att_q_norm[j], att_k_norm[j],
                                           att_lambda[j], att_subln[j], att_w_out[j], lam_init,
                                           cos, sin, need_ctx_out)
        x = x + gate[:, None] * y_lat
        if need_ctx_out:
            ctx = ctx + cgate * y_ctx
    return x


def setup_inputs(seed=0):
    out = dict(first_inputs(seed))
    for name, value in second_inputs(seed + 1).items():
        if name != "x":
            out[name + "_2"] = value
    return out


def reference(
    x, mem, ev_norm_g, ev_w_in, ev_q_norm_g, ev_w_uq, ev_kv_norm_g, ev_w_ukv, ev_mem_norm_g,
    ev_w_mem_kv, ev_w_out, od_norm_g, od_w_in, od_sinks, od_mem_norm_g, od_w_mem_kv, od_w_out,
    final_norm_g, c_2, ctx_2, c_ctx_2, mod_w_2, mod_b_2, norm_g_2, lru_w_in_2, lru_conv_w_2,
    lru_conv_b_2, lru_gate_w_2, lru_gate_b_2, lru_lambda_2, lru_w_out_2, att_w_in_2,
    att_q_norm_2, att_k_norm_2, att_lambda_2, att_subln_2, att_w_out_2,
):
    x = first_block(
        x, mem, ev_norm_g, ev_w_in, ev_q_norm_g, ev_w_uq, ev_kv_norm_g, ev_w_ukv, ev_mem_norm_g,
        ev_w_mem_kv, ev_w_out, od_norm_g, od_w_in, od_sinks, od_mem_norm_g, od_w_mem_kv,
        od_w_out, final_norm_g,
    )
    return second_block(
        x, c_2, ctx_2, c_ctx_2, mod_w_2, mod_b_2, norm_g_2, lru_w_in_2, lru_conv_w_2,
        lru_conv_b_2, lru_gate_w_2, lru_gate_b_2, lru_lambda_2, lru_w_out_2, att_w_in_2,
        att_q_norm_2, att_k_norm_2, att_lambda_2, att_subln_2, att_w_out_2,
    )


_drawn_inputs = setup_inputs


def setup_inputs(seed=0):
    import zlib

    import numpy as np

    out = dict(_drawn_inputs(seed))
    spreads = {}
    factors = {'ev_norm_g': 8.0,
     'ev_q_norm_g': 8.0,
     'ev_kv_norm_g': 8.0,
     'ev_mem_norm_g': 8.0,
     'od_norm_g': 8.0,
     'od_sinks': 33.362,
     'od_mem_norm_g': 8.0,
     'final_norm_g': 2.807,
     'lru_conv_b_2': 3.117,
     'lru_gate_b_2': 25.695,
     'att_q_norm_2': 8.0,
     'att_k_norm_2': 8.0,
     'att_lambda_2': 6.981,
     'att_subln_2': 4.822}
    for name, (base, spread) in spreads.items():
        noise = np.random.default_rng([zlib.crc32(name.encode()), seed]).standard_normal(out[name].shape)
        drawn = base * np.exp(spread * noise) if base else spread * noise
        out[name] = __import__('jax').numpy.asarray(drawn.astype(out[name].dtype))
    for name, factor in factors.items():
        out[name] = (out[name] * factor).astype(out[name].dtype)
    return out
```

```python
import math
from contextlib import ExitStack

import numpy as np

import concourse.bass as bass
from concourse import mybir

F32 = mybir.dt.float32
ACT = mybir.ActivationFunctionType
ALU = mybir.AluOpType
AX = mybir.AxisListType.X

P = 128
SEQ = 256
D = 2048
KT = D // P
TT = SEQ // P
EPS = 1e-6
NEG = -1e30

MLA_HEADS, MLA_QR, MLA_KVR, NOPE, ROPE, MLA_DV = 8, 512, 256, 128, 64, 128
MOBA_HEADS, DH = 8, 128
MEM_HEADS = 4
MEMW = MEM_HEADS * DH
EV_VW = MLA_HEADS * MLA_DV + MOBA_HEADS * DH + MEMW
EV_CKV = MLA_QR
EV_KPE = EV_CKV + MLA_KVR
EV_QKV = EV_KPE + ROPE
EV_QM = EV_QKV + 3 * MOBA_HEADS * DH
EV_GATE = EV_QM + MEMW
EV_IN = EV_GATE + EV_VW
SWA_HEADS, SWA_KV, SWA_DH, SWA_WINDOW = 16, 2, 64, 128
DIL_HEADS = 6
DIL_PATTERNS = ((128, 1), (512, 4), (2048, 16))
OD_KC = SWA_HEADS * SWA_DH
OD_VC = OD_KC + SWA_KV * SWA_DH
OD_QD = OD_VC + SWA_KV * SWA_DH
OD_KD = OD_QD + DIL_HEADS * DH
OD_VD = OD_KD + DIL_HEADS * DH
OD_QM = OD_VD + DIL_HEADS * DH
OD_GATE = OD_QM + MEMW
OD_VW = SWA_HEADS * SWA_DH + DIL_HEADS * DH + MEMW
OD_IN = OD_GATE + OD_VW
EV_QA = EV_QKV
EV_KVA = EV_QA + MLA_HEADS * (NOPE + ROPE)
ATT_HEADS, ATT_DH = 16, 64
GROUPS = 4
LRU_C = 8.0
LAM_INIT = 0.8 - 0.6 * math.exp(-0.3 * 1)

CHUNK = 512
SLOTS = 8

CONSTS = {}


def _lay_consts():
    at = 0
    for name, width in (("ident", P), ("mla", TT * 4 * 32), ("r32", TT * 4 * 16), ("r16", TT * 4 * 8),
                        ("axial", TT * 2 * 64), ("causal", 2 * SEQ), ("swa", 2 * SEQ), ("dil", 2 * SEQ)):
        CONSTS[name] = (at, width)
        at += width
    return at


NCONST = _lay_consts()


def shape_constants():
    out = np.zeros((P, NCONST), np.float32)

    def put(name, a):
        at, width = CONSTS[name]
        out[:, at:at + width] = a.reshape(P, width)

    put("ident", np.eye(P, dtype=np.float32))
    pos = np.arange(SEQ, dtype=np.float32)
    for name, rot in (("mla", ROPE), ("r32", DH // 4), ("r16", SWA_DH // 4)):
        inv = (1.0 / (np.float32(500000.0) ** (np.arange(0, rot, 2, dtype=np.float32) / np.float32(rot)))).astype(np.float32)
        ang = (pos[:, None] * inv[None]).astype(np.float32)
        c, s = np.cos(ang), np.sin(ang)
        table = np.stack([np.concatenate([c, c], 1), np.concatenate([-s, s], 1)], 1)
        put(name, table.reshape(TT, P, 2 * rot).transpose(1, 0, 2))
    nf = ATT_DH // 4
    inv = (np.float32(10000.0) ** (-np.arange(nf, dtype=np.float32) / np.float32(nf))).astype(np.float32)
    t = np.arange(SEQ)
    ang = np.stack([(t // 64).astype(np.float32)[:, None] * inv, (t % 64).astype(np.float32)[:, None] * inv], 1)
    c, s = np.cos(ang).astype(np.float32), np.sin(ang).astype(np.float32)
    table = np.stack([np.stack([c, c], 2).reshape(SEQ, 64), np.stack([-s, s], 2).reshape(SEQ, 64)], 1)
    put("axial", table.reshape(TT, P, 128).transpose(1, 0, 2))
    q, k = np.arange(SEQ)[:, None], np.arange(SEQ)[None]
    dist = q - k

    def mask(times):
        bias = np.where(times > 0, np.log(np.maximum(times, 1).astype(np.float64)), NEG).astype(np.float32)
        return bias.reshape(TT, P, SEQ).transpose(1, 0, 2)

    put("causal", mask((dist >= 0).astype(int)))
    put("swa", mask(((dist >= 0) & (dist <= SWA_WINDOW - 1)).astype(int)))
    put("dil", mask(sum(((dist >= 0) & (dist % dil == 0) & (dist // dil <= window // dil)).astype(int)
                        for window, dil in DIL_PATTERNS)))
    return out


VECTORS = (
    (("ev_norm_g", 0, 16), ("ev_mem_norm_g", 0, 16), ("od_norm_g", 0, 16), ("od_mem_norm_g", 0, 16),
     ("c_2", 0, 16), ("c_ctx_2", None, 16), ("ev_q_norm_g", 0, 4), ("ev_kv_norm_g", 0, 2)),
    (("norm_g_2", None, 32), ("lru_lambda_2", 0, 32), ("lru_conv_b_2", 0, 16)),
    (("lru_conv_w_2", 0, 64), ("lru_gate_b_2", 0, 64)),
    (("mod_b_2", None, 96),),
)
VEC_ROWS = [sum(n for _, _, n in tile) for tile in VECTORS]
VEC_AT = {}
for _t, _tile in enumerate(VECTORS):
    _row = 0
    for _name, _, _n in _tile:
        VEC_AT[_name] = _t * P + _row
        _row += _n

STAGE_UNITS = (("mkv0", 16), ("mkv1", 16), ("ev_a", 16), ("ev_b", 96), ("uq", 6), ("ukv", 4), ("ev_out", 40),
               ("od_b", 96), ("od_c", 8), ("od_out", 36), ("lru_in", 64), ("lru_out", 32), ("att_in", 128),
               ("att_out", 32))
UNIT0 = {}
_at = 0
for _name, _n in STAGE_UNITS:
    UNIT0[_name] = _at
    _at += _n
CHUNK_UNITS = {name: 8 for name, _ in STAGE_UNITS} | {"uq": 2, "ukv": 1, "ev_out": 10, "od_out": 9}


def multiplied(stage, c):
    return UNIT0[stage] + (c + 1) * CHUNK_UNITS[stage]


CHUNK0 = {"mkv0": 0, "mkv1": 2, "ev_a": 4, "ev_b": 6, "uq": 18, "ukv": 21, "od_b": 25, "od_c": 37}
RES0 = {"ev_out": 0, "od_out": 4, "lru_out": 8, "att_out": 12}


class Heads:

    def __init__(self, name, n0, turns, kind, q, k, v, gate, y0, mask, scale, mod_layer, mod_chunk0, mod0, mem=None, sink=None):
        self.name, self.n0, self.turns, self.kind = name, n0, turns, kind
        self.q, self.k, self.v, self.gate, self.y0 = q, k, v, gate, y0
        self.mask, self.scale = mask, scale
        self.mod_layer, self.mod_chunk0, self.mod0 = mod_layer, mod_chunk0, mod0
        self.mem, self.sink = mem, sink


EV_Y_B = MLA_HEADS
EV_Y_M = MLA_HEADS + MOBA_HEADS
OD_Y_D = SWA_HEADS * SWA_DH // P
OD_Y_M = OD_Y_D + DIL_HEADS
SC128, SC64 = DH ** -0.5, SWA_DH ** -0.5
MEM_EV = Heads("mem_ev", 0, 2, "plain", EV_QM, 0, MEMW, EV_GATE + EV_Y_M * P, EV_Y_M, None, SC128, 0, 0, 0, mem=0)
MOBA = Heads("moba", 4, 4, "plain", EV_QKV, EV_QKV + 1024, EV_QKV + 2048, EV_GATE + EV_Y_B * P, EV_Y_B, "causal", SC128, 0, 2, 2)
MLA = Heads("mla", 12, 4, "mla", EV_QA, EV_KVA, EV_KVA + NOPE, EV_GATE, 0, "causal", (NOPE + ROPE) ** -0.5, 0, 6, 6)
SWA = [Heads(f"swa{j}", 20 + 8 * j, 4, "swa", 512 * j, OD_KC + 64 * j, OD_VC + 64 * j, OD_GATE + 512 * j, 4 * j, "swa", SC64,
             1, 4 * j, 10 + 4 * j, sink=8 * j) for j in range(2)]
DIL = Heads("dil", 36, 3, "plain", OD_QD, OD_KD, OD_VD, OD_GATE + OD_Y_D * P, OD_Y_D, "dil", SC128, 1, 8, 18)
MEM_OD = Heads("mem_od", 42, 2, "plain", OD_QM, 0, MEMW, OD_GATE + OD_Y_M * P, OD_Y_M, None, SC128, 0, 10, 21, mem=1)
EV_LOOPS = (MEM_EV, MOBA, MLA)
OD_LOOPS = (*SWA, DIL, MEM_OD)
N_HEADS = 46
N_MOD = 24


def build(nc, t, consts, out):
    ctx = ExitStack()
    with ctx:
        def sb(name, shape):
            return ctx.enter_context(nc.sbuf_tensor(name, shape, F32))

        def sem(name):
            return ctx.enter_context(nc.semaphore(name))

        PS = ctx.enter_context(nc.psum_tensor("ps", [P, 8, CHUNK], F32))
        X = sb("x_res", [P, TT, D])
        CT = sb("ctx_res", [P, TT * D])
        AT = sb("act_t", [P, 2 * KT * SEQ])
        RA = sb("ring", [P, SLOTS, 1024])
        RF = sb("mod_ring", [P, SLOTS, CHUNK])
        HB = sb("proj", [P, TT * EV_IN])
        CST = sb("consts", [P, NCONST])
        GT = sb("vectors_t", [P, 4 * P])
        CTT = sb("cond_t", [P, KT, 2])
        MODT = sb("mod_t", [P, 2, 48, 2])
        MODS = sb("mod_rows", [P, CHUNK])
        BC = sb("bcast", [P, 512 + 16])
        AR = sb("arena", [P, 5632])
        ST = sb("stats", [P, 9, 4])
        HS = sb("head_stats", [P, 2, 16])
        SC = sb("scalars", [P, 512])

        def const(name):
            at, width = CONSTS[name]
            return CST[:, at:at + width]

        ident = const("ident")
        MKV = CT[:].rearrange("p (l t c) -> p l t c", l=2, t=TT)
        CX = CT[:].rearrange("p (t d) -> p t d", t=TT)
        XT = AT[:, 0:KT * SEQ].rearrange("p (k s) -> p k s", s=SEQ)
        MT0 = AT[:, KT * SEQ:2 * KT * SEQ].rearrange("p (k s) -> p k s", s=SEQ)
        HT = AT[:].rearrange("p (k s) -> p k s", s=2 * SEQ)
        HE = HB[:].rearrange("p (t c) -> p t c", c=EV_IN)
        HO = HB[:, 0:TT * OD_IN].rearrange("p (t c) -> p t c", c=OD_IN)
        MEMX = HB[:, 0:TT * D].rearrange("p (t d) -> p t d", t=TT)
        MT1 = HB[:, TT * D:2 * TT * D].rearrange("p (k s) -> p k s", s=SEQ)
        JUNK = HB[:, 2 * TT * D:2 * TT * D + D]
        GR = HB[:, 2 * TT * D + D:2 * TT * D + D + 4 * P].rearrange("p (v c) -> p v c", c=P)
        CQT = AT[:, 20 * SEQ:24 * SEQ].rearrange("p (k s) -> p k s", s=SEQ)
        CKVT = AT[:, 24 * SEQ:26 * SEQ].rearrange("p (k s) -> p k s", s=SEQ)

        def vec(name, k=0, n=1):
            return GT[:, VEC_AT[name] + k:VEC_AT[name] + k + n]

        def carve(parts):
            at, views = 0, []
            for n in parts:
                views.append(AR[:, at:at + n])
                at += n
            return views
        a_qs, a_ks, a_qkt, a_qrt, KPT, a_s, a_pt, a_ys = carve((768, 512, 1024, 512, 256, 1024, 1024, 512))
        QS = a_qs.rearrange("p (a t c) -> p a t c", a=2, t=TT)
        KS = a_ks.rearrange("p (a t c) -> p a t c", a=2, t=TT)
        QKT = a_qkt.rearrange("p (a c) -> p a c", a=2)
        QRT = a_qrt.rearrange("p (a c) -> p a c", a=2)
        S = a_s.rearrange("p (a t c) -> p a t c", a=2, t=TT)
        PT = a_pt.rearrange("p (a c) -> p a c", a=2)
        YS = a_ys.rearrange("p (a t c) -> p a t c", a=2, t=TT)
        ROT_A, ROT_B = a_s[:, 0:512], a_s[:, 512:1024]
        NM, LS, RL, ES, SN = (HS[:, :, j:j + 2] for j in (0, 2, 4, 6, 8))
        SINK = BC[:, 512:528]

        l_xc, l_gw, l_ri, l_sg, l_hs = carve((1024, 1024, 2048, 512, 1024))
        XC = l_xc.rearrange("p (b c s) -> p b c s", b=2, c=2)
        GW = l_gw.rearrange("p (b j d) -> p b j d", b=2, j=4)
        RI = l_ri.rearrange("p (j s) -> p j s", j=4)
        SG = l_sg
        HSC = l_hs.rearrange("p (d s) -> p d s", d=2)
        YL = HB[:, 0:KT * 2 * SEQ].rearrange("p (k s) -> p k s", s=2 * SEQ)
        LA = HB[:, 8192:9216].rearrange("p (d s) -> p d s", d=2)
        LW = HB[:, 9216:10240].rearrange("p (d s) -> p d s", d=2)
        LAF, LWF, LTMP = HB[:, 8192:9216], HB[:, 9216:10240], HB[:, 10240:11264]
        LTAB = SC[:, 164:164 + 18 * 12].rearrange("p (k j) -> p k j", j=12)
        BV = SC[:, 380:404].rearrange("p (b j) -> p b j", b=2)
        NSINK = SC[:, 404:436].rearrange("p (h t) -> p h t", t=TT)
        NLAM = SC[:, 436:437]
        MSC = SC[:, 440:504]
        DT1S = AR[:, 0:128]
        XN = HB[:, 0:TT * D].rearrange("p (t d) -> p t d", t=TT)
        CN = HB[:, TT * D:2 * TT * D].rearrange("p (t d) -> p t d", t=TT)
        FG = RF[:].rearrange("p a b -> p (a b)")[:, 0:D]
        G_LAT = AT[:, 0:D]
        G_CTX = AT[:, D:2 * D]
        G_ATT = CT[:, 0:D]

        d_qkt, d_e, d_pt, d_os = carve((1536, 2048, 1024, 1024))
        DQK = d_qkt.rearrange("p (a c) -> p a c", a=2)
        DE = d_e.rearrange("p (a c s) -> p a c s", a=2, c=2)
        DPT = d_pt.rearrange("p (a c) -> p a c", a=2)
        OS = d_os.rearrange("p (t c) -> p t c", t=TT)
        RQK = HB[:, 0:3072].rearrange("p (t c) -> p t c", t=6)
        DSQ = HB[:, 3072:6144]
        RV = HB[:, 6144:8192].rearrange("p (t c) -> p t c", t=4)
        RG = HB[:, 8192:9216].rearrange("p (t c) -> p t c", t=2)
        DT1 = HB[:, 9216:9728]
        DT2 = HB[:, 9728:10240]
        DS48, DS8 = HB[:, 10240:10288], HB[:, 10288:10296]
        DYT = RF[:].rearrange("p a b -> p (a b)").rearrange("p (k s) -> p k s", s=SEQ)
        SUBG, QG, KG, LV = BC[:, 0:128], BC[:, 128:192], BC[:, 192:256], BC[:, 256:512]

        ONES = AR[:, 0:P]

        def DIAG(j):
            return AR[:, P + (j % 2) * 512:P + (j % 2) * 512 + 512].rearrange("p (k d) -> p k d", k=4)

        s_const, s_rows, s_mem, s_x, s_bc, s_ctx, s_fg, s_out = map(sem, (
            "const_loaded", "vector_rows_loaded", "mem_loaded", "x_loaded", "bcast_loaded", "ctx_loaded",
            "final_g_loaded", "out_stored"))
        s_w = [sem(f"weights_landed{j}") for j in range(SLOTS)]
        s_wfree = sem("weight_units_used")
        s_f = [sem(f"mod_weights_landed{j}") for j in range(SLOTS)]
        s_ffree = sem("mod_units_used")
        s_vt, s_vec, s_cond = map(sem, ("vectors_transposed", "vectors_ready", "cond_ready"))
        s_sq, s_ms, s_rt, s_rs = map(sem, ("squares_summed", "mean_square", "root_taken", "rstd_ready"))
        s_xn, s_xt, s_xeD, s_xeA = map(sem, ("rows_normalized", "rows_transposed", "acts_by_vector", "acts_by_scalar"))
        s_ge, s_rh, s_re = map(sem, ("chunk_evicted", "residual_gated", "residual_added"))
        s_rope, s_ra, s_rb = map(sem, ("rope_done", "rope_cos", "rope_sin"))
        s_ct, s_cte, s_kpt = map(sem, ("latents_transposed", "latents_ready", "kpe_ready"))
        s_stg, s_t1, s_qk, s_sc, s_sm, s_mx, s_ex, s_pt, s_pe, s_o, s_rl, s_ys, s_yt, s_ye = map(sem, (
            "head_staged", "head_qk_transposed", "head_qk_ready", "head_scores", "head_masked", "head_max",
            "head_exp", "head_p_transposed", "head_p_ready", "head_out", "head_recip", "head_y", "head_y_transposed",
            "head_y_ready"))
        s_sk, s_es, s_l2 = map(sem, ("sink_shifted", "sink_exp", "sink_added"))
        s_mods, s_modt, s_modd = map(sem, ("mod_rows_ready", "mod_transposed", "mod_ready"))
        s_dve = sem("vector_step")
        s_lam = sem("lru_decay_ready")
        s_exl = sem("lru_exp_ready")
        SQUARED = np.cumsum([2, 2, 4, 2, 2, 2, 2, 2, 2]).tolist()
        s_msc = sem("mod_scale_ready")
        s_gw = [sem(f"gate_weights_landed{b}") for b in range(2)]
        s_cv, s_xc, s_gt, s_sg, s_gs, s_ab, s_w2a, s_w2, s_sqr, s_ix, s_b, s_sn, s_y = map(sem, (
            "lru_conv_tap", "lru_conv", "lru_gates", "lru_sigmoids", "lru_silu", "lru_a",
            "lru_a2", "lru_1ma2", "lru_sqrt", "lru_ix", "lru_b", "lru_scan", "lru_y"))
        s_sk2, s_xf, s_bv, s_hsum, s_ltab = map(sem, ("sink_max", "x_final", "lru_block_vectors", "lru_sum", "lru_table_ready"))
        s_dg, s_gb, s_gbe = map(sem, ("gate_diag", "gate_bcast", "gate_bcast_ready"))
        s_dqe, s_ds, s_dm, s_dp0 = map(sem, ("diff_chunk_evicted", "diff_step", "diff_ms", "diff_root"))
        s_qn = sem("diff_qk_ready")
        s_e1, s_e2, s_e3, s_e4, s_e5, s_e6, s_e7, s_e8, s_e9, s_e10, s_e11 = map(sem, (
            "diff_qkt", "diff_qkt_ready", "diff_scores", "diff_max", "diff_exp", "diff_recip", "diff_part", "diff_attn",
            "diff_pt", "diff_pt_ready", "diff_o"))
        s_oe, s_os, s_om, s_or, s_on, s_oy, s_dyt, s_dye = map(sem, (
            "diff_o_ready", "diff_o_sq", "diff_o_ms", "diff_o_root", "diff_o_norm", "diff_y", "diff_y_transposed",
            "diff_y_ready"))
        s_lm = sem("diff_lambda")

        N_CONST_BC = 5
        S_ROWS = 16 * sum(len(tile) for tile in VECTORS)
        block = ctx.enter_context(nc.Block())

        def w_view(w, ksub):
            return w.rearrange("(k p) n -> p k n", p=P)

        @block.sync
        def _(sp):
            sp.dma_start(CST[:], consts).then_inc(s_const, 16)
            for v, tile in enumerate(VECTORS):
                row = 0
                for name, layer, n in tile:
                    src = t[name] if layer is None else t[name][layer]
                    while len(src.shape) > 1:
                        src = src.rearrange("a b -> (a b)") if len(src.shape) == 2 else src.rearrange("a b c -> (a b) c") \
                            if len(src.shape) == 3 else src.rearrange("a b c d -> (a b) c d")
                    sp.dma_start(GR[row:row + n, v, :], src.rearrange("(r c) -> r c", c=P)).then_inc(s_rows, 16)
                    row += n
            sp.dma_start(MEMX, t["mem"].rearrange("b (t p) d -> p (b t) d", p=P)).then_inc(s_mem, 16)
            sp.dma_start(X[:], t["x"].rearrange("b (t p) d -> p (b t) d", p=P)).then_inc(s_x, 16)

            def unit(idx, w, k0, nk, col, n, i=None, per=0):
                dst = RA[:, idx % SLOTS, 0:nk * n].rearrange("p (k n) -> p k n", k=nk)
                cols = col if i is None else sp.snap(col)
                if idx >= SLOTS:
                    sp.wait_ge(s_wfree, idx - SLOTS + 1 + (0 if i is None else i * per))
                sp.dma_start(dst, w_view(w, 0)[:, k0:k0 + nk, bass.ds(cols, n)]).then_inc(s_w[idx % SLOTS], 16)

            def chunks(stage, w, col0, count, first=0, n=CHUNK, kt=KT, ksub=2):
                per = -(-kt // ksub)
                for c in range(first, first + count):
                    for u in range(per):
                        unit(UNIT0[stage] + c * per + u, w, u * ksub, min(ksub, kt - u * ksub), col0 + c * CHUNK, n)

            def chunk_loop(stage, w, col0, first, count):
                with sp.Fori(0, count) as i:
                    for u in range(KT // 2):
                        unit(UNIT0[stage] + first * 8 + u, w, u * 2, 2, i * CHUNK + (col0 + first * CHUNK), CHUNK, i, 8)

            def mod_units(chunk, layer, c, i=None):
                src = w_view(t["mod_w_2"][layer], 0)
                col = c * CHUNK if i is None else sp.snap(i * CHUNK + c * CHUNK)
                for u in range(KT):
                    f = chunk * KT + u
                    if f >= SLOTS:
                        sp.wait_ge(s_ffree, f - SLOTS + 1 + (0 if i is None else i * KT))
                    sp.dma_start(RF[:, f % SLOTS, :], src[:, u, bass.ds(col, CHUNK)]).then_inc(s_f[f % SLOTS], 16)

            def mod_loop(h):
                first = 1 if h.mod0 == 0 else 0
                if first:
                    mod_units(0, h.mod_layer, h.mod_chunk0)
                with sp.Fori(0, h.turns - first) as i:
                    mod_units(h.mod0 + first, h.mod_layer, h.mod_chunk0 + first, i)

            chunks("mkv0", t["ev_w_mem_kv"][0], 0, 2)
            chunks("mkv1", t["od_w_mem_kv"][0], 0, 2)
            chunks("ev_a", t["ev_w_in"][0], 0, 1)
            for u in range(8):
                unit(UNIT0["ev_a"] + 8 + u, t["ev_w_in"][0], 2 * u, 2, EV_CKV, EV_QKV - EV_CKV)
            chunk_loop("ev_b", t["ev_w_in"][0], EV_QKV, 0, 12)
            chunks("uq", t["ev_w_uq"][0], 0, 3, kt=4)
            chunks("ukv", t["ev_w_ukv"][0], 0, 2, kt=2)
            mod_loop(MEM_EV)
            mod_loop(MOBA)
            chunks("ukv", t["ev_w_ukv"][0], 0, 2, first=2, kt=2)
            chunks_out = lambda stage, w, kt, c, n: chunks(stage, w, 0, n, first=c, kt=kt)
            mod_loop(MLA)
            chunks_out("ev_out", t["ev_w_out"][0], EV_VW // P, 0, 4)
            chunk_loop("od_b", t["od_w_in"][0], 0, 0, 12)
            chunks("od_c", t["od_w_in"][0], 12 * CHUNK, 1, n=OD_IN - 12 * CHUNK)
            for h in OD_LOOPS:
                mod_loop(h)
            mod_units(N_MOD - 1, 1, 11)
            chunks_out("od_out", t["od_w_out"][0], OD_VW // P, 0, 4)

            gwv = t["lru_gate_w_2"][0].rearrange("d g n c e -> c d g n e")
            lw = t["lru_w_in_2"][0]

            def lru_units(i):
                loop = i is not None
                for b in range(2):
                    n = sp.snap(i * 2 + b) if loop else b
                    for part in range(2):
                        for half in range(2):
                            idx = UNIT0["lru_in"] + b * 4 + part * 2 + half
                            unit(idx, lw, half * 8, 8, i * 256 + (part * D + b * P) if loop else part * D + b * P, P,
                                 i, 8)
                    if loop:
                        sp.wait_ge(s_gt, i * 2 + b - 1)
                    for d in range(2):
                        for g in range(2):
                            sp.dma_start(GW[:, b, d * 2 + g, :], gwv[:, d, g, bass.ds(n, 1), :]).then_inc(s_gw[b], 16)
            lru_units(None)
            with sp.Fori(1, KT // 2) as i:
                lru_units(i)
            chunk_loop("lru_out", t["lru_w_out_2"][0], 0, 0, 4)
            with sp.Fori(0, GROUPS) as i:
                for j, part in enumerate((0, 3, 1, 2)):
                    for u in range(8):
                        unit(UNIT0["att_in"] + j * 8 + u, t["att_w_in_2"][0], u * 2, 2, i * CHUNK + part * D, CHUNK, i, 32)
            chunk_loop("att_out", t["att_w_out_2"][0], 0, 0, 4)
            ov = out.rearrange("b (t p) d -> p (b t) d", p=P)
            for c in range(4):
                sp.wait_ge(s_re, RES0["att_out"] + c + 1)
                sp.dma_start(ov[:, :, c * CHUNK:(c + 1) * CHUNK], X[:, :, c * CHUNK:(c + 1) * CHUNK]).then_inc(s_out, 16)
            sp.wait_ge(s_out, 64)

        @block.tensor
        def _(pe):
            def arrived(idx, i=None, per=0):
                v = 16 * (idx // SLOTS + 1)
                pe.wait_ge(s_w[idx % SLOTS], v if i is None else i * (16 * per // SLOTS) + v)

            def product(unit0, kt, ksub, n, banks, lhs, i=None, per=0):
                for u in range(-(-kt // ksub)):
                    arrived(unit0 + u, i, per)
                    slot = RA[:, (unit0 + u) % SLOTS, 0:ksub * n].rearrange("p (k n) -> p k n", k=ksub)
                    for k in range(u * ksub, min(kt, (u + 1) * ksub)):
                        for m, bank in enumerate(banks):
                            mm = pe.matmul(PS[:, bank, 0:n], lhs(k, m), slot[:, k - u * ksub, :],
                                           start=(k == 0), stop=(k == kt - 1))
                    mm.then_inc(s_wfree, 1)
                return mm

            def chunk(stage, c, unit0, kt, n, lhs, i=None, per=0, step=0):
                g = CHUNK0[stage] + c
                if g >= 2:
                    pe.wait_ge(s_ge, g - 1 if i is None else i * step + (g - 1))
                b = 2 * (g % 2)
                product(unit0, kt, 2, n, (b, b + 1), lhs, i, per)

            def residual(stage, lhs, kt):
                per = -(-kt // 2)
                for c in range(4):
                    q = RES0[stage] + c
                    if c >= 2:
                        pe.wait_ge(s_re, q - 1)
                    b = 2 * (c % 2)
                    product(UNIT0[stage] + c * per, kt, 2, CHUNK, (b, b + 1), lhs)

            fills = [0]

            def to_features(rows):
                for j in range(8):
                    p = fills[0]
                    if p >= 4:
                        pe.wait_ge(s_xeA if p % 2 else s_xeD, (p - 4) // 2 + 1)
                    for k in range(2):
                        for tt in range(TT):
                            at = (k * TT + tt) * P
                            mm = pe.transpose(PS[:, 4 + p % 4, at:at + P], rows[:, tt, (2 * j + k) * P:(2 * j + k + 1) * P], ident)
                    mm.then_inc(s_xt, 1)
                    fills[0] += 1

            def features_ready(n):
                pe.wait_ge(s_xeD, 4 * n)
                pe.wait_ge(s_xeA, 4 * n)

            def fill_mod(m, units, i=None):
                for u in units:
                    f = m * KT + u
                    v = 16 * (f // SLOTS + 1)
                    pe.wait_ge(s_f[f % SLOTS], v if i is None else i * (16 * KT // SLOTS) + v)
                    mm = pe.matmul(PS[0:2, 0, :], CTT[:, u, :], RF[:, f % SLOTS, :], start=(u == 0), stop=(u == KT - 1))
                    mm.then_inc(s_ffree, 1)

            def turn_mod(m, i=None):
                pe.wait_ge(s_mods, m + 1 if i is None else i + (m + 1))
                pe.wait_ge(s_modd, m + 1 if i is None else i + (m + 1))
                for j in range(4):
                    mm = pe.transpose(PS[:, 1, j * P:(j + 1) * P], MODS[:, j * P:(j + 1) * P], ident)
                mm.then_inc(s_modt, 1)

            def head_loop(h):
                H = HE if h in EV_LOOPS else HO
                with pe.Fori(0, h.turns) as i:
                    n = lambda a, plus: i * 2 + (h.n0 + a + plus)
                    pair = h.kind == "swa"
                    for a in range(1 if pair else 2):
                        pe.wait_ge(s_stg, n(1 if pair else a, 1))
                        pe.wait_ge(s_ye, n(1 if pair else a, 1))
                        for tt in range(TT):
                            pe.transpose(PS[:, 4 + a, tt * P:(tt + 1) * P], QS[:, a, tt, 0:P], ident)
                        for tt in range(TT):
                            mm = pe.transpose(PS[:, 4 + a, SEQ + tt * P:SEQ + (tt + 1) * P], KS[:, a, tt, :], ident)
                        if h.kind == "mla":
                            for tt in range(TT):
                                mm = pe.transpose(PS[0:ROPE, 6 + a, tt * P:(tt + 1) * P], QS[:, a, tt, NOPE:NOPE + ROPE], ident)
                        mm.then_inc(s_t1, 2 if pair else 1)
                    fill_mod(h.mod0, range(0, 6), i)
                    for a in range(2):
                        pe.wait_ge(s_qk, n(1 if pair else a, 1))
                        if pair:
                            qk = QKT[64 * a:64 * a + 64, 0, :]
                        else:
                            qk = QKT[:, a, :]
                        for tt in range(TT):
                            mla = h.kind == "mla"
                            mm = pe.matmul(PS[:, 6 + a, tt * SEQ:(tt + 1) * SEQ], qk[:, tt * P:(tt + 1) * P], qk[:, SEQ:2 * SEQ],
                                           start=True, stop=not mla)
                            if mla:
                                mm = pe.matmul(PS[:, 6 + a, tt * SEQ:(tt + 1) * SEQ], QRT[0:ROPE, a, tt * P:(tt + 1) * P],
                                               KPT[0:ROPE, :], start=False, stop=True)
                        mm.then_inc(s_sc, 1)
                    fill_mod(h.mod0, range(6, 12), i)
                    for a in range(2):
                        pe.wait_ge(s_ex, n(a, 1))
                        for tt in range(TT):
                            for kt in range(TT):
                                mm = pe.transpose(PS[:, 4 + a, kt * SEQ + tt * P:kt * SEQ + (tt + 1) * P],
                                                  S[:, a, tt, kt * P:(kt + 1) * P], ident)
                        mm.then_inc(s_pt, 1)
                    fill_mod(h.mod0, range(12, 16), i)
                    for a in range(2):
                        pe.wait_ge(s_pe, n(a, 1))
                        for tt in range(TT):
                            for kt in range(TT):
                                if pair:
                                    v = H[:, kt, h.v:h.v + SWA_DH]
                                elif h.mem is not None:
                                    v = MKV[:, h.mem, kt, bass.ds(i * 256 + (h.v + a * P), P)]
                                else:
                                    width = NOPE + MLA_DV if h.kind == "mla" else P
                                    v = H[:, kt, bass.ds(i * (2 * width) + (h.v + a * width), P)]
                                w = SWA_DH if pair else P
                                mm = pe.matmul(PS[:, 6 + a, tt * P:tt * P + w],
                                               PT[:, a, kt * SEQ + tt * P:kt * SEQ + (tt + 1) * P], v,
                                               start=(kt == 0), stop=(kt == TT - 1))
                        mm.then_inc(s_o, 1)
                    turn_mod(h.mod0, i)
                    for a in range(1 if pair else 2):
                        pe.wait_ge(s_ys, n(1 if pair else a, 1))
                        for tt in range(TT):
                            mm = pe.transpose(PS[:, 4 + a, tt * P:(tt + 1) * P], YS[:, a, tt, :], ident)
                        mm.then_inc(s_yt, 2 if pair else 1)

            pe.sem_inc(s_t1, 2)
            pe.wait_ge(s_const, 16)
            pe.wait_ge(s_rows, S_ROWS)
            for v, rows in enumerate(VEC_ROWS):
                mm = pe.transpose(PS[:, 0, v * P:v * P + rows], GR[0:rows, v, :], ident[0:rows, 0:rows])
            mm.then_inc(s_vt, 1)
            pe.wait_ge(s_mem, 16)
            to_features(MEMX)
            pe.wait_ge(s_x, 16)
            to_features(X)
            pe.wait_ge(s_vec, 4)
            features_ready(1)
            for l, lhs in enumerate((MT0, MT1)):
                for c in range(2):
                    chunk(f"mkv{l}", c, UNIT0[f"mkv{l}"] + 8 * c, KT, CHUNK, lambda k, m: lhs[:, k, m * P:(m + 1) * P])
            features_ready(2)
            xt = lambda k, m: XT[:, k, m * P:(m + 1) * P]
            chunk("ev_a", 0, UNIT0["ev_a"], KT, CHUNK, xt)
            chunk("ev_a", 1, UNIT0["ev_a"] + 8, KT, EV_QKV - EV_CKV, xt)
            with pe.Fori(0, 6) as i:
                for c in range(2):
                    chunk("ev_b", c, UNIT0["ev_b"] + 8 * c, KT, CHUNK, xt, i, 16, 2)
            pe.wait_ge(s_xeD, 8)
            pe.wait_ge(s_ge, 6)
            for k in range(6):
                col = k * P if k < 4 else EV_CKV + (k - 4) * P
                for tt in range(TT):
                    at = (k % 2 * TT + tt) * P
                    mm = pe.transpose(PS[:, 4 + k // 2, at:at + P], HE[:, tt, col:col + P], ident)
            pe.wait_ge(s_rope, 1)
            for tt in range(TT):
                mm = pe.transpose(PS[0:ROPE, 7, tt * P:(tt + 1) * P], HE[:, tt, EV_KPE:EV_KPE + ROPE], ident)
            mm.then_inc(s_ct, 1)
            pe.wait_ge(s_cte, 1)
            pe.wait_ge(s_cond, 1)
            pe.wait_ge(s_ge, CHUNK0["uq"])
            head_loop(MEM_EV)
            head_loop(MOBA)
            pe.wait_ge(s_modd, MLA.mod0 + 1)
            for c in range(3):
                chunk("uq", c, UNIT0["uq"] + 2 * c, 4, CHUNK, lambda k, m: CQT[:, k, m * P:(m + 1) * P])
            for c in range(4):
                chunk("ukv", c, UNIT0["ukv"] + c, 2, CHUNK, lambda k, m: CKVT[:, k, m * P:(m + 1) * P])
            pe.wait_ge(s_ge, CHUNK0["od_b"])
            head_loop(MLA)
            pe.wait_ge(s_ye, 20 + 2)
            pe.wait_ge(s_modd, SWA[0].mod0 + 1)
            yt = lambda k, m: AT[:, k * SEQ + m * P:k * SEQ + (m + 1) * P]
            residual("ev_out", yt, EV_VW // P)
            pe.wait_ge(s_re, RES0["od_out"])
            to_features(X)
            features_ready(3)
            with pe.Fori(0, 6) as i:
                for c in range(2):
                    chunk("od_b", c, UNIT0["od_b"] + 8 * c, KT, CHUNK, xt, i, 16, 2)
            chunk("od_c", 0, UNIT0["od_c"], KT, OD_IN - 12 * CHUNK, xt)
            pe.wait_ge(s_ge, CHUNK0["od_c"] + 1)
            for h in OD_LOOPS:
                head_loop(h)
            fill_mod(N_MOD - 1, range(KT))
            turn_mod(N_MOD - 1)
            pe.wait_ge(s_ye, N_HEADS + 2)
            pe.wait_ge(s_modd, N_MOD + 1)
            residual("od_out", yt, OD_VW // P)

            pe.wait_ge(s_xn, 1)
            to_features(CN)
            pe.wait_ge(s_xn, 2)
            to_features(XN)
            features_ready(5)

            with pe.Fori(0, KT // 2) as i:
                for b in range(2):
                    n = lambda plus: i * 2 + (b + plus)
                    pe.wait_ge(s_xc, n(1))
                    for part in range(2):
                        if part:
                            pe.wait_ge(s_gs, n(1))
                        for half in range(2):
                            idx = UNIT0["lru_in"] + b * 4 + part * 2 + half
                            arrived(idx, i, 8)
                            for k in range(8):
                                mm = pe.matmul(PS[:, part * 2 + b, :], RA[:, idx % SLOTS, k * P:(k + 1) * P], HT[:, half * 8 + k, :],
                                               start=(half == 0 and k == 0), stop=(half == 1 and k == 7))
                            mm.then_inc(s_wfree, 1)
                    pe.wait_ge(s_xc, n(3))
                    pe.wait_ge(s_gw[b], i * 64 + 64)
                    pe.wait_ge(s_sg, n(1))
                    for j in range(4):
                        mm = pe.matmul(PS[:, 4 + j, :], GW[:, b, j, :], XC[:, b, :, :].rearrange("p c s -> p (c s)"),
                                       start=True, stop=True)
                    mm.then_inc(s_gt, 1)

            def gate_rows(first, banks, base):
                for j in range(4):
                    if j >= 2 or base:
                        pe.wait_ge(s_gbe, base + j - 1)
                    pe.wait_ge(s_dg, base + j + 1)
                    for k in range(4):
                        mm = pe.matmul(PS[:, banks + j % 2, k * P:(k + 1) * P], ONES, DIAG(base + j)[:, k, :], start=True, stop=True)
                    mm.then_inc(s_gb, 1)

            pe.wait_ge(s_y, KT + 2)
            gate_rows(0, 0, 0)
            gate_rows(1, 0, 4)
            pe.wait_ge(s_gbe, 8)
            with pe.Fori(0, 2) as i:
                for c in range(2):
                    pe.wait_ge(s_re, i * 2 + (RES0["lru_out"] + c - 1))
                    product(UNIT0["lru_out"] + c * 8, KT, 2, CHUNK, range(4 * c, 4 * c + 4),
                            lambda k, m: YL[:, k, m * P:(m + 1) * P], i, 16)

            pe.wait_ge(s_re, RES0["att_out"])
            pe.wait_ge(s_xn, 3)
            to_features(CN)
            pe.wait_ge(s_xn, 4)
            to_features(XN)
            features_ready(7)
            with pe.Fori(0, GROUPS) as i:
                for j, tiles in enumerate(((2, 3), (2, 3), (0, 1, 2, 3), (0, 1, 2, 3))):
                    b0 = (0, 2, 4, 0)[j]
                    if j == 0:
                        pe.wait_ge(s_dye, i + 1)
                    if j == 3:
                        pe.wait_ge(s_dqe, i * 4 + 2)
                    product(UNIT0["att_in"] + j * 8, KT, 2, CHUNK, range(b0, b0 + len(tiles)),
                            lambda k, m: HT[:, k, tiles[m] * P:(tiles[m] + 1) * P], i, 32)
                pe.wait_ge(s_dqe, i * 4 + 4)
                pe.wait_ge(s_qn, i + 1)
                for j in range(4):
                    a = j % 2
                    if j >= 1:
                        pe.wait_ge(s_e2, i * 4 + j)
                    for kt in range(4):
                        pe.transpose(PS[:, 4, kt * P:(kt + 1) * P], RQK[:, kt, j * P:(j + 1) * P], ident)
                    for tt in range(TT):
                        mm = pe.transpose(PS[:, 5, tt * P:(tt + 1) * P], RQK[:, 4 + tt, j * P:(j + 1) * P], ident)
                    mm.then_inc(s_e1, 1)
                    pe.wait_ge(s_e2, i * 4 + (j + 1))
                    for tt in range(TT):
                        e = tt
                        s = 2 * j + tt
                        if s >= 2:
                            pe.wait_ge(s_e5, i * 8 + (s - 1))
                        for c in range(2):
                            mm = pe.matmul(PS[:, 2 * e + c, :], DQK[64 * c:64 * c + 64, a, CHUNK + tt * P:CHUNK + (tt + 1) * P],
                                           DQK[64 * c:64 * c + 64, a, 0:CHUNK], start=True, stop=True)
                        mm.then_inc(s_e3, 1)
                    for tt in range(TT):
                        s = 2 * j + tt
                        pe.wait_ge(s_e8, i * 8 + (s + 1))
                        if s >= 1:
                            pe.wait_ge(s_e10, i * 8 + s)
                        for kt in range(4):
                            mm = pe.transpose(PS[:, 6, kt * P:(kt + 1) * P], DE[:, tt, 0, kt * P:(kt + 1) * P], ident)
                        mm.then_inc(s_e9, 1)
                        pe.wait_ge(s_e10, i * 8 + (s + 1))
                        if s >= 1:
                            pe.wait_ge(s_oe, i * 8 + s)
                        for kt in range(4):
                            mm = pe.matmul(PS[:, 7, 0:P], DPT[:, tt, kt * P:(kt + 1) * P], RV[:, kt, j * P:(j + 1) * P],
                                           start=(kt == 0), stop=(kt == 3))
                        mm.then_inc(s_e11, 1)
                pe.wait_ge(s_oy, i + 1)
                for j in range(4):
                    for tt in range(TT):
                        mm = pe.transpose(PS[:, 4 + j // 2, (j % 2 * TT + tt) * P:(j % 2 * TT + tt + 1) * P],
                                          OS[:, tt, j * P:(j + 1) * P], ident)
                mm.then_inc(s_dyt, 1)
            pe.wait_ge(s_dye, GROUPS + 1)
            gate_rows(2, 4, 8)
            pe.wait_ge(s_gbe, 12)
            with pe.Fori(0, 2) as i:
                for c in range(2):
                    pe.wait_ge(s_re, i * 2 + (RES0["att_out"] + c - 1))
                    product(UNIT0["att_out"] + c * 8, KT, 2, CHUNK, (2 * c, 2 * c + 1),
                            lambda k, m: DYT[:, k, m * P:(m + 1) * P], i, 16)

        @block.scalar
        def _(act):
            act.dma_start(SUBG, t["att_subln_2"][0].unsqueeze(0).to_broadcast([P, 128])).then_inc(s_bc, 16)
            act.dma_start(QG, t["att_q_norm_2"][0].unsqueeze(0).to_broadcast([P, 64])).then_inc(s_bc, 16)
            act.dma_start(KG, t["att_k_norm_2"][0].unsqueeze(0).to_broadcast([P, 64])).then_inc(s_bc, 16)
            act.dma_start(LV, t["att_lambda_2"][0].rearrange("a b -> (a b)").unsqueeze(0).to_broadcast([P, 256])).then_inc(s_bc, 16)
            act.dma_start(SINK, t["od_sinks"][0].unsqueeze(0).to_broadcast([P, 16])).then_inc(s_bc, 16)

            def squares(r, rows):
                for j, row in enumerate(rows):
                    if SQUARED[r] - len(rows) + j:
                        act.wait_ge(s_sq, SQUARED[r] - len(rows) + j)
                    act.activation(JUNK[:, 0:row.shape[-1]], row, ACT.Square, accum_out=ST[:, r, j:j + 1]).then_inc(s_sq, 1)

            def root(r, n):
                act.wait_ge(s_ms, r + 1)
                act.activation(ST[:, r, 0:n], ST[:, r, 0:n], ACT.Sqrt).then_inc(s_rt, 1)

            fills = [0]

            def take_features(scales, shifts, dests):
                for j in range(8):
                    p = fills[0]
                    fills[0] += 1
                    if p % 2 == 0:
                        continue
                    act.wait_ge(s_xt, p + 1)
                    for k in range(2):
                        src = PS[:, 4 + p % 4, k * SEQ:(k + 1) * SEQ]
                        for scale, dest in zip(scales, dests):
                            bias = 0.0 if shifts is None else shifts(2 * j + k)
                            ins = act.activation(dest(2 * j + k), src, ACT.Identity, scale=scale(2 * j + k), bias=bias)
                    ins.then_inc(s_xeA, 1)

            def evict(stage, c, dest, r, j0=0, n=CHUNK, silu=False, i=None, step=0):
                g = CHUNK0[stage] + c
                act.wait_ge(s_wfree, multiplied(stage, c) if i is None else i * (8 * step) + multiplied(stage, c))
                for m in range(TT):
                    ins = act.activation(dest(m), PS[:, 2 * (g % 2) + m, 0:n], ACT.Silu if silu else ACT.Copy,
                                         scale=ST[:, r, j0 + m:j0 + m + 1])
                ins.then_inc(s_ge, 1)

            def head_loop(h):
                with act.Fori(0, h.turns) as i:
                    n = lambda a, plus: i * 2 + (h.n0 + a + plus)
                    pair = h.kind == "swa"
                    for a in range(1 if pair else 2):
                        act.wait_ge(s_t1, n(1 if pair else a, 3))
                        ins = act.copy(QKT[:, a, :], PS[:, 4 + a, :])
                        if h.kind == "mla":
                            ins = act.copy(QRT[0:ROPE, a, :], PS[0:ROPE, 6 + a, 0:SEQ])
                        ins.then_inc(s_qk, 2 if pair else 1)
                    for a in range(2):
                        act.wait_ge(s_mx, n(a, 1))
                        for tt in range(TT):
                            ins = act.activation(S[:, a, tt, :], S[:, a, tt, :], ACT.Exp, bias=NM[:, a, tt:tt + 1],
                                                 accum_out=LS[:, a, tt:tt + 1])
                        if pair:
                            ins = act.activation(ES[:, a, :], SN[:, a, :], ACT.Exp)
                        ins.then_inc(s_ex, 1)
                    for a in range(1 if pair else 2):
                        act.wait_ge(s_yt, n(1 if pair else a, 1))
                        y = i * SEQ + h.y0 * SEQ if pair else i * (2 * SEQ) + (h.y0 + a) * SEQ
                        act.copy(AT[:, bass.ds(y, SEQ)], PS[:, 4 + a, 0:SEQ]).then_inc(s_ye, 2 if pair else 1)

            act.wait_ge(s_mem, 16)
            squares(0, [MEMX[:, tt, :] for tt in range(TT)])
            act.wait_ge(s_x, 16)
            squares(1, [X[:, tt, :] for tt in range(TT)])
            root(0, 2)
            root(1, 2)
            act.wait_ge(s_vec, 4)
            gvec = lambda name: (lambda k: vec(name, k))
            take_features([gvec("ev_mem_norm_g"), gvec("od_mem_norm_g")], None,
                          [lambda k: MT0[:, k, :], lambda k: MT1[:, k, :]])
            take_features([gvec("ev_norm_g")], None, [lambda k: XT[:, k, :]])
            act.activation(CTT[:], GT[:, VEC_AT["c_2"]:VEC_AT["c_2"] + 32].rearrange("p (v k) -> p k v", v=2),
                           ACT.Silu).then_inc(s_cond, 1)
            act.sem_inc(s_ye, 2)
            act.wait_ge(s_lam, 1)
            act.activation(SC[:, 0:32], SC[:, 0:32], ACT.Exp, scale=-1.0)
            act.activation(SC[:, 64:66], SC[:, 64:66], ACT.Exp).then_inc(s_exl, 1)
            act.wait_ge(s_rs, 2)
            for l in range(2):
                for c in range(2):
                    evict(f"mkv{l}", c, lambda m: MKV[:, l, m, c * CHUNK:(c + 1) * CHUNK], 0)
            evict("ev_a", 0, lambda m: HE[:, m, 0:MLA_QR], 1)
            evict("ev_a", 1, lambda m: HE[:, m, EV_CKV:EV_QKV], 1, n=EV_QKV - EV_CKV)
            ev = lambda c, i=None: (lambda m: HE[:, m, EV_QKV + c * CHUNK:EV_QKV + (c + 1) * CHUNK] if i is None
                                    else HE[:, m, bass.ds(i * 1024 + (EV_QKV + c * CHUNK), CHUNK)])
            with act.Fori(0, 3) as i:
                for c in range(2):
                    evict("ev_b", c, ev(c, i), 1, i=i, step=2)
            evict("ev_b", 6, ev(6), 1)
            evict("ev_b", 7, ev(7), 1, silu=True)
            with act.Fori(0, 2) as i:
                for c in range(8, 10):
                    evict("ev_b", c, ev(c, i), 1, silu=True, i=i, step=2)
            for j, (lo, hi) in enumerate(((0, MLA_QR), (0, MLA_QR), (EV_CKV, EV_KPE), (EV_CKV, EV_KPE))):
                act.wait_ge(s_sq, SQUARED[1] + j)
                act.activation(a_pt[:, 0:hi - lo], HE[:, j % 2, lo:hi], ACT.Square, accum_out=ST[:, 2, j:j + 1]).then_inc(s_sq, 1)
            root(2, 4)
            head_loop(MEM_EV)
            head_loop(MOBA)
            act.wait_ge(s_rs, 3)
            for c in range(3):
                evict("uq", c, lambda m: HE[:, m, EV_QA + c * CHUNK:EV_QA + (c + 1) * CHUNK], 2, 0)
            for c in range(4):
                evict("ukv", c, lambda m: HE[:, m, EV_KVA + c * CHUNK:EV_KVA + (c + 1) * CHUNK], 2, 2)
            head_loop(MLA)

            act.wait_ge(s_re, RES0["od_out"])
            squares(3, [X[:, tt, :] for tt in range(TT)])
            take_features([gvec("od_norm_g")], None, [lambda k: XT[:, k, :]])
            root(3, 2)
            act.wait_ge(s_rs, 4)
            od = lambda c, i=None: (lambda m: HO[:, m, c * CHUNK:(c + 1) * CHUNK] if i is None
                                    else HO[:, m, bass.ds(i * 1024 + c * CHUNK, CHUNK)])
            with act.Fori(0, 4) as i:
                for c in range(2):
                    evict("od_b", c, od(c, i), 3, i=i, step=2)
            with act.Fori(0, 2) as i:
                for c in range(8, 10):
                    evict("od_b", c, od(c, i), 3, silu=True, i=i, step=2)
            evict("od_c", 0, lambda m: HO[:, m, 12 * CHUNK:OD_IN], 3, n=OD_IN - 12 * CHUNK, silu=True)
            for h in OD_LOOPS:
                head_loop(h)
            act.wait_ge(s_o, N_HEADS)
            act.dma_start(CX, t["ctx_2"].rearrange("b (t p) d -> p (b t) d", p=P)).then_inc(s_ctx, 16)
            act.wait_ge(s_ffree, N_MOD * KT)
            act.dma_start(FG, t["final_norm_g"].unsqueeze(0).to_broadcast([P, D])).then_inc(s_fg, 16)

            act.wait_ge(s_re, RES0["lru_out"])
            squares(4, [X[:, tt, :] for tt in range(TT)])
            root(4, 2)
            act.wait_ge(s_ctx, 16)
            squares(5, [CX[:, tt, :] for tt in range(TT)])
            root(5, 2)
            act.wait_ge(s_xf, 1)
            squares(6, [X[:, tt, :] for tt in range(TT)])
            root(6, 2)
            mod_scale = lambda j: (lambda k: MSC[:, 16 * j + k:16 * j + k + 1])
            mod_shift = lambda l, w: (lambda k: MODT[:, l, k, w:w + 1])
            act.wait_ge(s_msc, 4)
            take_features([mod_scale(1)], mod_shift(0, 1), [lambda k: HT[:, k, 0:SEQ]])
            take_features([mod_scale(0)], mod_shift(0, 0), [lambda k: HT[:, k, SEQ:2 * SEQ]])
            act.sem_inc(s_sg, 1)
            with act.Fori(0, KT // 2) as i:
                for b in range(2):
                    n = lambda plus: i * 2 + (b + plus)
                    act.wait_ge(s_gt, n(1))
                    act.wait_ge(s_y, n(2))
                    for j in range(4):
                        act.activation(RI[:, j, :], PS[:, 4 + j, :], ACT.Sigmoid, bias=BV[:, b, 5 + j:6 + j])
                    act.activation(SG, PS[:, 2 + b, :], ACT.Sigmoid).then_inc(s_sg, 1)
                    act.wait_ge(s_sg, n(2))
                    for d in range(2):
                        act.activation(LA[:, d, :], RI[:, 2 * d, :], ACT.Exp, scale=BV[:, b, 9 + d:10 + d])
                    for d in range(2):
                        ins = act.activation(LW[:, d, :], RI[:, 2 * d, :], ACT.Tanh, scale=BV[:, b, 9 + d:10 + d])
                    ins.then_inc(s_ab, 1)
                    act.wait_ge(s_w2, n(1))
                    act.activation(LWF, LWF, ACT.Sqrt, scale=-1.0).then_inc(s_sqr, 1)

            def gate_rows_out(dest, banks, base):
                for j in range(4):
                    act.wait_ge(s_gb, base + j + 1)
                    act.copy(dest[:, j * CHUNK:(j + 1) * CHUNK], PS[:, banks + j % 2, :]).then_inc(s_gbe, 1)
            gate_rows_out(G_LAT, 0, 0)
            gate_rows_out(G_CTX, 0, 4)

            act.wait_ge(s_re, RES0["att_out"])
            squares(7, [CX[:, tt, :] for tt in range(TT)])
            root(7, 2)
            squares(8, [X[:, tt, :] for tt in range(TT)])
            root(8, 2)
            take_features([mod_scale(3)], mod_shift(1, 1), [lambda k: HT[:, k, 0:SEQ]])
            take_features([mod_scale(2)], mod_shift(1, 0), [lambda k: HT[:, k, SEQ:2 * SEQ]])
            act.sem_inc(s_dye, 1)
            with act.Fori(0, GROUPS) as i:
                for j, (dest, tiles, b0) in enumerate(((RQK[:, 4:6, :], 2, 0), (RG, 2, 2), (RQK[:, 0:4, :], 4, 4), (RV, 4, 0))):
                    act.wait_ge(s_wfree, i * 32 + multiplied("att_in", j))
                    for m in range(tiles):
                        if j == 1:
                            ins = act.activation(dest[:, m, :], PS[:, b0 + m, :], ACT.Silu)
                        else:
                            ins = act.copy(dest[:, m, :], PS[:, b0 + m, :])
                    ins.then_inc(s_dqe, 1)
                act.wait_ge(s_dm, i + 1)
                act.activation(DS48, DS48, ACT.Sqrt).then_inc(s_dp0, 1)
                for j in range(4):
                    a = j % 2
                    act.wait_ge(s_e1, i * 4 + (j + 1))
                    act.copy(DQK[:, a, 0:CHUNK], PS[:, 4, :])
                    act.copy(DQK[:, a, CHUNK:CHUNK + SEQ], PS[:, 5, 0:SEQ]).then_inc(s_e2, 1)
                    for tt in range(TT):
                        act.wait_ge(s_e4, i * 8 + (2 * j + tt + 1))
                        for c in range(2):
                            ins = act.activation(DE[:, tt, c, :], PS[:, 2 * tt + c, :], ACT.Exp, bias=NM[:, tt, c:c + 1],
                                                 accum_out=LS[:, tt, c:c + 1])
                        ins.then_inc(s_e5, 1)
                    for tt in range(TT):
                        act.wait_ge(s_e9, i * 8 + (2 * j + tt + 1))
                        act.copy(DPT[:, tt, :], PS[:, 6, :]).then_inc(s_e10, 1)
                act.wait_ge(s_om, i + 1)
                act.activation(DS8, DS8, ACT.Sqrt).then_inc(s_or, 1)
                act.wait_ge(s_dyt, i + 1)
                for j in range(2):
                    ins = act.copy(DYT[:, bass.ds(i * 4 + 2 * j, 2), :], PS[:, 4 + j, :].rearrange("p (k s) -> p k s", k=2))
                ins.then_inc(s_dye, 1)
            gate_rows_out(G_ATT, 4, 8)

        @block.vector
        def _(dve):
            steps = [0]

            def link(ins):
                steps[0] += 1
                ins.then_inc(s_dve, 1)
                dve.wait_ge(s_dve, steps[0])

            def mean_square(r, widths):
                dve.wait_ge(s_sq, SQUARED[r])
                at = 0
                for n, width in widths:
                    ins = dve.tensor_scalar(ST[:, r, at:at + n], ST[:, r, at:at + n], 1.0 / width, EPS, ALU.mult, ALU.add)
                    at += n
                ins.then_inc(s_ms, 1)

            def rstd(r, n):
                dve.wait_ge(s_rt, r + 1)
                dve.reciprocal(ST[:, r, 0:n], ST[:, r, 0:n]).then_inc(s_rs, 1)

            fills = [0]

            def take_features(scales, shifts, dests):
                for j in range(8):
                    p = fills[0]
                    fills[0] += 1
                    if p % 2:
                        continue
                    dve.wait_ge(s_xt, p + 1)
                    for k in range(2):
                        src = PS[:, 4 + p % 4, k * SEQ:(k + 1) * SEQ]
                        for scale, dest in zip(scales, dests):
                            kk = 2 * j + k
                            if shifts is None:
                                ins = dve.tensor_scalar(dest(kk), src, scale(kk), None, ALU.mult)
                            else:
                                ins = dve.tensor_scalar(dest(kk), src, scale(kk), shifts(kk), ALU.mult, ALU.add)
                    ins.then_inc(s_xeD, 1)

            def rope(x, table, rot, heads):
                tab = const(table).rearrange("p (t z c) -> p t z c", t=TT, z=2)
                half = rot // 2
                ra = ROT_A[:, 0:heads * rot].rearrange("p (h c) -> p h c", h=heads)
                rb = ROT_B[:, 0:heads * rot].rearrange("p (h c) -> p h c", h=heads)

                def wide(z, tt, lo, hi):
                    return tab[:, tt, z, lo:hi].unsqueeze(1).to_broadcast([P, heads, hi - lo])
                for tt in range(TT):
                    v = x(tt)
                    dve.tensor_tensor(out=ra, in0=v, in1=wide(0, tt, 0, rot), op=ALU.mult)
                    dve.tensor_tensor(out=rb[:, :, 0:half], in0=v[:, :, half:rot], in1=wide(1, tt, 0, half), op=ALU.mult)
                    link(dve.tensor_tensor(out=rb[:, :, half:rot], in0=v[:, :, 0:half], in1=wide(1, tt, half, rot), op=ALU.mult))
                    link(dve.tensor_tensor(out=v, in0=ra, in1=rb, op=ALU.add))
                dve.sem_inc(s_rope, 1)

            def residual_add(stage):
                for c in range(4):
                    q = RES0[stage] + c
                    dve.wait_ge(s_wfree, multiplied(stage, c))
                    for m in range(TT):
                        x = X[:, m, c * CHUNK:(c + 1) * CHUNK]
                        ins = dve.tensor_tensor(out=x, in0=PS[:, 2 * (c % 2) + m, :], in1=x, op=ALU.add)
                    ins.then_inc(s_re, 1)

            def mod_rows(m, i=None):
                dve.wait_ge(s_ffree, KT * (m + 1) if i is None else i * KT + KT * (m + 1))
                dve.tensor_copy(MODS[0:2, :], PS[0:2, 0, :]).then_inc(s_mods, 1)

            def mod_columns(m, layer, c, i=None):
                dve.wait_ge(s_modt, m + 1 if i is None else i + (m + 1))
                at = 4 * c if i is None else i * 4 + 4 * c
                bias = GT[:, bass.ds(at + (VEC_AT["mod_b_2"] + 48 * layer), 4)]
                dve.tensor_tensor(out=MODT[:, layer, bass.ds(at, 4), :], in0=PS[:, 1, :].rearrange("p (k w) -> p k w", w=P)[:, :, 0:2],
                                  in1=bias.unsqueeze(2).to_broadcast([P, 4, 2]), op=ALU.add).then_inc(s_modd, 1)

            def head_loop(h):
                H = HE if h in EV_LOOPS else HO
                with dve.Fori(0, h.turns) as i:
                    n = lambda a, plus: i * 2 + (h.n0 + a + plus)
                    pair = h.kind == "swa"
                    for a in range(2):
                        dve.wait_ge(s_sc, n(a, 1))
                        flat = S[:, a, :, :].rearrange("p t c -> p (t c)")
                        if h.mask is None:
                            ins = dve.tensor_scalar(flat, PS[:, 6 + a, :], h.scale, None, ALU.mult)
                        else:
                            ins = dve.scalar_tensor_tensor(out=flat, in0=PS[:, 6 + a, :], scalar=h.scale, in1=const(h.mask),
                                                           op0=ALU.mult, op1=ALU.add)
                        ins.then_inc(s_sm, 1)
                        dve.wait_ge(s_sm, n(a, 1))
                        ins = dve.tensor_reduce(NM[:, a, :], S[:, a, :, :], AX, ALU.max, negate=True)
                        if pair:
                            ins.then_inc(s_sk, 1)
                            w = i * 2 + (h.sink + a + 1)
                            dve.wait_ge(s_sk, w)
                            nsink = NSINK[:, bass.ds(i * 2 + (h.sink + a), 1), :].squeeze(1)
                            dve.tensor_tensor(out=NM[:, a, :], in0=NM[:, a, :], in1=nsink, op=ALU.min).then_inc(s_sk2, 1)
                            dve.wait_ge(s_sk2, w)
                            ins = dve.tensor_tensor(out=SN[:, a, :], in0=NM[:, a, :], in1=nsink, op=ALU.subtract)
                        ins.then_inc(s_mx, 1)
                    for a in range(2):
                        dve.wait_ge(s_pt, n(a, 1))
                        dve.tensor_copy(PT[:, a, :], PS[:, 4 + a, :]).then_inc(s_pe, 1)
                    mod_rows(h.mod0, i)
                    for a in range(2):
                        dve.wait_ge(s_o, n(a, 1))
                        if pair:
                            dve.tensor_tensor(out=LS[:, a, :], in0=LS[:, a, :], in1=ES[:, a, :], op=ALU.add).then_inc(s_l2, 1)
                            dve.wait_ge(s_l2, i * 2 + (h.sink + a + 1))
                        dve.reciprocal(RL[:, a, :], LS[:, a, :]).then_inc(s_rl, 1)
                        dve.wait_ge(s_rl, n(a, 1))
                        w = SWA_DH if pair else P
                        for tt in range(TT):
                            y = YS[:, 0, tt, a * w:(a + 1) * w] if pair else YS[:, a, tt, :]
                            gate = H[:, tt, bass.ds(i * (2 * w) + (h.gate + a * w), w)]
                            ins = dve.scalar_tensor_tensor(out=y, in0=PS[:, 6 + a, tt * P:tt * P + w], scalar=RL[:, a, tt:tt + 1],
                                                           in1=gate, op0=ALU.mult, op1=ALU.mult)
                        ins.then_inc(s_ys, 1)
                    mod_columns(h.mod0, h.mod_layer, h.mod_chunk0, i)

            dve.wait_ge(s_vt, 1)
            for v, rows in enumerate(VEC_ROWS):
                dve.tensor_copy(GT[:, v * P:v * P + rows], PS[:, 0, v * P:v * P + rows]).then_inc(s_vec, 1)
            link(dve.memset(MODS[:], 0.0))
            dve.sem_inc(s_modd, 1)
            dve.wait_ge(s_vec, 4)
            mean_square(0, [(2, D)])
            mean_square(1, [(2, D)])
            gvec = lambda name: (lambda k: vec(name, k))
            take_features([gvec("ev_mem_norm_g"), gvec("od_mem_norm_g")], None,
                          [lambda k: MT0[:, k, :], lambda k: MT1[:, k, :]])
            rstd(0, 2)
            take_features([gvec("ev_norm_g")], None, [lambda k: XT[:, k, :]])
            rstd(1, 2)

            lam = vec("lru_lambda_2", 0, 32)
            dve.wait_ge(s_bc, 16 * N_CONST_BC)
            link(dve.tensor_scalar(SC[:, 32:64], lam, -1.0, None, ALU.mult))
            dve.tensor_tensor(out=SC[:, 0:32], in0=lam, in1=SC[:, 32:64], op=ALU.max)
            dve.tensor_tensor(out=DT1S[:, 0:64], in0=LV[:, 0:64], in1=LV[:, 64:128], op=ALU.mult)
            link(dve.tensor_tensor(out=DT1S[:, 64:128], in0=LV[:, 128:192], in1=LV[:, 192:256], op=ALU.mult))
            dve.tensor_reduce(SC[:, 64:66], DT1S[:, 0:128].rearrange("p (z c) -> p z c", z=2), AX, ALU.add).then_inc(s_lam, 1)
            dve.wait_ge(s_exl, 1)
            link(dve.tensor_tensor(out=SC[:, 66:67], in0=SC[:, 65:66], in1=SC[:, 64:65], op=ALU.subtract))
            link(dve.tensor_scalar(NLAM, SC[:, 66:67], -LAM_INIT, None, ALU.add))
            dve.tensor_scalar(SUBG, SUBG, 1.0 - LAM_INIT, None, ALU.mult)
            dve.tensor_scalar(QG, QG, ATT_DH ** -0.5, None, ALU.mult)
            dve.tensor_scalar(NSINK, SINK.unsqueeze(2).to_broadcast([P, SWA_HEADS, 2]), -1.0, None, ALU.mult)
            y, z, z2, acc = SC[:, 0:32], SC[:, 68:100], SC[:, 100:132], SC[:, 132:164]
            link(dve.tensor_scalar(z, y, 2.0, None, ALU.add))
            link(dve.reciprocal(z, z))
            link(dve.tensor_tensor(out=z, in0=z, in1=y, op=ALU.mult))
            link(dve.tensor_tensor(out=z2, in0=z, in1=z, op=ALU.mult))
            link(dve.tensor_scalar(acc, z2, 1.0 / 19, 1.0 / 17, ALU.mult, ALU.add))
            for k in range(15, 0, -2):
                link(dve.tensor_tensor(out=acc, in0=acc, in1=z2, op=ALU.mult))
                link(dve.tensor_scalar(acc, acc, 1.0 / k, None, ALU.add))
            link(dve.tensor_tensor(out=acc, in0=acc, in1=z, op=ALU.mult))
            link(dve.tensor_scalar(z, SC[:, 32:64], 0.0, None, ALU.max))
            link(dve.scalar_tensor_tensor(out=acc, in0=acc, scalar=2.0, in1=z, op0=ALU.mult, op1=ALU.add))
            link(dve.memset(LTAB[:], 0.0))
            for lo, n, src in ((0, 4, vec("lru_conv_w_2", 0, 64)), (4, 1, vec("lru_conv_b_2", 0, 16)), (5, 4, vec("lru_gate_b_2", 0, 64))):
                dve.tensor_copy(LTAB[:, 0:KT, lo:lo + n], src.rearrange("p (j k) -> p k j", j=n))
            link(dve.tensor_scalar(LTAB[:, 0:KT, 9:11], acc.rearrange("p (d k) -> p k d", d=2), -LRU_C, None, ALU.mult))
            dve.sem_inc(s_ltab, 1)

            dve.wait_ge(s_ge, CHUNK0["ev_b"])
            rope(lambda tt: HE[:, tt, EV_KPE:EV_KPE + ROPE].unsqueeze(1), "mla", ROPE, 1)
            dve.wait_ge(s_ge, CHUNK0["ev_b"] + 4)
            rope(lambda tt: HE[:, tt, EV_QKV:EV_QKV + 2048].rearrange("p (h c) -> p h c", c=DH)[:, :, 0:32], "r32", 32, 16)
            mean_square(2, [(2, MLA_QR), (2, MLA_KVR)])
            dve.wait_ge(s_ct, 1)
            for k in range(6):
                name, kk, dest = ("ev_q_norm_g", k, CQT) if k < 4 else ("ev_kv_norm_g", k - 4, CKVT)
                dve.tensor_scalar(dest[:, kk, :], PS[:, 4 + k // 2, (k % 2) * SEQ:(k % 2 + 1) * SEQ], vec(name, kk), None, ALU.mult)
            dve.tensor_copy(KPT[0:ROPE, :], PS[0:ROPE, 7, 0:SEQ]).then_inc(s_cte, 1)
            rstd(2, 4)
            head_loop(MEM_EV)
            head_loop(MOBA)
            dve.wait_ge(s_ge, CHUNK0["ukv"])
            rope(lambda tt: HE[:, tt, EV_QA:EV_KVA].rearrange("p (h c) -> p h c", c=NOPE + ROPE)[:, :, NOPE:NOPE + ROPE],
                 "mla", ROPE, MLA_HEADS)
            head_loop(MLA)
            residual_add("ev_out")

            mean_square(3, [(2, D)])
            take_features([gvec("od_norm_g")], None, [lambda k: XT[:, k, :]])
            rstd(3, 2)
            dve.wait_ge(s_ge, CHUNK0["od_b"] + 6)
            rope(lambda tt: HO[:, tt, 0:OD_VC].rearrange("p (h c) -> p h c", c=SWA_DH)[:, :, 0:16], "r16", 16, 18)
            rope(lambda tt: HO[:, tt, OD_QD:OD_VD].rearrange("p (h c) -> p h c", c=DH)[:, :, 0:32], "r32", 32, 12)
            dve.wait_ge(s_ge, CHUNK0["od_c"] + 1)
            for h in OD_LOOPS:
                head_loop(h)
            mod_rows(N_MOD - 1)
            mod_columns(N_MOD - 1, 1, 11)
            dve.wait_ge(s_modd, N_MOD + 1)
            for l in range(2):
                for w in range(2):
                    j = 2 * l + w
                    dve.scalar_tensor_tensor(out=MSC[:, 16 * j:16 * j + 16], in0=MODT[:, l, KT:2 * KT, w], scalar=1.0,
                                             in1=vec("norm_g_2", 16 * l, 16), op0=ALU.add, op1=ALU.mult).then_inc(s_msc, 1)
            residual_add("od_out")

            def normalized(dest, rows, r):
                for tt in range(TT):
                    ins = dve.tensor_scalar(dest[:, tt, :], rows[:, tt, :], ST[:, r, tt:tt + 1], None, ALU.mult)
                ins.then_inc(s_xn, 1)

            mean_square(4, [(2, D)])
            rstd(4, 2)
            dve.wait_ge(s_rs, 5)
            dve.wait_ge(s_fg, 16)
            for tt in range(TT):
                ins = dve.scalar_tensor_tensor(out=X[:, tt, :], in0=X[:, tt, :], scalar=ST[:, 4, tt:tt + 1], in1=FG,
                                               op0=ALU.mult, op1=ALU.mult)
            ins.then_inc(s_xf, 1)
            mean_square(5, [(2, D)])
            rstd(5, 2)
            dve.wait_ge(s_rs, 6)
            normalized(CN, CX, 5)
            mean_square(6, [(2, D)])
            rstd(6, 2)
            dve.wait_ge(s_rs, 7)
            normalized(XN, X, 6)
            mod_scale = lambda j: (lambda k: MSC[:, 16 * j + k:16 * j + k + 1])
            mod_shift = lambda l, w: (lambda k: MODT[:, l, k, w:w + 1])
            take_features([mod_scale(1)], mod_shift(0, 1), [lambda k: HT[:, k, 0:SEQ]])
            take_features([mod_scale(0)], mod_shift(0, 0), [lambda k: HT[:, k, SEQ:2 * SEQ]])

            def conv(i, b, n):
                dve.wait_ge(s_wfree, n(0) * 4 + (UNIT0["lru_in"] + 2))
                dve.wait_ge(s_bv, n(1))
                u = PS[:, b, :].rearrange("p (c s) -> p c s", c=2)
                xc = XC[:, b, :, :]
                taps = BV[:, b, :]
                dve.tensor_scalar(xc, u, taps[:, 2:3], taps[:, 4:5], ALU.mult, ALU.add).then_inc(s_cv, 1)
                for step, (j, lo, hi) in enumerate(((0, 2, SEQ), (1, 1, SEQ), (3, 0, SEQ - 1))):
                    dve.wait_ge(s_cv, n(0) * 3 + (step + 1))
                    ins = dve.scalar_tensor_tensor(out=xc[:, :, lo:hi], in0=u[:, :, lo + j - 2:hi + j - 2], scalar=taps[:, j:j + 1],
                                                   in1=xc[:, :, lo:hi], op0=ALU.mult, op1=ALU.add)
                    ins.then_inc(s_cv if step < 2 else s_xc, 1)

            def recur(i, b, n):
                dve.wait_ge(s_ab, n(1))
                dve.tensor_tensor(out=LTMP, in0=LAF, in1=LAF, op=ALU.mult).then_inc(s_w2a, 1)
                dve.wait_ge(s_w2a, n(1))
                dve.scalar_tensor_tensor(out=LWF, in0=LTMP, scalar=1.0, in1=LWF, op0=ALU.add, op1=ALU.mult).then_inc(s_w2, 1)
                dve.tensor_tensor(out=SG, in0=PS[:, 2 + b, :], in1=SG, op=ALU.mult).then_inc(s_gs, 1)
                dve.wait_ge(s_sqr, n(1))
                dve.wait_ge(s_ix, n(1))
                dve.tensor_tensor(out=LW[:], in0=LW[:], in1=RI[:, 1::2, :], op=ALU.mult).then_inc(s_b, 1)
                dve.wait_ge(s_b, n(1))
                scan = lambda h, at, lo, hi, step, h0: dve.tensor_tensor_scan(
                    out=HSC[:, h, lo:hi][:, ::step], data0=LA[:, h, lo:hi][:, ::step], data1=LW[:, h, lo:hi][:, ::step],
                    initial=h0, op0=ALU.mult, op1=ALU.add)
                scan(0, 0, 0, 2 * SEQ, 1, 0.0)
                scan(1, 0, 0, SEQ, -1, 0.0).then_inc(s_sn, 1)
                dve.wait_ge(s_sn, n(0) * 2 + 1)
                scan(1, 0, SEQ, 2 * SEQ, -1, HSC[:, 1, 0:1]).then_inc(s_sn, 1)
                dve.wait_ge(s_sn, n(0) * 2 + 2)
                dve.tensor_tensor(out=HSC[:, 0, :], in0=HSC[:, 0, :], in1=HSC[:, 1, :], op=ALU.add).then_inc(s_hsum, 1)
                dve.wait_ge(s_hsum, n(1))
                y = YL[:, n(0), :] if isinstance(i, int) else YL[:, bass.ds(n(0), 1), :].squeeze(1)
                dve.tensor_tensor(out=y, in0=HSC[:, 0, :], in1=SG, op=ALU.mult).then_inc(s_y, 1)

            at = lambda i, b: (lambda plus: i * 2 + (b + plus))
            for s, n in ((s_xc, 2), (s_gs, 2), (s_y, 2)):
                dve.sem_inc(s, n)
            conv(0, 0, at(0, 0))
            with dve.Fori(0, KT // 2 - 1) as i:
                conv(i, 1, at(i, 1))
                recur(i, 0, at(i, 0))
                conv(i, 0, at(i, 2))
                recur(i, 1, at(i, 1))
            last = KT // 2 - 1
            conv(last, 1, at(last, 1))
            recur(last, 0, at(last, 0))
            recur(last, 1, at(last, 1))

            def gate_diagonals(layer, w, base):
                for j in range(4):
                    if base + j >= 2:
                        dve.wait_ge(s_gb, base + j - 1)
                    for k in range(4):
                        ins = dve.tensor_scalar(DIAG(base + j)[:, k, :], ident, MODT[:, layer, 2 * KT + 4 * j + k, w:w + 1], None, ALU.mult)
                    ins.then_inc(s_dg, 1)

            dve.memset(ONES, 1.0)
            gate_diagonals(0, 0, 0)
            gate_diagonals(0, 1, 4)

            def gated_residual(stage, tiles, gates, bank_step, scratch):
                with dve.Fori(0, 2) as i:
                    for c in range(2):
                        v = lambda plus: i * 2 + (RES0[stage] + c + plus)
                        cols = bass.ds(i * 1024 + c * CHUNK, CHUNK)
                        dve.wait_ge(s_wfree, i * 16 + multiplied(stage, c))
                        dve.wait_ge(s_gbe, 8 if stage == "lru_out" else 12)
                        dve.wait_ge(s_re, v(0))
                        for m in range(len(tiles)):
                            ins = dve.tensor_tensor(out=scratch[:, m * CHUNK:(m + 1) * CHUNK], in0=PS[:, bank_step * c + m, :],
                                                    in1=gates[m][:, cols], op=ALU.mult)
                        ins.then_inc(s_rh, 1)
                        dve.wait_ge(s_rh, v(1) - RES0["lru_out"])
                        for m in range(len(tiles)):
                            x = tiles[m][:, cols]
                            ins = dve.tensor_tensor(out=x, in0=scratch[:, m * CHUNK:(m + 1) * CHUNK], in1=x, op=ALU.add)
                        ins.then_inc(s_re, 1)
            gated_residual("lru_out", [CX[:, 0, :], CX[:, 1, :], X[:, 0, :], X[:, 1, :]], [G_CTX, G_CTX, G_LAT, G_LAT], 4,
                           HB[:, 8192:10240])

            mean_square(7, [(2, D)])
            rstd(7, 2)
            dve.wait_ge(s_rs, 8)
            normalized(CN, CX, 7)
            mean_square(8, [(2, D)])
            rstd(8, 2)
            dve.wait_ge(s_rs, 9)
            normalized(XN, X, 8)
            take_features([mod_scale(3)], mod_shift(1, 1), [lambda k: HT[:, k, 0:SEQ]])
            take_features([mod_scale(2)], mod_shift(1, 0), [lambda k: HT[:, k, SEQ:2 * SEQ]])
            axial = const("axial").rearrange("p (t z a y f) -> p t z a y f", t=TT, z=2, a=2, y=2)
            PER = 12 + 4 * TT * 3 + 5
            with dve.Fori(0, GROUPS) as i:
                done = [0]

                def link(ins):
                    done[0] += 1
                    ins.then_inc(s_ds, 1)
                    dve.wait_ge(s_ds, i * PER + done[0])
                dve.wait_ge(s_dqe, i * 4 + 3)
                flat = RQK[:].rearrange("p t c -> p (t c)")
                by64 = flat.rearrange("p (g c) -> p g c", c=ATT_DH)
                link(dve.tensor_tensor(out=DSQ, in0=flat, in1=flat, op=ALU.mult))
                link(dve.tensor_reduce(DS48, DSQ.rearrange("p (g c) -> p g c", c=ATT_DH), AX, ALU.add))
                dve.tensor_scalar(DS48, DS48, 1.0 / ATT_DH, EPS, ALU.mult, ALU.add).then_inc(s_dm, 1)
                dve.wait_ge(s_dp0, i + 1)
                link(dve.reciprocal(DS48, DS48))
                link(dve.tensor_tensor(out=by64, in0=by64, in1=DS48.unsqueeze(2).to_broadcast([P, 48, ATT_DH]), op=ALU.mult))
                dve.tensor_tensor(out=by64[:, 0:32, :], in0=by64[:, 0:32, :], in1=KG.unsqueeze(1).to_broadcast([P, 32, ATT_DH]), op=ALU.mult)
                ins = dve.tensor_tensor(out=by64[:, 32:48, :], in0=by64[:, 32:48, :], in1=QG.unsqueeze(1).to_broadcast([P, 16, ATT_DH]), op=ALU.mult)
                for tile in range(2, 6):
                    x = RQK[:, tile, :]
                    cos = axial[:, tile % 2, 0].rearrange("p a y f -> p (a y f)").unsqueeze(1).to_broadcast([P, 8, ATT_DH])
                    parts = lambda v: v.rearrange("p (h a y f) -> p h a y f", h=8, a=2, y=2)
                    if tile == 2:
                        link(ins)
                    dve.tensor_tensor(out=DT1.rearrange("p (h c) -> p h c", h=8), in0=x.rearrange("p (h c) -> p h c", h=8), in1=cos, op=ALU.mult)
                    for y in range(2):
                        sin = axial[:, tile % 2, 1, :, y, :].unsqueeze(1).to_broadcast([P, 8, 2, 16])
                        ins = dve.tensor_tensor(out=parts(DT2)[:, :, :, y, :], in0=parts(x)[:, :, :, 1 - y, :], in1=sin, op=ALU.mult)
                    link(ins)
                    ins = dve.tensor_tensor(out=x, in0=DT1, in1=DT2, op=ALU.add)
                    if tile < 5:
                        link(ins)
                ins.then_inc(s_qn, 1)
                for j in range(4):
                    for tt in range(TT):
                        dve.wait_ge(s_e3, i * 8 + (2 * j + tt + 1))
                        dve.tensor_reduce(NM[:, tt, :], PS[:, 2 * tt:2 * tt + 2, :], AX, ALU.max, negate=True).then_inc(s_e4, 1)
                    for tt in range(TT):
                        dve.wait_ge(s_e5, i * 8 + (2 * j + tt + 1))
                        link(dve.reciprocal(RL[:, tt, :], LS[:, tt, :]))
                        link(dve.tensor_tensor(out=RL[:, tt, 1:2], in0=RL[:, tt, 1:2], in1=NLAM, op=ALU.mult))
                        link(dve.tensor_scalar(DE[:, tt, 1, :], DE[:, tt, 1, :], RL[:, tt, 1:2], None, ALU.mult))
                        dve.scalar_tensor_tensor(out=DE[:, tt, 0, :], in0=DE[:, tt, 0, :], scalar=RL[:, tt, 0:1], in1=DE[:, tt, 1, :],
                                                 op0=ALU.mult, op1=ALU.add).then_inc(s_e8, 1)
                    for tt in range(TT):
                        dve.wait_ge(s_e11, i * 8 + (2 * j + tt + 1))
                        ins = dve.tensor_copy(OS[:, tt, j * P:(j + 1) * P], PS[:, 7, 0:P])
                        ins.then_inc(s_oe, 1)
                dve.wait_ge(s_oe, i * 8 + 8)
                oflat = OS[:].rearrange("p t c -> p (t c)")
                oh = oflat.rearrange("p (g c) -> p g c", c=P)
                link(dve.tensor_tensor(out=DSQ[:, 0:1024], in0=oflat, in1=oflat, op=ALU.mult))
                link(dve.tensor_reduce(DS8, DSQ[:, 0:1024].rearrange("p (g c) -> p g c", c=P), AX, ALU.add))
                dve.tensor_scalar(DS8, DS8, 1.0 / P, EPS, ALU.mult, ALU.add).then_inc(s_om, 1)
                dve.wait_ge(s_or, i + 1)
                link(dve.reciprocal(DS8, DS8))
                link(dve.tensor_tensor(out=oh, in0=oh, in1=DS8.unsqueeze(2).to_broadcast([P, 8, P]), op=ALU.mult))
                link(dve.tensor_tensor(out=oh, in0=oh, in1=SUBG.unsqueeze(1).to_broadcast([P, 8, P]), op=ALU.mult))
                dve.tensor_tensor(out=oflat, in0=oflat, in1=RG[:].rearrange("p t c -> p (t c)"), op=ALU.mult).then_inc(s_oy, 1)
                assert done[0] == PER, (done[0], PER)
            dve.wait_ge(s_dye, GROUPS + 1)
            dve.memset(ONES, 1.0)
            gate_diagonals(1, 0, 8)
            gated_residual("att_out", [X[:, 0, :], X[:, 1, :]], [G_ATT, G_ATT], 2, HB[:, 11264:12288])

        @block.gpsimd
        def _(pool):
            def stage_heads(h):
                H = HE if h in EV_LOOPS else HO
                wq = NOPE + ROPE if h.kind == "mla" else P
                wk = NOPE + MLA_DV if h.kind == "mla" else P
                with pool.Fori(0, h.turns) as i:
                    pair = h.kind == "swa"
                    for a in range(1 if pair else 2):
                        pool.wait_ge(s_t1, i * 2 + (h.n0 + (1 if pair else a) + 1))
                        q = H[:, :, bass.ds(i * (P if pair else 2 * wq) + (h.q + a * wq), wq)]
                        pool.tensor_copy(QS[:, a, :, 0:wq], q)
                        if pair:
                            for z in range(2):
                                ins = pool.tensor_copy(KS[:, a, :, 64 * z:64 * z + 64], H[:, :, h.k:h.k + SWA_DH])
                        elif h.mem is not None:
                            ins = pool.tensor_copy(KS[:, a, :, :], MKV[:, h.mem, :, bass.ds(i * 256 + (h.k + a * P), P)])
                        else:
                            ins = pool.tensor_copy(KS[:, a, :, :], H[:, :, bass.ds(i * (2 * wk) + (h.k + a * wk), P)])
                        ins.then_inc(s_stg, 2 if pair else 1)

            pool.wait_ge(s_ge, CHUNK0["uq"])
            stage_heads(MEM_EV)
            pool.wait_ge(s_rope, 2)
            stage_heads(MOBA)
            pool.wait_ge(s_ge, CHUNK0["od_b"])
            pool.wait_ge(s_rope, 3)
            stage_heads(MLA)
            pool.wait_ge(s_ge, CHUNK0["od_c"] + 1)
            pool.wait_ge(s_rope, 5)
            for h in OD_LOOPS:
                stage_heads(h)

            def block_vectors(b, n):
                pool.tensor_copy(BV[:, b, :], LTAB[:, n, :]).then_inc(s_bv, 1)
            pool.wait_ge(s_ltab, 1)
            for b in range(2):
                block_vectors(b, b)
            with pool.Fori(0, KT // 2) as i:
                for b in range(2):
                    n = lambda plus: i * 2 + (b + plus)
                    pool.wait_ge(s_sg, n(2))
                    for d in range(2):
                        ins = pool.tensor_tensor(out=RI[:, 2 * d + 1, :], in0=RI[:, 2 * d + 1, :],
                                                 in1=XC[:, b, :, :].rearrange("p c s -> p (c s)"), op=ALU.mult)
                    ins.then_inc(s_ix, 1)
                    pool.wait_ge(s_y, n(3))
                    pool.tensor_copy(BV[:, b, :], LTAB[:, bass.ds(n(2), 1), :].squeeze(1)).then_inc(s_bv, 1)


_INS = ("x", "mem", "ev_norm_g", "ev_w_in", "ev_q_norm_g", "ev_w_uq", "ev_kv_norm_g", "ev_w_ukv", "ev_mem_norm_g",
        "ev_w_mem_kv", "ev_w_out", "od_norm_g", "od_w_in", "od_sinks", "od_mem_norm_g", "od_w_mem_kv", "od_w_out",
        "final_norm_g", "c_2", "ctx_2", "c_ctx_2", "mod_w_2", "mod_b_2", "norm_g_2", "lru_w_in_2", "lru_conv_w_2",
        "lru_conv_b_2", "lru_gate_w_2", "lru_gate_b_2", "lru_lambda_2", "lru_w_out_2", "att_w_in_2", "att_q_norm_2",
        "att_k_norm_2", "att_lambda_2", "att_subln_2", "att_w_out_2")


def kernel(**inputs):
    import concourse.bacc as bacc
    from concourse.bass_utils import run_bass_kernel_spmd

    nc = bacc.Bacc("TRN2", target_bir_lowering=False, num_devices=1)
    arrays, args = {}, {}
    for name in _INS:
        a = np.ascontiguousarray(inputs[name])
        arrays[f"in_{name}"] = a
        args[name] = nc.dram_tensor(f"in_{name}", a.shape, mybir.dt.from_np(a.dtype), kind="ExternalInput").ap()
    arrays["shape_constants"] = shape_constants()
    consts = nc.dram_tensor("shape_constants", (P, NCONST), F32, kind="ExternalInput").ap()
    out = nc.dram_tensor("out", (1, SEQ, D), F32, kind="ExternalOutput").ap()
    build(nc, args, consts, out)
    return run_bass_kernel_spmd(nc, [arrays], core_ids=[0]).results[0]["out"]
```

```python
import math
from contextlib import ExitStack

import numpy as np

import concourse.bass as bass
from concourse import mybir

F32 = mybir.dt.float32
F32R = mybir.dt.float32r
ACT = mybir.ActivationFunctionType
ALU = mybir.AluOpType
AX = mybir.AxisListType.X

P = 128
SEQ = 256
D = 2048
KT = D // P
TT = SEQ // P
EPS = 1e-6
NEG = -1e30

MLA_HEADS, MLA_QR, MLA_KVR, NOPE, ROPE, MLA_DV = 8, 512, 256, 128, 64, 128
MOBA_HEADS, DH = 8, 128
MEM_HEADS = 4
MEMW = MEM_HEADS * DH
EV_VW = MLA_HEADS * MLA_DV + MOBA_HEADS * DH + MEMW
EV_CKV = MLA_QR
EV_KPE = EV_CKV + MLA_KVR
EV_LAT = EV_KPE + ROPE
EV_QKV = 0
EV_QM = EV_QKV + 3 * MOBA_HEADS * DH
EV_GATE = EV_QM + MEMW
EV_W = EV_GATE + EV_VW
SWA_HEADS, SWA_KV, SWA_DH, SWA_WINDOW = 16, 2, 64, 128
DIL_HEADS = 6
DIL_PATTERNS = ((128, 1), (512, 4), (2048, 16))
OD_KC = SWA_HEADS * SWA_DH
OD_VC = OD_KC + SWA_KV * SWA_DH
OD_QD = OD_VC + SWA_KV * SWA_DH
OD_KD = OD_QD + DIL_HEADS * DH
OD_VD = OD_KD + DIL_HEADS * DH
OD_QM = OD_VD + DIL_HEADS * DH
OD_GATE = OD_QM + MEMW
OD_VW = SWA_HEADS * SWA_DH + DIL_HEADS * DH + MEMW
OD_IN = OD_GATE + OD_VW
EV_QA = EV_QKV
EV_KVA = EV_QA + MLA_HEADS * (NOPE + ROPE)
ATT_HEADS, ATT_DH = 16, 64
GROUPS = 4
LRU_C = 8.0
LAM_INIT = 0.8 - 0.6 * math.exp(-0.3 * 1)

CHUNK = 512
SLOTS = 4
UNIT = 2 * CHUNK

CONSTS = {}


def _lay_consts():
    at = 0
    for name, width in (("ident", P), ("axial", TT * 2 * 64), ("mla", TT * 4 * 32), ("r32", TT * 4 * 16),
                        ("r16", TT * 4 * 8), ("causal", 2 * SEQ), ("swa", 2 * SEQ), ("dil", 2 * SEQ)):
        CONSTS[name] = (at, width)
        at += width
    return at


NCONST = _lay_consts()
NCONST_ALL = CONSTS["mla"][0]


def shape_constants():
    out = np.zeros((P, NCONST), np.float32)

    def put(name, a):
        at, width = CONSTS[name]
        out[:, at:at + width] = a.reshape(P, width)

    put("ident", np.eye(P, dtype=np.float32))
    pos = np.arange(SEQ, dtype=np.float32)
    for name, rot in (("mla", ROPE), ("r32", DH // 4), ("r16", SWA_DH // 4)):
        inv = (1.0 / (np.float32(500000.0) ** (np.arange(0, rot, 2, dtype=np.float32) / np.float32(rot)))).astype(np.float32)
        ang = (pos[:, None] * inv[None]).astype(np.float32)
        c, s = np.cos(ang), np.sin(ang)
        table = np.stack([np.concatenate([c, c], 1), np.concatenate([-s, s], 1)], 1)
        put(name, table.reshape(TT, P, 2 * rot).transpose(1, 0, 2))
    nf = ATT_DH // 4
    inv = (np.float32(10000.0) ** (-np.arange(nf, dtype=np.float32) / np.float32(nf))).astype(np.float32)
    t = np.arange(SEQ)
    ang = np.stack([(t // 64).astype(np.float32)[:, None] * inv, (t % 64).astype(np.float32)[:, None] * inv], 1)
    c, s = np.cos(ang).astype(np.float32), np.sin(ang).astype(np.float32)
    table = np.stack([np.stack([c, c], 2).reshape(SEQ, 64), np.stack([-s, s], 2).reshape(SEQ, 64)], 1)
    put("axial", table.reshape(TT, P, 128).transpose(1, 0, 2))
    q, k = np.arange(SEQ)[:, None], np.arange(SEQ)[None]
    dist = q - k

    def mask(times):
        bias = np.where(times > 0, np.log(np.maximum(times, 1).astype(np.float64)), NEG).astype(np.float32)
        return bias.reshape(TT, P, SEQ).transpose(1, 0, 2)

    put("causal", mask((dist >= 0).astype(int)))
    put("swa", mask(((dist >= 0) & (dist <= SWA_WINDOW - 1)).astype(int)))
    put("dil", mask(sum(((dist >= 0) & (dist % dil == 0) & (dist // dil <= window // dil)).astype(int)
                        for window, dil in DIL_PATTERNS)))
    return out


VECTORS = (
    (("ev_norm_g", 0, 16), ("ev_mem_norm_g", 0, 16), ("od_norm_g", 0, 16), ("od_mem_norm_g", 0, 16),
     ("c_2", 0, 16), ("c_ctx_2", None, 16), ("ev_q_norm_g", 0, 4), ("ev_kv_norm_g", 0, 2)),
    (("norm_g_2", None, 32), ("lru_lambda_2", 0, 32), ("lru_conv_b_2", 0, 16)),
    (("lru_conv_w_2", 0, 64), ("lru_gate_b_2", 0, 64)),
    (("mod_b_2", None, 96),),
)
VEC_ROWS = [sum(n for _, _, n in tile) for tile in VECTORS]
VEC_COL = [sum(VEC_ROWS[:t]) for t in range(len(VECTORS) + 1)]
VEC_AT = {}
for _t, _tile in enumerate(VECTORS):
    _row = 0
    for _name, _, _n in _tile:
        VEC_AT[_name] = VEC_COL[_t] + _row
        _row += _n

STAGES = (("mkv0", 16), ("mkv1", 16), ("ev_a", 16), ("ev_b", 96), ("mod_mem_ev", 16), ("mod_moba", 32), ("uq", 6), ("ukv", 4),
          ("mod_mla", 32), ("ev_out", 40), ("od_b", 96), ("od_c", 8), ("mod_swa0", 32), ("mod_swa1", 32), ("mod_dil", 24),
          ("mod_mem_od", 16), ("mod_last", 8), ("od_out", 36), ("lru_in", 64), ("lru_out", 32), ("att_in", 128), ("att_out", 32))
UNIT0 = {}
LO_BY = []


def by_gpsimd(stage, u):
    return stage == "lru_in" or (stage.startswith("mod_") and stage != "mod_last" and u % 8 in (4, 5, 6))


_made = [0, 0]
for _name, _n in STAGES:
    UNIT0[_name] = len(LO_BY)
    for _u in range(_n):
        _pool = by_gpsimd(_name, _u)
        LO_BY.append((_pool, _made[_pool]))
        _made[_pool] += 1
CHUNK_UNITS = {name: 8 for name, _ in STAGES} | {"uq": 2, "ukv": 1, "ev_out": 10, "od_out": 9}


def multiplied(stage, c):
    return UNIT0[stage] + (c + 1) * CHUNK_UNITS[stage]


CHUNK0 = {"mkv0": 0, "mkv1": 2, "ev_a": 4, "ev_b": 6, "uq": 18, "ukv": 21, "od_b": 25, "od_c": 37}
RES0 = {"ev_out": 0, "od_out": 4, "lru_out": 8, "att_out": 12}


class Heads:

    def __init__(self, name, n0, turns, kind, q, k, v, gate, y0, mask, scale, mod_layer, mod_chunk0, mod0, mem=None, sink=None):
        self.name, self.n0, self.turns, self.kind = name, n0, turns, kind
        self.q, self.k, self.v, self.gate, self.y0 = q, k, v, gate, y0
        self.mask, self.scale = mask, scale
        self.mod_layer, self.mod_chunk0, self.mod0 = mod_layer, mod_chunk0, mod0
        self.mem, self.sink = mem, sink


EV_Y_B = MLA_HEADS
EV_Y_M = MLA_HEADS + MOBA_HEADS
OD_Y_D = SWA_HEADS * SWA_DH // P
OD_Y_M = OD_Y_D + DIL_HEADS
SC128, SC64 = DH ** -0.5, SWA_DH ** -0.5
MEM_EV = Heads("mem_ev", 0, 2, "plain", EV_QM, 0, MEMW, EV_GATE + EV_Y_M * P, EV_Y_M, None, SC128, 0, 0, 0, mem=0)
MOBA = Heads("moba", 4, 4, "plain", EV_QKV, EV_QKV + 1024, EV_QKV + 2048, EV_GATE + EV_Y_B * P, EV_Y_B, "causal", SC128, 0, 2, 2)
MLA = Heads("mla", 12, 4, "mla", EV_QA, EV_KVA, EV_KVA + NOPE, EV_GATE, 0, "causal", (NOPE + ROPE) ** -0.5, 0, 6, 6)
SWA = [Heads(f"swa{j}", 20 + 8 * j, 4, "swa", 512 * j, OD_KC + 64 * j, OD_VC + 64 * j, OD_GATE + 512 * j, 4 * j, "swa", SC64,
             1, 4 * j, 10 + 4 * j, sink=8 * j) for j in range(2)]
DIL = Heads("dil", 36, 3, "plain", OD_QD, OD_KD, OD_VD, OD_GATE + OD_Y_D * P, OD_Y_D, "dil", SC128, 1, 8, 18)
MEM_OD = Heads("mem_od", 42, 2, "plain", OD_QM, 0, MEMW, OD_GATE + OD_Y_M * P, OD_Y_M, None, SC128, 0, 10, 21, mem=1)
EV_LOOPS = (MEM_EV, MOBA, MLA)
OD_LOOPS = (*SWA, DIL, MEM_OD)
N_HEADS = 46
N_MOD = 24


def build(nc, t, consts, out):
    ctx = ExitStack()
    with ctx:
        def sb(name, shape, dtype=F32, owner=ctx):
            return owner.enter_context(nc.sbuf_tensor(name, shape, dtype))

        def sem(name):
            return ctx.enter_context(nc.semaphore(name))

        PS = ctx.enter_context(nc.psum_tensor("ps", [P, 8, CHUNK], F32))
        X = sb("x_res", [P, TT, D])
        CST = sb("consts", [P, NCONST_ALL])
        GT = sb("vectors_t", [P, VEC_COL[-1]])
        CS = sb("cond_t", [P, 4 * KT + P], F32R)
        MODT = sb("mod_t", [P, 2, 48, 2])
        BC = sb("bcast", [P, 272])
        ST = sb("stats", [P, 9, 4])
        HS = sb("head_stats", [P, 2, 16])
        SC = sb("scalars", [P, 512])
        RA = sb("ring", [P, SLOTS, UNIT])
        WH = sb("ring_hi", [P, SLOTS, UNIT], F32R)
        WL = sb("ring_lo", [P, SLOTS, UNIT], F32R)
        with ExitStack() as first:
            MKVB = sb("mem_kv", [P, 2 * TT * 2 * MEMW], owner=first)
            with ExitStack() as start:
                MEMB = sb("mem_rows", [P, TT * D], owner=start)
                M1H = sb("mem_hi", [P, KT * SEQ], F32R, owner=start)
                M1L = sb("mem_lo", [P, KT * SEQ], F32R, owner=start)
                GRB = sb("vector_rows", [P, 4 * P], owner=start)
            HB = sb("proj", [P, 12800], owner=first)
            ATH = sb("act_hi", [P, 20 * SEQ], F32R, owner=first)
            ATL = sb("act_lo", [P, 20 * SEQ], F32R, owner=first)
            AR = sb("arena", [P, 5632], owner=first)
            CSTA = sb("consts_first", [P, NCONST - NCONST_ALL], owner=first)
        BUF = sb("second_block", [P, 17536])
        FTH = sb("features_hi", [P, KT, 2 * SEQ], F32R)
        FTL = sb("features_lo", [P, KT, 2 * SEQ], F32R)

        def const(name):
            at, width = CONSTS[name]
            if at < NCONST_ALL:
                return CST[:, at:at + width]
            return CSTA[:, at - NCONST_ALL:at - NCONST_ALL + width]

        def vec(name, k=0, n=1):
            return GT[:, VEC_AT[name] + k:VEC_AT[name] + k + n]

        def at(v, i=None, per=0):
            return v if i is None else i * per + v

        def carve(buf, first, parts):
            views = []
            for n in parts:
                views.append(buf[:, first:first + n])
                first += n
            return views

        ident = const("ident")
        SUBG, QG, KG, SINK = BC[:, 0:128], BC[:, 128:192], BC[:, 192:256], BC[:, 256:272]

        MKV = MKVB[:].rearrange("p (l t c) -> p l t c", l=2, t=TT)
        HE = HB[:, 0:TT * EV_W].rearrange("p (t c) -> p t c", c=EV_W)
        HO = HB[:, 0:TT * OD_IN].rearrange("p (t c) -> p t c", c=OD_IN)
        MEMX = MEMB[:].rearrange("p (t d) -> p t d", t=TT)
        GR = GRB[:].rearrange("p (v c) -> p v c", c=P)
        HQ = AR[:, 0:TT * EV_LAT].rearrange("p (t c) -> p t c", c=EV_LAT)
        LV, LVP = AR[:, 2048:2304], AR[:, 2304:2432]
        COND = AR[:, 2432:2464].rearrange("p (k v) -> p k v", v=2)
        CSV = CS[:, 0:4 * KT].rearrange("p (k v) -> p k v", v=4)
        JUNK_A = AR[:, 3072:3072 + D]
        TMP_X = AR[:, 0:2048].rearrange("p (j c) -> p j c", j=4)
        TMP_LAT = AR[:, 3072:5120].rearrange("p (j c) -> p j c", j=4)

        a_qs, a_ks, a_qkt, a_qrt, KPT, a_s, a_pt, a_ys = carve(AR, 0, (768, 512, 1024, 512, 256, 1024, 1024, 512))
        QS = a_qs.rearrange("p (a t c) -> p a t c", a=2, t=TT)
        KS = a_ks.rearrange("p (a t c) -> p a t c", a=2, t=TT)
        QKT = a_qkt.rearrange("p (a c) -> p a c", a=2)
        QRT = a_qrt.rearrange("p (a c) -> p a c", a=2)
        S = a_s.rearrange("p (a t c) -> p a t c", a=2, t=TT)
        PT = a_pt.rearrange("p (a c) -> p a c", a=2)
        YS = a_ys.rearrange("p (a t c) -> p a t c", a=2, t=TT)
        ROT_A, ROT_B = a_s[:, 0:512], a_s[:, 512:1024]
        MODS_EV, MODS_OD = HB[:, TT * EV_W:TT * EV_W + CHUNK], a_qrt
        NM, LS, RL, ES, SN = (HS[:, :, j:j + 2] for j in (0, 2, 4, 6, 8))

        XN, CN, CX = (BUF[:, j * TT * D:(j + 1) * TT * D].rearrange("p (t d) -> p t d", t=TT) for j in range(3))
        FG = BUF[:, 12288:12288 + D]
        TMP_B = BUF[:, 14336:16384].rearrange("p (j c) -> p j c", j=4)
        YL = BUF[:, 0:KT * 2 * SEQ].rearrange("p (k s) -> p k s", s=2 * SEQ)
        l_xc, l_gw, l_ri, SG, l_hs, LAF, LWF = carve(BUF, 8192, (1024, 1024, 2048, 512, 1024, 1024, 1024))
        XC = l_xc.rearrange("p (b c s) -> p b c s", b=2, c=2)
        GW = l_gw.rearrange("p (b j d) -> p b j d", b=2, j=4)
        RI = l_ri.rearrange("p (j s) -> p j s", j=4)
        HSC = l_hs.rearrange("p (d s) -> p d s", d=2)
        LTMP = l_hs
        LA = LAF.rearrange("p (d s) -> p d s", d=2)
        LW = LWF.rearrange("p (d s) -> p d s", d=2)
        LTAB = SC[:, 164:164 + 18 * 12].rearrange("p (k j) -> p k j", j=12)
        BV = SC[:, 380:404].rearrange("p (b j) -> p b j", b=2)
        NSINK = SC[:, 404:436].rearrange("p (h t) -> p h t", t=TT)
        NLAM = SC[:, 436:437]
        MSC = SC[:, 440:504]
        G_LAT, G_CTX, G_ATT = BUF[:, 12288:14336], BUF[:, 14336:16384], BUF[:, 0:D]
        ONES = BUF[:, 17408:17536]

        def DIAG(j):
            first = (16384 if j < 8 else D) + (j % 2) * 512
            return BUF[:, first:first + 512].rearrange("p (k d) -> p k d", k=4)

        d_qk, d_v, d_g, d_y, d_qkt, d_e, d_pt, d_os = carve(BUF, 0, (3072, 2048, 1024, 4096, 3072, 2048, 1024, 1024))
        RQK = d_qk.rearrange("p (t c) -> p t c", t=6)
        RV = d_v.rearrange("p (t c) -> p t c", t=4)
        RG = d_g.rearrange("p (t c) -> p t c", t=2)
        DYT = d_y.rearrange("p (k s) -> p k s", s=SEQ)
        DQK = d_qkt.rearrange("p (h c) -> p h c", h=4)
        DE = d_e.rearrange("p (a c s) -> p a c s", a=2, c=2)
        DPT = d_pt.rearrange("p (a c) -> p a c", a=2)
        OS = d_os.rearrange("p (t c) -> p t c", t=TT)
        DSQ = BUF[:, 13312:16384]
        DT1, DT2 = d_qkt[:, 0:512], d_qkt[:, 512:1024]
        DS48, DS8 = SC[:, 0:48], SC[:, 48:56]
        DYH, DYL = FTH[:, :, 0:SEQ], FTL[:, :, 0:SEQ]

        s_const, s_consta, s_rows, s_mem, s_x, s_bc, s_ctx, s_fg, s_cx2, s_out = map(sem, (
            "const_loaded", "first_const_loaded", "vector_rows_loaded", "mem_loaded", "x_loaded", "bcast_loaded",
            "ctx_loaded", "final_g_loaded", "ctx_loaded_again", "out_stored"))
        s_w = [sem(f"weights_landed{j}") for j in range(SLOTS)]
        s_hi, s_lo, s_lop, s_wused = map(sem, ("weights_hi", "weights_lo_by_vector", "weights_lo_by_gpsimd", "weight_units_used"))
        s_vt, s_vec, s_cond, s_cs = map(sem, ("vectors_transposed", "vectors_ready", "cond_hi", "cond_ready"))
        s_sq, s_ms, s_rt, s_rs = map(sem, ("squares_summed", "mean_square", "root_taken", "rstd_ready"))
        s_xn, s_xt, s_tmp, s_xh, s_xl = map(sem, ("rows_normalized", "rows_transposed", "features_scaled", "features_hi", "features_lo"))
        s_ge, s_rh, s_re = map(sem, ("chunk_evicted", "residual_gated", "residual_added"))
        s_rope, s_kpe, s_kpt = map(sem, ("rope_done", "kpe_transposed", "kpe_ready"))
        s_stg, s_t1, s_qk, s_sc, s_sm, s_mx, s_ex, s_pt, s_pe, s_o, s_rl, s_ys, s_yt, s_yh, s_ye = map(sem, (
            "head_staged", "head_qk_transposed", "head_qk_ready", "head_scores", "head_masked", "head_max",
            "head_exp", "head_p_transposed", "head_p_ready", "head_out", "head_recip", "head_y", "head_y_transposed",
            "head_y_hi", "head_y_lo"))
        s_sk, s_sk2, s_l2 = map(sem, ("sink_shifted", "sink_max", "sink_added"))
        s_mods, s_modt, s_modb, s_modd, s_msc = map(sem, ("mod_rows_ready", "mod_transposed", "mod_biased", "mod_ready", "mod_scale_ready"))
        s_dve = sem("vector_step")
        s_lam, s_exl, s_ltab, s_xf = map(sem, ("lru_decay_ready", "lru_exp_ready", "lru_table_ready", "x_final"))
        SQUARED = np.cumsum([2, 2, 4, 2, 2, 2, 2, 2, 2]).tolist()
        s_gw = [sem(f"gate_weights_landed{b}") for b in range(2)]
        s_cv, s_xc, s_gt, s_sg, s_gs, s_ab, s_w2a, s_w2, s_sqr, s_ix, s_b, s_sn, s_hsum, s_y, s_bv = map(sem, (
            "lru_conv_tap", "lru_conv", "lru_gates", "lru_sigmoids", "lru_silu", "lru_a", "lru_a2", "lru_1ma2", "lru_sqrt",
            "lru_ix", "lru_b", "lru_scan", "lru_sum", "lru_y", "lru_block_vectors"))
        s_yhi, s_ylo = map(sem, ("y_hi", "y_lo"))
        s_dg, s_gb, s_gbe = map(sem, ("gate_diag", "gate_bcast", "gate_bcast_ready"))
        s_dqe, s_dstep, s_tstep, s_pstep, s_dm, s_dp0, s_qn = map(sem, (
            "diff_chunk_evicted", "diff_head_step", "diff_tail_step", "diff_prep_step", "diff_qk_ms", "diff_qk_root", "diff_qk_normal"))
        s_e1, s_e2, s_e3, s_e4, s_e5, s_e8, s_e9, s_e10, s_e11, s_oe = map(sem, (
            "diff_qk_transposed", "diff_qk_ready", "diff_scores", "diff_max", "diff_exp", "diff_weights",
            "diff_w_transposed", "diff_w_ready", "diff_o", "diff_o_ready"))
        s_om, s_or, s_oy, s_dyt, s_dye = map(sem, ("diff_o_ms", "diff_o_root", "diff_y", "diff_y_transposed", "diff_y_ready"))

        N_CONST_BC = 5
        S_ROWS = 16 * sum(len(tile) for tile in VECTORS)
        OUT_AHEAD = 6
        block = ctx.enter_context(nc.Block())

        def landed(U, i=None, per=0):
            return at(16 * (U // SLOTS + 1), i, 16 * per // SLOTS)

        def lo_made(U, i=None, per=0, turns=0):
            pool, before = LO_BY[U]
            stage0 = max(u0 for u0 in UNIT0.values() if u0 <= U)
            a_turn = sum(LO_BY[u][0] == pool for u in range(stage0, stage0 + per))
            return s_lop if pool else s_lo, at(before + 1 - turns * a_turn, i, a_turn)

        @block.sync
        def _(sp):
            sp.dma_start(CST[:], consts[:, 0:NCONST_ALL]).then_inc(s_const, 16)
            for v, tile in enumerate(VECTORS):
                row = 0
                for name, layer, n in tile:
                    src = t[name] if layer is None else t[name][layer]
                    while len(src.shape) > 1:
                        src = src.rearrange("a b -> (a b)") if len(src.shape) == 2 else src.rearrange("a b c -> (a b) c") \
                            if len(src.shape) == 3 else src.rearrange("a b c d -> (a b) c d")
                    sp.dma_start(GR[row:row + n, v, :], src.rearrange("(r c) -> r c", c=P)).then_inc(s_rows, 16)
                    row += n
            sp.dma_start(MEMX, t["mem"].rearrange("b (t p) d -> p (b t) d", p=P)).then_inc(s_mem, 16)
            sp.dma_start(X[:], t["x"].rearrange("b (t p) d -> p (b t) d", p=P)).then_inc(s_x, 16)

            def unit(U, w, k0, nk, col, n, i=None, per=0):
                dst = RA[:, U % SLOTS, 0:nk * n].rearrange("p (k n) -> p k n", k=nk)
                cols = col if i is None else sp.snap(col)
                if U + per >= SLOTS:
                    sp.wait_ge(*lo_made(U + per - SLOTS, i, per, 1 if per else 0))
                src = w.rearrange("(k p) n -> p k n", p=P)[:, k0:k0 + nk, bass.ds(cols, n)]
                sp.dma_start(dst, src).then_inc(s_w[U % SLOTS], 16)

            def chunks(stage, w, col0, count, n=CHUNK, kt=KT):
                per = -(-kt // 2)
                for c in range(count):
                    for u in range(per):
                        unit(UNIT0[stage] + c * per + u, w, u * 2, min(2, kt - u * 2), col0 + c * CHUNK, n)

            def chunk_loop(stage, w, col0, count):
                chunks(stage, w, col0, 1)
                with sp.Fori(1, count) as i:
                    for u in range(KT // 2):
                        unit(UNIT0[stage] + u, w, u * 2, 2, i * CHUNK + col0, CHUNK, i, KT // 2)

            def mod_loop(h):
                chunk_loop("mod_" + h.name, t["mod_w_2"][h.mod_layer], h.mod_chunk0 * CHUNK, h.turns)

            sp.dma_start(CSTA[:], consts[:, NCONST_ALL:NCONST]).then_inc(s_consta, 16)
            chunks("mkv0", t["ev_w_mem_kv"][0], 0, 2)
            chunks("mkv1", t["od_w_mem_kv"][0], 0, 2)
            chunks("ev_a", t["ev_w_in"][0], 0, 1)
            for u in range(8):
                unit(UNIT0["ev_a"] + 8 + u, t["ev_w_in"][0], 2 * u, 2, EV_CKV, EV_LAT - EV_CKV)
            chunk_loop("ev_b", t["ev_w_in"][0], EV_LAT, EV_W // CHUNK)
            mod_loop(MEM_EV)
            mod_loop(MOBA)
            chunks("uq", t["ev_w_uq"][0], 0, 3, kt=4)
            chunks("ukv", t["ev_w_ukv"][0], 0, 4, kt=2)
            mod_loop(MLA)
            chunks("ev_out", t["ev_w_out"][0], 0, 4, kt=EV_VW // P)
            chunk_loop("od_b", t["od_w_in"][0], 0, OD_IN // CHUNK)
            chunks("od_c", t["od_w_in"][0], OD_IN // CHUNK * CHUNK, 1, n=OD_IN % CHUNK)
            for h in OD_LOOPS:
                mod_loop(h)
            chunks("mod_last", t["mod_w_2"][1], 11 * CHUNK, 1)
            chunks("od_out", t["od_w_out"][0], 0, 4, kt=OD_VW // P)

            gwv = t["lru_gate_w_2"][0].rearrange("d g n c e -> c d g n e")
            lw = t["lru_w_in_2"][0]

            def lru_units(i):
                loop = i is not None
                for b in range(2):
                    n = sp.snap(i * 2 + b) if loop else b
                    for part in range(2):
                        for half in range(2):
                            U = UNIT0["lru_in"] + b * 4 + part * 2 + half
                            unit(U, lw, half * 8, 8, i * 256 + (part * D + b * P) if loop else part * D + b * P, P, i, 8 if loop else 0)
                    if loop:
                        sp.wait_ge(s_gt, i * 2 + b - 1)
                    else:
                        sp.wait_ge(s_xn, 1)
                    for d in range(2):
                        for g in range(2):
                            sp.dma_start(GW[:, b, d * 2 + g, :], gwv[:, d, g, bass.ds(n, 1), :]).then_inc(s_gw[b], 16)
            lru_units(None)
            with sp.Fori(1, KT // 2) as i:
                lru_units(i)
            chunk_loop("lru_out", t["lru_w_out_2"][0], 0, 4)

            def att_units(i=None):
                for j in range(4):
                    for u in range(8):
                        unit(UNIT0["att_in"] + j * 8 + u, t["att_w_in_2"][0], u * 2, 2, j * D if i is None else i * CHUNK + j * D,
                             CHUNK, i, 32)
            att_units()
            with sp.Fori(1, GROUPS) as i:
                att_units(i)
            chunk_loop("att_out", t["att_w_out_2"][0], 0, 4)
            ov = out.rearrange("b (t p) d -> p (b t) d", p=P)
            for c in range(4):
                sp.wait_ge(s_re, RES0["att_out"] + c + 1)
                sp.dma_start(ov[:, :, c * CHUNK:(c + 1) * CHUNK], X[:, :, c * CHUNK:(c + 1) * CHUNK]).then_inc(s_out, 16)
            sp.wait_ge(s_out, 64)

        @block.tensor
        def _(pe):
            def split_ready(U, i=None, per=0):
                pe.wait_ge(*lo_made(U, i, per))

            def multiply(U, k0, nk, kt, n, tiles, x, i=None, per=0, hold=None):
                split_ready(U, i, per)
                wh, wl = (W[:, U % SLOTS, 0:nk * n].rearrange("p (k n) -> p k n", k=nk) for W in (WH, WL))
                for k in range(k0, k0 + nk):
                    for m, bank in tiles:
                        if hold is not None and k == k0 and m == hold[0]:
                            pe.wait_ge(*hold[1])
                        xh, xl = x(k, m)
                        for j, (a, w) in enumerate(((xh, wh), (xh, wl), (xl, wh))):
                            mm = pe.matmul(PS[:, bank, 0:n], a, w[:, k - k0, :], start=(k == 0 and j == 0), stop=(k == kt - 1 and j == 2))
                mm.then_inc(s_wused, 1)

            def product(stage, c, kt, n, tiles, x, i=None, per=0):
                units = -(-kt // 2)
                for u in range(units):
                    multiply(UNIT0[stage] + c * units + u, 2 * u, min(2, kt - 2 * u), kt, n, tiles, x, i, per)

            def chunk(stage, c, kt, n, x, i=None, per=0, step=0):
                g = CHUNK0[stage] + c
                if g >= 2:
                    pe.wait_ge(s_ge, at(g - 1, i, step))
                product(stage, c, kt, n, [(m, 2 * (g % 2) + m) for m in range(TT)], x, i, per)

            def residual(stage, kt):
                for c in range(4):
                    if c >= 2:
                        pe.wait_ge(s_re, RES0[stage] + c - 1)
                    product(stage, c, kt, CHUNK, [(m, 2 * (c % 2) + m) for m in range(TT)], xt)

            def xt(k, m):
                cols = slice(k * SEQ + m * P, k * SEQ + (m + 1) * P)
                return ATH[:, cols], ATL[:, cols]

            fills = [0]

            def to_features(rows, first=0, count=8, before=None):
                for j in range(first, first + count):
                    q = fills[0]
                    if q >= 4:
                        pe.wait_ge(s_tmp, q - 3)
                    if before is not None:
                        before(j)
                    for k in range(2):
                        for tt in range(TT):
                            col = (k * TT + tt) * P
                            mm = pe.transpose(PS[:, 4 + q % 4, col:col + P], rows(tt, 2 * j + k), ident)
                    mm.then_inc(s_xt, 1)
                    fills[0] += 1

            def tiles_of(rows):
                return lambda tt, k: rows[:, tt, k * P:(k + 1) * P]

            def features_ready(ahead=0):
                pe.wait_ge(s_xl, fills[0] - ahead)

            def fill_mod(stage, units, i=None):
                for u in units:
                    U = UNIT0[stage] + u
                    split_ready(U, i, 8)
                    for k in range(2 * u, 2 * u + 2):
                        for W in (WH, WL):
                            mm = pe.matmul(PS[:, 0, :], CS[:, 4 * k:4 * k + P], W[:, U % SLOTS, k % 2 * CHUNK:(k % 2 + 1) * CHUNK],
                                           start=(k == 0 and W is WH), stop=(k == KT - 1 and W is WL))
                    mm.then_inc(s_wused, 1)

            def turn_mod(m, rows, i=None):
                pe.wait_ge(s_mods, at(m + 1, i, 1))
                pe.wait_ge(s_modd, at(m + 1, i, 1))
                for j in range(4):
                    mm = pe.transpose(PS[:, 1, j * P:(j + 1) * P], rows[:, j * P:(j + 1) * P], ident)
                mm.then_inc(s_modt, 1)

            def head_loop(h):
                H = HE if h in EV_LOOPS else HO
                mod = "mod_" + h.name
                with pe.Fori(0, h.turns) as i:
                    n = lambda a, plus: i * 2 + (h.n0 + a + plus)
                    pair = h.kind == "swa"
                    for a in range(1 if pair else 2):
                        pe.wait_ge(s_stg, n(1 if pair else a, 1))
                        for tt in range(TT):
                            pe.transpose(PS[:, 2 + a, tt * P:(tt + 1) * P], QS[:, a, tt, 0:P], ident)
                        for tt in range(TT):
                            mm = pe.transpose(PS[:, 2 + a, SEQ + tt * P:SEQ + (tt + 1) * P], KS[:, a, tt, :], ident)
                        if h.kind == "mla":
                            for tt in range(TT):
                                mm = pe.transpose(PS[0:ROPE, 6 + a, tt * P:(tt + 1) * P], QS[:, a, tt, NOPE:NOPE + ROPE], ident)
                        mm.then_inc(s_t1, 2 if pair else 1)
                    fill_mod(mod, range(0, 2), i)
                    for a in range(2):
                        pe.wait_ge(s_qk, n(1 if pair else a, 1))
                        if pair:
                            qk = QKT[64 * a:64 * a + 64, 0, :]
                        else:
                            qk = QKT[:, a, :]
                        for tt in range(TT):
                            mla = h.kind == "mla"
                            mm = pe.matmul(PS[:, 6 + a, tt * SEQ:(tt + 1) * SEQ], qk[:, tt * P:(tt + 1) * P], qk[:, SEQ:2 * SEQ],
                                           start=True, stop=not mla)
                            if mla:
                                mm = pe.matmul(PS[:, 6 + a, tt * SEQ:(tt + 1) * SEQ], QRT[0:ROPE, a, tt * P:(tt + 1) * P],
                                               KPT[0:ROPE, :], start=False, stop=True)
                        mm.then_inc(s_sc, 1)
                    fill_mod(mod, range(2, 4), i)
                    for a in range(2):
                        pe.wait_ge(s_ex, n(a, 1))
                        pe.wait_ge(s_ye, n(a, 1))
                        for tt in range(TT):
                            for kt in range(TT):
                                mm = pe.transpose(PS[:, 4 + a, kt * SEQ + tt * P:kt * SEQ + (tt + 1) * P],
                                                  S[:, a, tt, kt * P:(kt + 1) * P], ident)
                        mm.then_inc(s_pt, 1)
                    fill_mod(mod, range(4, 6), i)
                    for a in range(2):
                        pe.wait_ge(s_pe, n(a, 1))
                        for tt in range(TT):
                            for kt in range(TT):
                                if pair:
                                    v = H[:, kt, h.v:h.v + SWA_DH]
                                elif h.mem is not None:
                                    v = MKV[:, h.mem, kt, bass.ds(i * 256 + (h.v + a * P), P)]
                                else:
                                    width = NOPE + MLA_DV if h.kind == "mla" else P
                                    v = H[:, kt, bass.ds(i * (2 * width) + (h.v + a * width), P)]
                                w = SWA_DH if pair else P
                                mm = pe.matmul(PS[:, 6 + a, tt * P:tt * P + w],
                                               PT[:, a, kt * SEQ + tt * P:kt * SEQ + (tt + 1) * P], v,
                                               start=(kt == 0), stop=(kt == TT - 1))
                        mm.then_inc(s_o, 1)
                    fill_mod(mod, range(6, 8), i)
                    for a in range(1 if pair else 2):
                        pe.wait_ge(s_ys, n(1 if pair else a, 1))
                        for tt in range(TT):
                            mm = pe.transpose(PS[:, 4 + a, tt * P:(tt + 1) * P], YS[:, a, tt, :], ident)
                        mm.then_inc(s_yt, 2 if pair else 1)
                    turn_mod(h.mod0, MODS_EV if h in EV_LOOPS else MODS_OD, i)

            pe.sem_inc(s_t1, 2)
            pe.wait_ge(s_const, 16)
            pe.wait_ge(s_rows, S_ROWS)
            for v, rows in enumerate(VEC_ROWS):
                mm = pe.transpose(PS[:, 0, v * P:v * P + rows], GR[0:rows, v, :], ident[0:rows, 0:rows])
            mm.then_inc(s_vt, 1)
            def mem0(k, m):
                return xt(k, m)

            def mem1(k, m):
                cols = slice(k * SEQ + m * P, k * SEQ + (m + 1) * P)
                return M1H[:, cols], M1L[:, cols]
            pe.wait_ge(s_mem, 16)
            to_features(tiles_of(MEMX))
            to_features(tiles_of(MEMX), 0, 4)
            pe.wait_ge(s_vec, 4)
            features_ready(4)
            chunk("mkv0", 0, KT, CHUNK, mem0)
            to_features(tiles_of(MEMX), 4, 4)
            chunk("mkv0", 1, KT, CHUNK, mem0)
            pe.wait_ge(s_x, 16)
            to_features(tiles_of(X), 0, 4)
            features_ready(4)
            chunk("mkv1", 0, KT, CHUNK, mem1)
            to_features(tiles_of(X), 4, 4)
            chunk("mkv1", 1, KT, CHUNK, mem1)
            features_ready()
            chunk("ev_a", 0, KT, CHUNK, xt)
            chunk("ev_a", 1, KT, EV_LAT - EV_CKV, xt)
            with pe.Fori(0, 6) as i:
                for c in range(2):
                    chunk("ev_b", c, KT, CHUNK, xt, i, 16, 2)
            pe.wait_ge(s_ge, CHUNK0["uq"])
            pe.wait_ge(s_rope, 1)
            to_features(tiles_of(HQ), 0, 3)
            for tt in range(TT):
                mm = pe.transpose(PS[0:ROPE, 3, tt * P:(tt + 1) * P], HQ[:, tt, EV_KPE:EV_KPE + ROPE], ident)
            mm.then_inc(s_kpe, 1)
            features_ready()
            pe.wait_ge(s_kpt, 1)
            pe.wait_ge(s_cs, 1)
            head_loop(MEM_EV)
            head_loop(MOBA)
            pe.wait_ge(s_modd, MLA.mod0 + 1)
            for c in range(3):
                chunk("uq", c, 4, CHUNK, xt)
            for c in range(4):
                chunk("ukv", c, 2, CHUNK, lambda k, m: xt(k + 4, m))
            pe.wait_ge(s_ge, CHUNK0["od_b"])
            head_loop(MLA)
            pe.wait_ge(s_ye, 20 + 2)
            pe.wait_ge(s_modd, SWA[0].mod0 + 1)
            residual("ev_out", EV_VW // P)

            def x_complete(stage):
                return lambda j: pe.wait_ge(s_re, RES0[stage] + j // 2 + 1)
            to_features(tiles_of(X), before=x_complete("ev_out"))
            features_ready()
            with pe.Fori(0, 6) as i:
                for c in range(2):
                    chunk("od_b", c, KT, CHUNK, xt, i, 16, 2)
            chunk("od_c", 0, KT, OD_IN % CHUNK, xt)
            pe.wait_ge(s_ge, CHUNK0["od_c"] + 1)
            for h in OD_LOOPS:
                head_loop(h)
            fill_mod("mod_last", range(8))
            turn_mod(N_MOD - 1, MODS_OD)
            pe.wait_ge(s_ye, N_HEADS + 2)
            pe.wait_ge(s_modd, N_MOD + 1)
            residual("od_out", OD_VW // P)

            pe.wait_ge(s_re, RES0["lru_out"])
            pe.wait_ge(s_xn, 1)
            to_features(tiles_of(CN))
            pe.wait_ge(s_xn, 2)
            to_features(tiles_of(XN))
            features_ready()

            with pe.Fori(0, KT // 2) as i:
                for b in range(2):
                    n = lambda plus: i * 2 + (b + plus)
                    pe.wait_ge(s_xc, n(1))
                    for part in range(2):
                        if part:
                            pe.wait_ge(s_gs, n(1))
                        for half in range(2):
                            U = UNIT0["lru_in"] + b * 4 + part * 2 + half
                            split_ready(U, i, 8)
                            for k in range(8):
                                w = slice(k * P, (k + 1) * P)
                                kk = half * 8 + k
                                for j, (W, x) in enumerate(((WH, FTH), (WH, FTL), (WL, FTH))):
                                    mm = pe.matmul(PS[:, part * 2 + b, :], W[:, U % SLOTS, w], x[:, kk, :],
                                                   start=(kk == 0 and j == 0), stop=(kk == KT - 1 and j == 2))
                            mm.then_inc(s_wused, 1)
                    pe.wait_ge(s_xc, n(3))
                    pe.wait_ge(s_gw[b], i * 64 + 64)
                    pe.wait_ge(s_sg, n(1))
                    for j in range(4):
                        mm = pe.matmul(PS[:, 4 + j, :], GW[:, b, j, :], XC[:, b, :, :].rearrange("p c s -> p (c s)"),
                                       start=True, stop=True)
                    mm.then_inc(s_gt, 1)

            def gate_row(j, bank, held):
                if held:
                    pe.wait_ge(s_gbe, held)
                pe.wait_ge(s_dg, j + 1)
                for k in range(4):
                    mm = pe.matmul(PS[:, bank, k * P:(k + 1) * P], ONES, DIAG(j)[:, k, :], start=True, stop=True)
                mm.then_inc(s_gb, 1)

            pe.wait_ge(s_y, KT + 2)
            for j in range(8):
                gate_row(j, 4 + j % 4, j - 3 if j >= 4 else 0)

            def ft(k, m):
                return FTH[:, k, m * P:(m + 1) * P], FTL[:, k, m * P:(m + 1) * P]

            def lru_y(k, m):
                if m == 0:
                    pe.wait_ge(s_ylo, k + 1)
                return ft(k, m)
            all_tiles = lambda b0: [(m, b0 + m) for m in range(4)]
            product("lru_out", 0, KT, CHUNK, all_tiles(0), lru_y)
            pe.wait_ge(s_gbe, 8)
            product("lru_out", 1, KT, CHUNK, all_tiles(4), ft)
            for c in range(2, 4):
                pe.wait_ge(s_re, RES0["lru_out"] + c - 1)
                product("lru_out", c, KT, CHUNK, all_tiles(4 * (c % 2)), ft)

            pe.wait_ge(s_re, RES0["att_out"])
            pe.wait_ge(s_xn, 3)
            to_features(tiles_of(CN))
            pe.wait_ge(s_xn, 4)
            to_features(tiles_of(XN))
            features_ready()

            def wait(s, value):
                if not isinstance(value, int) or value > 0:
                    pe.wait_ge(s, value)

            def att_unit(i, u):
                part, v = divmod(u, 8)
                hold = None
                if part == 0:
                    tiles = [(2, 0), (3, 1)]
                    if v == 0:
                        wait(s_dqe, i * 4 + 4)
                elif part == 1:
                    tiles = [(2, 2), (3, 3), (0, 0), (1, 1)]
                    if v == 0:
                        hold = (0, (s_dqe, i * 4 + 5))
                elif part == 2:
                    tiles = [(m, 4 + m) for m in range(4)]
                    if v == 0:
                        wait(s_oe, i * 8 + 8)
                else:
                    tiles = [(2, 0), (3, 1)]
                    if v == 0:
                        pe.wait_ge(s_dqe, i * 4 + 6)
                multiply(UNIT0["att_in"] + 32 + u, 2 * v, 2, KT, CHUNK, tiles, ft, i, 32, hold)

            def qk_transposes(i, j):
                if j == 0:
                    pe.wait_ge(s_qn, i + 2)
                    wait(s_dye, i + 1)
                else:
                    pe.wait_ge(s_e2, i * 4 + (4 + j))
                for kt in range(4):
                    pe.transpose(PS[:, 2, kt * P:(kt + 1) * P], RQK[:, kt, j * P:(j + 1) * P], ident)
                for tt in range(TT):
                    mm = pe.transpose(PS[:, 3, tt * P:(tt + 1) * P], RQK[:, 4 + tt, j * P:(j + 1) * P], ident)
                mm.then_inc(s_e1, 1)

            def scores(i, s):
                j, tt = divmod(s, 2)
                if s == 0:
                    pe.wait_ge(s_dqe, i * 4 + 3)
                else:
                    pe.wait_ge(s_e5, i * 8 + s)
                if tt == 0:
                    pe.wait_ge(s_e2, i * 4 + (j + 1))
                for c in range(2):
                    mm = pe.matmul(PS[:, 4 + c, :], DQK[64 * c:64 * c + 64, j, CHUNK + tt * P:CHUNK + (tt + 1) * P],
                                   DQK[64 * c:64 * c + 64, j, 0:CHUNK], start=True, stop=True)
                mm.then_inc(s_e3, 1)

            def weights_transposes(i, s):
                pe.wait_ge(s_e8, i * 8 + (s + 1))
                if s >= 1:
                    pe.wait_ge(s_e10, i * 8 + s)
                for kt in range(4):
                    mm = pe.transpose(PS[:, 6, kt * P:(kt + 1) * P], DE[:, s % 2, 0, kt * P:(kt + 1) * P], ident)
                mm.then_inc(s_e9, 1)

            def weights_values(i, s):
                pe.wait_ge(s_e10, i * 8 + (s + 1))
                if s >= 1:
                    pe.wait_ge(s_oe, i * 8 + s)
                j = s // 2
                for kt in range(4):
                    mm = pe.matmul(PS[:, 7, 0:P], DPT[:, s % 2, kt * P:(kt + 1) * P], RV[:, kt, j * P:(j + 1) * P],
                                   start=(kt == 0), stop=(kt == 3))
                mm.then_inc(s_e11, 1)

            def y_transposes(i):
                pe.wait_ge(s_oy, i + 1)
                for j in range(4):
                    for tt in range(TT):
                        col = (j % 2 * TT + tt) * P
                        mm = pe.transpose(PS[:, 2 + j // 2, col:col + P], OS[:, tt, j * P:(j + 1) * P], ident)
                mm.then_inc(s_dyt, 1)

            def projections_behind(i, heads):
                for u in range(16, 24):
                    att_unit(i, u)
                if heads:
                    pe.wait_ge(s_dqe, i * 4 + 6)
                    y_transposes(i)
                for u in range(24, 28):
                    att_unit(i, u)
                for j in range(4):
                    att_unit(i, 28 + j)
                    qk_transposes(i, j)

            for u in range(16):
                att_unit(-1, u)
            projections_behind(-1, False)
            with pe.Fori(0, GROUPS - 1) as i:
                scores(i, 0)
                for s in range(8):
                    att_unit(i, 2 * s)
                    weights_transposes(i, s)
                    if s < 7:
                        scores(i, s + 1)
                    att_unit(i, 2 * s + 1)
                    weights_values(i, s)
                projections_behind(i, True)

            def att_y(k, m):
                return DYH[:, k, m * P:(m + 1) * P], DYL[:, k, m * P:(m + 1) * P]

            def out_unit(c, u):
                if c == 0:
                    pe.wait_ge(s_ylo, KT + 2 * u + 2)
                multiply(UNIT0["att_out"] + 8 * c + u, 2 * u, 2, KT, CHUNK, [(m, 2 * (c % 2) + m) for m in range(TT)], att_y)
            last = GROUPS - 1
            scores(last, 0)
            pe.wait_ge(s_dqe, 4 * GROUPS)
            for s in range(8):
                if s < OUT_AHEAD:
                    out_unit(0, s)
                if s == 4:
                    pe.wait_ge(s_e2, 4 * GROUPS)
                if s >= 4:
                    gate_row(8 + s - 4, 2 + s % 2, 8 + s - 5 if s >= 6 else 0)
                weights_transposes(last, s)
                if s < 7:
                    scores(last, s + 1)
                weights_values(last, s)
            pe.wait_ge(s_gbe, 12)
            y_transposes(last)
            for c in range(4):
                if c >= 2:
                    pe.wait_ge(s_re, RES0["att_out"] + c - 1)
                for u in range(OUT_AHEAD if c == 0 else 0, 8):
                    out_unit(c, u)

        @block.scalar
        def _(act):
            act.dma_start(SUBG, t["att_subln_2"][0].unsqueeze(0).to_broadcast([P, 128])).then_inc(s_bc, 16)
            act.dma_start(QG, t["att_q_norm_2"][0].unsqueeze(0).to_broadcast([P, 64])).then_inc(s_bc, 16)
            act.dma_start(KG, t["att_k_norm_2"][0].unsqueeze(0).to_broadcast([P, 64])).then_inc(s_bc, 16)
            act.dma_start(LV, t["att_lambda_2"][0].rearrange("a b -> (a b)").unsqueeze(0).to_broadcast([P, 256])).then_inc(s_bc, 16)
            act.dma_start(SINK, t["od_sinks"][0].unsqueeze(0).to_broadcast([P, 16])).then_inc(s_bc, 16)

            def hi(U, n=UNIT, i=None, per=0):
                act.wait_ge(s_w[U % SLOTS], landed(U, i, per))
                if U >= SLOTS:
                    act.wait_ge(s_wused, at(U - SLOTS + 1, i, per))
                act.copy(WH[:, U % SLOTS, 0:n], RA[:, U % SLOTS, 0:n]).then_inc(s_hi, 1)

            def his(stage, units, n=UNIT, i=None, per=0):
                for u in units:
                    hi(UNIT0[stage] + u, n, i, per)

            def squares(r, rows, junk):
                for j, row in enumerate(rows):
                    if SQUARED[r] - len(rows) + j:
                        act.wait_ge(s_sq, SQUARED[r] - len(rows) + j)
                    act.activation(junk[:, 0:row.shape[-1]], row, ACT.Square, accum_out=ST[:, r, j:j + 1]).then_inc(s_sq, 1)

            def root(r, n):
                act.wait_ge(s_ms, r + 1)
                act.activation(ST[:, r, 0:n], ST[:, r, 0:n], ACT.Sqrt).then_inc(s_rt, 1)

            fills = [0]

            def scale_features(scale, shift, tmp, first=0, count=8):
                for j in range(first, first + count):
                    q = fills[0]
                    fills[0] += 1
                    act.wait_ge(s_xt, q + 1)
                    if q >= 4:
                        act.wait_ge(s_xl, q - 3)
                    for k in range(2):
                        ins = act.activation(tmp[:, q % 4, k * SEQ:(k + 1) * SEQ], PS[:, 4 + q % 4, k * SEQ:(k + 1) * SEQ], ACT.Identity,
                                             scale=scale(2 * j + k), bias=0.0 if shift is None else shift(2 * j + k))
                    ins.then_inc(s_tmp, 1)

            def evict(stage, c, dest, r, j0=0, n=CHUNK, silu=False, i=None, step=0):
                g = CHUNK0[stage] + c
                act.wait_ge(s_wused, at(multiplied(stage, c), i, 8 * step))
                for m in range(TT):
                    ins = act.activation(dest(m), PS[:, 2 * (g % 2) + m, 0:n], ACT.Silu if silu else ACT.Copy,
                                         scale=ST[:, r, j0 + m:j0 + m + 1])
                ins.then_inc(s_ge, 1)

            def head_loop(h):
                def modulation_hi(i, units):
                    for u in units:
                        U = UNIT0["mod_" + h.name] + u
                        if isinstance(i, int):
                            hi(U + 8 * i)
                        else:
                            hi(U, UNIT, i, 8)

                def turn(i):
                    n = lambda a, plus: i * 2 + (h.n0 + a + plus)
                    pair = h.kind == "swa"
                    for a in range(1 if pair else 2):
                        act.wait_ge(s_t1, n(1 if pair else a, 3))
                        ins = act.copy(QKT[:, a, :], PS[:, 2 + a, :])
                        if h.kind == "mla":
                            ins = act.copy(QRT[0:ROPE, a, :], PS[0:ROPE, 6 + a, 0:SEQ])
                        ins.then_inc(s_qk, 2 if pair else 1)
                    for a in range(2):
                        modulation_hi(i, [4 + a])
                        act.wait_ge(s_mx, n(a, 1))
                        for tt in range(TT):
                            ins = act.activation(S[:, a, tt, :], S[:, a, tt, :], ACT.Exp, bias=NM[:, a, tt:tt + 1],
                                                 accum_out=LS[:, a, tt:tt + 1])
                        if pair:
                            ins = act.activation(ES[:, a, :], SN[:, a, :], ACT.Exp)
                        ins.then_inc(s_ex, 1)
                    modulation_hi(i, range(6, 12))
                    for a in range(1 if pair else 2):
                        act.wait_ge(s_yt, n(1 if pair else a, 1))
                        y = i * SEQ + h.y0 * SEQ if pair else i * (2 * SEQ) + (h.y0 + a) * SEQ
                        act.copy(ATH[:, bass.ds(y, SEQ)], PS[:, 4 + a, 0:SEQ]).then_inc(s_yh, 2 if pair else 1)
                with act.Fori(0, h.turns - 1) as i:
                    turn(i)
                turn(h.turns - 1)

            def token_tiles(rows):
                return [rows[:, tt, :] for tt in range(TT)]

            his("mkv0", range(0, 4))
            act.wait_ge(s_vec, 4)
            gvec = lambda name: (lambda k: vec(name, k))
            scale_features(gvec("ev_mem_norm_g"), None, TMP_X)
            scale_features(gvec("od_mem_norm_g"), None, TMP_X, 0, 4)
            his("mkv0", range(4, 8))
            act.wait_ge(s_mem, 16)
            squares(0, token_tiles(MEMX), JUNK_A)
            act.wait_ge(s_x, 16)
            squares(1, token_tiles(X), JUNK_A)
            root(0, 2)
            root(1, 2)
            act.activation(COND, GT[:, VEC_AT["c_2"]:VEC_AT["c_2"] + 32].rearrange("p (v k) -> p k v", v=2), ACT.Silu).then_inc(s_cond, 1)
            act.wait_ge(s_cond, 1)
            act.copy(CSV[:, :, 0:2], COND).then_inc(s_cond, 1)
            act.wait_ge(s_lam, 1)
            act.activation(SC[:, 0:32], SC[:, 0:32], ACT.Exp, scale=-1.0)
            act.activation(SC[:, 64:66], SC[:, 64:66], ACT.Exp).then_inc(s_exl, 1)
            his("mkv0", range(8, 12))
            scale_features(gvec("od_mem_norm_g"), None, TMP_X, 4, 4)
            act.wait_ge(s_rs, 2)
            kv = lambda l, c: (lambda m: MKV[:, l, m, c * CHUNK:(c + 1) * CHUNK])
            evict("mkv0", 0, kv(0, 0), 0)
            his("mkv0", range(12, 16))
            his("mkv1", range(0, 4))
            scale_features(gvec("ev_norm_g"), None, TMP_X, 0, 4)
            evict("mkv0", 1, kv(0, 1), 0)
            his("mkv1", range(4, 12))
            scale_features(gvec("ev_norm_g"), None, TMP_X, 4, 4)
            evict("mkv1", 0, kv(1, 0), 0)
            his("mkv1", range(12, 16))
            his("ev_a", range(0, 4))
            evict("mkv1", 1, kv(1, 1), 0)
            his("ev_a", range(4, 8))
            narrow = 2 * (EV_LAT - EV_CKV)
            his("ev_a", range(8, 12), narrow)
            evict("ev_a", 0, lambda m: HQ[:, m, 0:MLA_QR], 1)
            his("ev_a", range(12, 16), narrow)
            his("ev_b", range(0, 4))
            evict("ev_a", 1, lambda m: HQ[:, m, EV_CKV:EV_LAT], 1, n=EV_LAT - EV_CKV)
            his("ev_b", range(4, 8))

            def to_rows(H, c, i=None):
                return lambda m: H[:, m, c * CHUNK:(c + 1) * CHUNK] if i is None else H[:, m, bass.ds(i * 1024 + c * CHUNK, CHUNK)]

            def split_and_evict(stage, H, c, r, silu, i=None):
                his(stage, range(8 * c + 8, 8 * c + 12), i=i, per=16)
                evict(stage, c, to_rows(H, c, i), r, silu=silu, i=i, step=2)
                his(stage, range(8 * c + 12, 8 * c + 16), i=i, per=16)

            with act.Fori(0, 3) as i:
                for c in range(2):
                    split_and_evict("ev_b", HE, c, 1, False, i)
            split_and_evict("ev_b", HE, 6, 1, False)
            with act.Fori(0, 2) as i:
                for c in range(7, 9):
                    split_and_evict("ev_b", HE, c, 1, True, i)
            his("mod_mem_ev", range(0, 4))
            evict("ev_b", 11, to_rows(HE, 11), 1, silu=True)
            act.wait_ge(s_rope, 2)
            squares(2, [HQ[:, j % 2, lo:hi_] for j, (lo, hi_) in enumerate(((0, MLA_QR), (0, MLA_QR), (EV_CKV, EV_KPE), (EV_CKV, EV_KPE)))],
                    JUNK_A)
            act.wait_ge(s_sq, SQUARED[2])
            scale_features(lambda k: vec("ev_q_norm_g", k) if k < 4 else vec("ev_kv_norm_g", k - 4), None, TMP_LAT, 0, 3)
            root(2, 4)
            head_loop(MEM_EV)
            head_loop(MOBA)
            act.wait_ge(s_rs, 3)
            uq = lambda c: (lambda m: HE[:, m, EV_QA + c * CHUNK:EV_QA + (c + 1) * CHUNK])
            ukv = lambda c: (lambda m: HE[:, m, EV_KVA + c * CHUNK:EV_KVA + (c + 1) * CHUNK])
            his("uq", range(4, 6))
            evict("uq", 0, uq(0), 2, 0)
            his("ukv", range(0, 2))
            evict("uq", 1, uq(1), 2, 0)
            his("ukv", range(2, 4))
            evict("uq", 2, uq(2), 2, 0)
            for c in range(4):
                evict("ukv", c, ukv(c), 2, 2)
                his("mod_mla", [c])
            head_loop(MLA)
            his("ev_out", range(4, 40))

            his("od_b", range(0, 4))
            scale_features(gvec("od_norm_g"), None, TMP_X)
            act.wait_ge(s_re, RES0["od_out"])
            squares(3, token_tiles(X), JUNK_A)
            root(3, 2)
            his("od_b", range(4, 8))
            act.wait_ge(s_rs, 4)
            with act.Fori(0, 4) as i:
                for c in range(2):
                    split_and_evict("od_b", HO, c, 3, False, i)
            with act.Fori(0, 1) as i:
                for c in range(8, 10):
                    split_and_evict("od_b", HO, c, 3, True, i)
            split_and_evict("od_b", HO, 10, 3, True)
            narrow = 2 * (OD_IN % CHUNK)
            his("od_c", range(0, 4), narrow)
            evict("od_b", 11, to_rows(HO, 11), 3, silu=True)
            his("od_c", range(4, 8), narrow)
            his("mod_swa0", range(0, 4))
            evict("od_c", 0, lambda m: HO[:, m, OD_IN // CHUNK * CHUNK:OD_IN], 3, n=OD_IN % CHUNK, silu=True)
            for h in OD_LOOPS:
                head_loop(h)
            act.wait_ge(s_ys, N_HEADS)
            act.dma_start(CX, t["ctx_2"].rearrange("b (t p) d -> p (b t) d", p=P)).then_inc(s_ctx, 16)
            act.dma_start(FG, t["final_norm_g"].unsqueeze(0).to_broadcast([P, D])).then_inc(s_fg, 16)
            his("mod_last", range(4, 8))
            his("od_out", range(0, 13))
            act.wait_ge(s_ctx, 16)
            squares(4, token_tiles(CX), BUF[:, 0:D])
            his("od_out", range(13, 18))
            root(4, 2)
            his("od_out", range(18, 36))

            his("lru_in", range(0, 4))
            act.wait_ge(s_re, RES0["lru_out"])
            squares(5, token_tiles(X), BUF[:, 0:D])
            root(5, 2)
            mod_scale = lambda j: (lambda k: MSC[:, 16 * j + k:16 * j + k + 1])
            mod_shift = lambda l, w: (lambda k: MODT[:, l, k, w:w + 1])
            act.wait_ge(s_msc, 4)
            scale_features(mod_scale(1), mod_shift(0, 1), TMP_B)
            act.wait_ge(s_xf, 1)
            squares(6, token_tiles(X), BUF[:, 0:D])
            root(6, 2)
            scale_features(mod_scale(0), mod_shift(0, 0), TMP_B)
            his("lru_in", range(4, 8))
            act.sem_inc(s_sg, 1)

            def lru_block(b, ahead, i=None):
                n = lambda plus: b + plus if i is None else i * 2 + (b + plus)
                act.wait_ge(s_gt, n(1))
                act.wait_ge(s_y, n(2))
                for j in range(4):
                    act.activation(RI[:, j, :], PS[:, 4 + j, :], ACT.Sigmoid, bias=BV[:, b % 2, 5 + j:6 + j])
                act.activation(SG, PS[:, 2 + b % 2, :], ACT.Sigmoid).then_inc(s_sg, 1)
                act.wait_ge(s_sg, n(2))
                for d in range(2):
                    act.activation(LA[:, d, :], RI[:, 2 * d, :], ACT.Exp, scale=BV[:, b % 2, 9 + d:10 + d])
                for d in range(2):
                    ins = act.activation(LW[:, d, :], RI[:, 2 * d, :], ACT.Tanh, scale=BV[:, b % 2, 9 + d:10 + d])
                ins.then_inc(s_ab, 1)
                if ahead is not None:
                    hi(ahead, UNIT, i, 8)
                act.wait_ge(s_w2, n(1))
                act.activation(LWF, LWF, ACT.Sqrt, scale=-1.0).then_inc(s_sqr, 1)
                if ahead is not None:
                    for u in range(1, 4):
                        hi(ahead + u, UNIT, i, 8)

            with act.Fori(0, KT // 2 - 1) as i:
                for b in range(2):
                    lru_block(b, UNIT0["lru_in"] + 8 + 4 * b, i)
            lru_block(KT - 2, UNIT0["lru_out"])
            lru_block(KT - 1, None)

            def y_hi(first, count, dest, src):
                for k in range(first, first + count):
                    act.copy(dest[:, k, :], src[:, k, :]).then_inc(s_yhi, 1)

            def gate_rows_out(dest, j, bank):
                act.wait_ge(s_gb, j + 1)
                act.copy(dest[:, j % 4 * CHUNK:(j % 4 + 1) * CHUNK], PS[:, bank, :]).then_inc(s_gbe, 1)

            act.wait_ge(s_y, KT + 2)
            act.dma_start(CX, t["ctx_2"].rearrange("b (t p) d -> p (b t) d", p=P)).then_inc(s_cx2, 16)
            for j in range(8):
                y_hi(j, 1, FTH, YL)
                gate_rows_out(G_LAT if j < 4 else G_CTX, j, 4 + j % 4)
            y_hi(8, 8, FTH, YL)
            his("lru_out", range(4, 8))
            with act.Fori(1, 4) as i:
                his("lru_out", range(8), i=i, per=8)

            his("att_in", range(0, 4))
            act.wait_ge(s_re, RES0["att_out"])
            squares(7, token_tiles(CX), BUF[:, 12288:12288 + D])
            root(7, 2)
            squares(8, token_tiles(X), BUF[:, 12288:12288 + D])
            root(8, 2)
            scale_features(mod_scale(3), mod_shift(1, 1), TMP_B)
            scale_features(mod_scale(2), mod_shift(1, 0), TMP_B)

            def att_hi(i, units):
                for u in units:
                    hi(UNIT0["att_in"] + 32 + u if not isinstance(i, int) else UNIT0["att_in"] + 32 * (i + 1) + u, UNIT,
                       None if isinstance(i, int) else i, 32)

            def take_chunk(i, part, dest, tiles, bank, silu=False):
                act.wait_ge(s_wused, i * 32 + (UNIT0["att_in"] + 32 + 8 * part + 8))
                for m in range(tiles):
                    ins = act.activation(dest[:, m, :], PS[:, bank + m, :], ACT.Silu) if silu else act.copy(dest[:, m, :], PS[:, bank + m, :])
                ins.then_inc(s_dqe, 1)

            def exponentials(i, s):
                act.wait_ge(s_e4, i * 8 + (s + 1))
                for c in range(2):
                    ins = act.activation(DE[:, s % 2, c, :], PS[:, 4 + c, :], ACT.Exp, bias=NM[:, s % 2, c:c + 1],
                                         accum_out=LS[:, s % 2, c:c + 1])
                ins.then_inc(s_e5, 1)

            def weights_out(i, s):
                act.wait_ge(s_e9, i * 8 + (s + 1))
                act.copy(DPT[:, s % 2, :], PS[:, 6, :]).then_inc(s_e10, 1)

            def outputs_root(i):
                act.wait_ge(s_om, i + 1)
                act.activation(DS8, DS8, ACT.Sqrt).then_inc(s_or, 1)

            def outputs_out(i):
                act.wait_ge(s_dyt, i + 1)
                for j in range(2):
                    y = DYT[:, 4 * i + 2 * j:4 * i + 2 * j + 2, :] if isinstance(i, int) else DYT[:, bass.ds(i * 4 + 2 * j, 2), :]
                    ins = act.copy(y, PS[:, 2 + j, :].rearrange("p (k s) -> p k s", k=2))
                ins.then_inc(s_dye, 1)

            def qk_out(i, j):
                act.wait_ge(s_e1, i * 4 + (j + 5))
                act.copy(DQK[:, j, 0:CHUNK], PS[:, 2, :])
                act.copy(DQK[:, j, CHUNK:CHUNK + SEQ], PS[:, 3, 0:SEQ]).then_inc(s_e2, 1)

            def projections_behind(i, heads):
                take_chunk(i, 1, RQK[:, 0:4, :], 4, 0)
                att_hi(i, [20])
                if heads:
                    outputs_root(i)
                att_hi(i, [21, 22, 23])
                act.wait_ge(s_dm, i + 2)
                act.activation(DS48, DS48, ACT.Sqrt).then_inc(s_dp0, 1)
                att_hi(i, range(24, 28))
                if heads:
                    outputs_out(i)
                take_chunk(i, 2, RV, 4, 4)
                att_hi(i, range(28, 32))
                for j in range(4):
                    att_hi(i, [32 + j])
                    qk_out(i, j)
                take_chunk(i, 3, RG, 2, 0, silu=True)

            att_hi(-1, range(4, 12))
            take_chunk(-1, 0, RQK[:, 4:6, :], 2, 0)
            att_hi(-1, range(12, 20))
            projections_behind(-1, False)
            with act.Fori(0, GROUPS - 1) as i:
                exponentials(i, 0)
                for s in range(8):
                    att_hi(i, [2 * s + 4])
                    weights_out(i, s)
                    if s < 7:
                        exponentials(i, s + 1)
                    att_hi(i, [2 * s + 5])
                    if s == 3:
                        take_chunk(i, 0, RQK[:, 4:6, :], 2, 0)
                projections_behind(i, True)

            last = GROUPS - 1
            exponentials(last, 0)
            y_hi(0, 2, DYH, DYT)
            for s in range(8):
                if s < OUT_AHEAD:
                    his("att_out", [s + 4])
                weights_out(last, s)
                if s < 7:
                    exponentials(last, s + 1)
                if s < OUT_AHEAD - 1:
                    y_hi(2 * s + 2, 2, DYH, DYT)
                if s >= 4:
                    gate_rows_out(G_ATT, 8 + s - 4, 2 + s % 2)
            outputs_root(last)
            outputs_out(last)
            act.wait_ge(s_dye, GROUPS)
            y_hi(2 * OUT_AHEAD, KT - 2 * OUT_AHEAD, DYH, DYT)
            his("att_out", range(OUT_AHEAD + 4, 16))
            with act.Fori(2, 4) as i:
                his("att_out", range(8), i=i, per=8)

        @block.vector
        def _(dve):
            steps = [0]

            def link(ins):
                steps[0] += 1
                ins.then_inc(s_dve, 1)
                dve.wait_ge(s_dve, steps[0])

            def lo(U, n=UNIT, i=None, per=0):
                dve.wait_ge(s_hi, at(U + 1, i, per))
                dve.tensor_tensor(out=WL[:, U % SLOTS, 0:n], in0=RA[:, U % SLOTS, 0:n], in1=WH[:, U % SLOTS, 0:n].bitcast(F32),
                                  op=ALU.subtract).then_inc(s_lo, 1)

            def los(stage, units, n=UNIT, i=None, per=0):
                for u in units:
                    lo(UNIT0[stage] + u, n, i, per)

            def mean_square(r, widths):
                dve.wait_ge(s_sq, SQUARED[r])
                first = 0
                for n, width in widths:
                    ins = dve.tensor_scalar(ST[:, r, first:first + n], ST[:, r, first:first + n], 1.0 / width, EPS, ALU.mult, ALU.add)
                    first += n
                ins.then_inc(s_ms, 1)

            def rstd(r, n):
                dve.wait_ge(s_rt, r + 1)
                dve.reciprocal(ST[:, r, 0:n], ST[:, r, 0:n]).then_inc(s_rs, 1)

            fills = [0]

            def split_features(dest_hi, dest_lo, tmp, first=0, count=8):
                for j in range(first, first + count):
                    q = fills[0]
                    fills[0] += 1
                    dve.wait_ge(s_tmp, q + 1)
                    src, h = tmp[:, q % 4, :], dest_hi(j)
                    if len(h.shape) == 3:
                        src = src.rearrange("p (k s) -> p k s", k=2)
                    dve.tensor_copy(h, src).then_inc(s_xh, 1)
                    dve.wait_ge(s_xh, q + 1)
                    dve.tensor_tensor(out=dest_lo(j), in0=src, in1=h.bitcast(F32), op=ALU.subtract).then_inc(s_xl, 1)

            def rope(x, table, rot, heads):
                tab = const(table).rearrange("p (t z c) -> p t z c", t=TT, z=2)
                half = rot // 2
                ra = ROT_A[:, 0:heads * rot].rearrange("p (h c) -> p h c", h=heads)
                rb = ROT_B[:, 0:heads * rot].rearrange("p (h c) -> p h c", h=heads)

                def wide(z, tt, first, end):
                    return tab[:, tt, z, first:end].unsqueeze(1).to_broadcast([P, heads, end - first])
                for tt in range(TT):
                    v = x(tt)
                    dve.tensor_tensor(out=ra, in0=v, in1=wide(0, tt, 0, rot), op=ALU.mult)
                    dve.tensor_tensor(out=rb[:, :, 0:half], in0=v[:, :, half:rot], in1=wide(1, tt, 0, half), op=ALU.mult)
                    link(dve.tensor_tensor(out=rb[:, :, half:rot], in0=v[:, :, 0:half], in1=wide(1, tt, half, rot), op=ALU.mult))
                    link(dve.tensor_tensor(out=v, in0=ra, in1=rb, op=ALU.add))
                dve.sem_inc(s_rope, 1)

            def residual_add(stage, c):
                dve.wait_ge(s_wused, multiplied(stage, c))
                for m in range(TT):
                    x = X[:, m, c * CHUNK:(c + 1) * CHUNK]
                    ins = dve.tensor_tensor(out=x, in0=PS[:, 2 * (c % 2) + m, :], in1=x, op=ALU.add)
                ins.then_inc(s_re, 1)

            def mod_rows(stage, rows, i=None):
                dve.wait_ge(s_wused, at(UNIT0[stage] + 8, i, 8))
                dve.tensor_copy(rows[0:4, :], PS[0:4, 0, :]).then_inc(s_mods, 1)

            def mod_columns(m, layer, c, i=None):
                dve.wait_ge(s_modt, at(m + 1, i, 1))
                first = at(4 * c, i, 4)
                bias = GT[:, bass.ds(first + (VEC_AT["mod_b_2"] + 48 * layer), 4)]
                to = MODT[:, layer, bass.ds(first, 4), :]
                rows = PS[:, 1, :].rearrange("p (k w) -> p k w", w=P)
                dve.tensor_tensor(out=to, in0=rows[:, :, 0:2], in1=bias.unsqueeze(2).to_broadcast([P, 4, 2]), op=ALU.add).then_inc(s_modb, 1)
                dve.wait_ge(s_modb, at(m + 1, i, 1))
                dve.tensor_tensor(out=to, in0=rows[:, :, 2:4], in1=to, op=ALU.add).then_inc(s_modd, 1)

            def head_loop(h):
                H = HE if h in EV_LOOPS else HO

                def modulation_lo(i, units):
                    for u in units:
                        U = UNIT0["mod_" + h.name] + u
                        if u < 8 and LO_BY[U][0]:
                            continue
                        if isinstance(i, int):
                            lo(U + 8 * i)
                        else:
                            lo(U, UNIT, i, 8)

                def turn(i):
                    n = lambda a, plus: i * 2 + (h.n0 + a + plus)
                    pair = h.kind == "swa"
                    for a in range(2):
                        dve.wait_ge(s_sc, n(a, 1))
                        flat = S[:, a, :, :].rearrange("p t c -> p (t c)")
                        if h.mask is None:
                            ins = dve.tensor_scalar(flat, PS[:, 6 + a, :], h.scale, None, ALU.mult)
                        else:
                            ins = dve.scalar_tensor_tensor(out=flat, in0=PS[:, 6 + a, :], scalar=h.scale, in1=const(h.mask),
                                                           op0=ALU.mult, op1=ALU.add)
                        ins.then_inc(s_sm, 1)
                        dve.wait_ge(s_sm, n(a, 1))
                        ins = dve.tensor_reduce(NM[:, a, :], S[:, a, :, :], AX, ALU.max, negate=True)
                        if pair:
                            ins.then_inc(s_sk, 1)
                            w = i * 2 + (h.sink + a + 1)
                            dve.wait_ge(s_sk, w)
                            nsink = NSINK[:, bass.ds(i * 2 + (h.sink + a), 1), :].squeeze(1)
                            dve.tensor_tensor(out=NM[:, a, :], in0=NM[:, a, :], in1=nsink, op=ALU.min).then_inc(s_sk2, 1)
                            dve.wait_ge(s_sk2, w)
                            ins = dve.tensor_tensor(out=SN[:, a, :], in0=NM[:, a, :], in1=nsink, op=ALU.subtract)
                        ins.then_inc(s_mx, 1)
                    modulation_lo(i, range(4, 6))
                    for a in range(2):
                        dve.wait_ge(s_pt, n(a, 1))
                        dve.tensor_copy(PT[:, a, :], PS[:, 4 + a, :]).then_inc(s_pe, 1)
                    modulation_lo(i, range(6, 9))
                    for a in range(2):
                        dve.wait_ge(s_o, n(a, 1))
                        if pair:
                            dve.tensor_tensor(out=LS[:, a, :], in0=LS[:, a, :], in1=ES[:, a, :], op=ALU.add).then_inc(s_l2, 1)
                            dve.wait_ge(s_l2, i * 2 + (h.sink + a + 1))
                        dve.reciprocal(RL[:, a, :], LS[:, a, :]).then_inc(s_rl, 1)
                        dve.wait_ge(s_rl, n(a, 1))
                        w = SWA_DH if pair else P
                        for tt in range(TT):
                            y = YS[:, 0, tt, a * w:(a + 1) * w] if pair else YS[:, a, tt, :]
                            gate = H[:, tt, bass.ds(i * (2 * w) + (h.gate + a * w), w)]
                            ins = dve.scalar_tensor_tensor(out=y, in0=PS[:, 6 + a, tt * P:tt * P + w], scalar=RL[:, a, tt:tt + 1],
                                                           in1=gate, op0=ALU.mult, op1=ALU.mult)
                        ins.then_inc(s_ys, 1)
                    mod_rows("mod_" + h.name, MODS_EV if h in EV_LOOPS else MODS_OD, i)
                    modulation_lo(i, range(9, 12))
                    for a in range(1 if pair else 2):
                        dve.wait_ge(s_yh, n(1 if pair else a, 1))
                        y = bass.ds(i * SEQ + h.y0 * SEQ if pair else i * (2 * SEQ) + (h.y0 + a) * SEQ, SEQ)
                        dve.tensor_tensor(out=ATL[:, y], in0=PS[:, 4 + a, 0:SEQ], in1=ATH[:, y].bitcast(F32),
                                          op=ALU.subtract).then_inc(s_ye, 2 if pair else 1)
                    mod_columns(h.mod0, h.mod_layer, h.mod_chunk0, i)
                with dve.Fori(0, h.turns - 1) as i:
                    turn(i)
                turn(h.turns - 1)

            dve.wait_ge(s_vt, 1)
            for v, rows in enumerate(VEC_ROWS):
                dve.tensor_copy(GT[:, VEC_COL[v]:VEC_COL[v] + rows], PS[:, 0, v * P:v * P + rows]).then_inc(s_vec, 1)
            dve.sem_inc(s_modd, 1)
            link(dve.memset(MODS_EV, 0.0))
            dve.sem_inc(s_ye, 2)
            dve.wait_ge(s_vec, 4)
            los("mkv0", range(0, 4))
            x_hi = lambda j: ATH[:, j * 2 * SEQ:(j + 1) * 2 * SEQ]
            x_lo = lambda j: ATL[:, j * 2 * SEQ:(j + 1) * 2 * SEQ]
            mem_hi = lambda j: M1H[:, j * 2 * SEQ:(j + 1) * 2 * SEQ]
            mem_lo = lambda j: M1L[:, j * 2 * SEQ:(j + 1) * 2 * SEQ]
            split_features(x_hi, x_lo, TMP_X)
            split_features(mem_hi, mem_lo, TMP_X, 0, 4)
            los("mkv0", range(4, 8))
            mean_square(0, [(2, D)])
            mean_square(1, [(2, D)])
            rstd(0, 2)
            rstd(1, 2)
            dve.memset(CS[:, 4 * KT:].bitcast(F32), 0.0)
            dve.wait_ge(s_cond, 2)
            dve.tensor_tensor(out=CSV[:, :, 2:4], in0=COND, in1=CSV[:, :, 0:2].bitcast(F32), op=ALU.subtract).then_inc(s_cs, 1)

            lam = vec("lru_lambda_2", 0, 32)
            dve.wait_ge(s_bc, 16 * N_CONST_BC)
            link(dve.tensor_scalar(SC[:, 32:64], lam, -1.0, None, ALU.mult))
            dve.tensor_tensor(out=SC[:, 0:32], in0=lam, in1=SC[:, 32:64], op=ALU.max)
            dve.tensor_tensor(out=LVP[:, 0:64], in0=LV[:, 0:64], in1=LV[:, 64:128], op=ALU.mult)
            link(dve.tensor_tensor(out=LVP[:, 64:128], in0=LV[:, 128:192], in1=LV[:, 192:256], op=ALU.mult))
            dve.tensor_reduce(SC[:, 64:66], LVP.rearrange("p (z c) -> p z c", z=2), AX, ALU.add).then_inc(s_lam, 1)
            los("mkv0", range(8, 12))
            split_features(mem_hi, mem_lo, TMP_X, 4, 4)
            los("mkv0", range(12, 16))
            los("mkv1", range(0, 4))
            split_features(x_hi, x_lo, TMP_X, 0, 4)
            los("mkv1", range(4, 8))
            dve.wait_ge(s_exl, 1)
            link(dve.tensor_tensor(out=SC[:, 66:67], in0=SC[:, 65:66], in1=SC[:, 64:65], op=ALU.subtract))
            link(dve.tensor_scalar(NLAM, SC[:, 66:67], -LAM_INIT, None, ALU.add))
            dve.tensor_scalar(SUBG, SUBG, 1.0 - LAM_INIT, None, ALU.mult)
            dve.tensor_scalar(QG, QG, ATT_DH ** -0.5, None, ALU.mult)
            dve.tensor_scalar(NSINK, SINK.unsqueeze(2).to_broadcast([P, SWA_HEADS, 2]), -1.0, None, ALU.mult)
            y, z, z2, acc = SC[:, 0:32], SC[:, 68:100], SC[:, 100:132], SC[:, 132:164]
            link(dve.tensor_scalar(z, y, 2.0, None, ALU.add))
            link(dve.reciprocal(z, z))
            link(dve.tensor_tensor(out=z, in0=z, in1=y, op=ALU.mult))
            link(dve.tensor_tensor(out=z2, in0=z, in1=z, op=ALU.mult))
            link(dve.tensor_scalar(acc, z2, 1.0 / 19, 1.0 / 17, ALU.mult, ALU.add))
            for k in range(15, 0, -2):
                link(dve.tensor_tensor(out=acc, in0=acc, in1=z2, op=ALU.mult))
                link(dve.tensor_scalar(acc, acc, 1.0 / k, None, ALU.add))
            link(dve.tensor_tensor(out=acc, in0=acc, in1=z, op=ALU.mult))
            link(dve.tensor_scalar(z, SC[:, 32:64], 0.0, None, ALU.max))
            link(dve.scalar_tensor_tensor(out=acc, in0=acc, scalar=2.0, in1=z, op0=ALU.mult, op1=ALU.add))
            link(dve.memset(LTAB[:], 0.0))
            for first, n, src in ((0, 4, vec("lru_conv_w_2", 0, 64)), (4, 1, vec("lru_conv_b_2", 0, 16)), (5, 4, vec("lru_gate_b_2", 0, 64))):
                dve.tensor_copy(LTAB[:, 0:KT, first:first + n], src.rearrange("p (j k) -> p k j", j=n))
            link(dve.tensor_scalar(LTAB[:, 0:KT, 9:11], acc.rearrange("p (d k) -> p k d", d=2), -LRU_C, None, ALU.mult))
            dve.sem_inc(s_ltab, 1)

            los("mkv1", range(8, 12))
            split_features(x_hi, x_lo, TMP_X, 4, 4)
            los("mkv1", range(12, 16))
            los("ev_a", range(8))
            los("ev_a", range(8, 16), 2 * (EV_LAT - EV_CKV))
            los("ev_b", range(8))
            dve.wait_ge(s_consta, 16)
            dve.wait_ge(s_ge, CHUNK0["ev_b"])
            rope(lambda tt: HQ[:, tt, EV_KPE:EV_KPE + ROPE].unsqueeze(1), "mla", ROPE, 1)
            with dve.Fori(1, 6) as i:
                los("ev_b", range(8), i=i, per=8)
            dve.wait_ge(s_ge, CHUNK0["ev_b"] + 4)
            rope(lambda tt: HE[:, tt, EV_QKV:EV_QKV + 2048].rearrange("p (h c) -> p h c", c=DH)[:, :, 0:32], "r32", 32, 16)
            with dve.Fori(6, 12) as i:
                los("ev_b", range(8), i=i, per=8)
            los("mod_mem_ev", range(0, 4))
            split_features(x_hi, x_lo, TMP_LAT, 0, 3)
            dve.wait_ge(s_kpe, 1)
            dve.tensor_copy(KPT[0:ROPE, :], PS[0:ROPE, 3, 0:SEQ]).then_inc(s_kpt, 1)
            mean_square(2, [(2, MLA_QR), (2, MLA_KVR)])
            rstd(2, 4)
            head_loop(MEM_EV)
            head_loop(MOBA)
            los("uq", range(4, 6))
            los("ukv", range(4))
            los("mod_mla", range(4))
            dve.wait_ge(s_ge, CHUNK0["ukv"])
            rope(lambda tt: HE[:, tt, EV_QA:EV_KVA].rearrange("p (h c) -> p h c", c=NOPE + ROPE)[:, :, NOPE:NOPE + ROPE],
                 "mla", ROPE, MLA_HEADS)
            head_loop(MLA)
            link(dve.memset(MODS_OD, 0.0))
            for c in range(4):
                if c:
                    los("ev_out", range(10 * c, 10 * c + 4))
                    residual_add("ev_out", c - 1)
                los("ev_out", range(10 * c + 4, 10 * c + 10))

            los("od_b", range(0, 4))
            residual_add("ev_out", 3)
            split_features(x_hi, x_lo, TMP_X)
            mean_square(3, [(2, D)])
            rstd(3, 2)
            los("od_b", range(4, 8))
            with dve.Fori(1, 8) as i:
                los("od_b", range(8), i=i, per=8)
            dve.wait_ge(s_ge, CHUNK0["od_b"] + 6)
            rope(lambda tt: HO[:, tt, 0:OD_VC].rearrange("p (h c) -> p h c", c=SWA_DH)[:, :, 0:16], "r16", 16, 18)
            rope(lambda tt: HO[:, tt, OD_QD:OD_VD].rearrange("p (h c) -> p h c", c=DH)[:, :, 0:32], "r32", 32, 12)
            with dve.Fori(8, 12) as i:
                los("od_b", range(8), i=i, per=8)
            los("od_c", range(8), 2 * (OD_IN % CHUNK))
            los("mod_swa0", range(4))
            dve.wait_ge(s_ge, CHUNK0["od_c"] + 1)
            for h in OD_LOOPS:
                head_loop(h)
            los("mod_last", range(4, 8))
            mod_rows("mod_last", MODS_OD)
            mod_columns(N_MOD - 1, 1, 11)
            dve.wait_ge(s_modd, N_MOD + 1)
            for l in range(2):
                for w in range(2):
                    j = 2 * l + w
                    dve.scalar_tensor_tensor(out=MSC[:, 16 * j:16 * j + 16], in0=MODT[:, l, KT:2 * KT, w], scalar=1.0,
                                             in1=vec("norm_g_2", 16 * l, 16), op0=ALU.add, op1=ALU.mult).then_inc(s_msc, 1)

            def normalized(dest, rows, r):
                dve.wait_ge(s_rs, r + 1)
                for tt in range(TT):
                    ins = dve.tensor_scalar(dest[:, tt, :], rows[:, tt, :], ST[:, r, tt:tt + 1], None, ALU.mult)
                ins.then_inc(s_xn, 1)

            los("od_out", range(0, 13))
            residual_add("od_out", 0)
            los("od_out", range(13, 18))
            mean_square(4, [(2, D)])
            los("od_out", range(18, 22))
            residual_add("od_out", 1)
            rstd(4, 2)
            normalized(CN, CX, 4)
            los("od_out", range(22, 31))
            residual_add("od_out", 2)
            los("od_out", range(31, 36))
            residual_add("od_out", 3)

            mean_square(5, [(2, D)])
            rstd(5, 2)
            dve.wait_ge(s_rs, 6)
            dve.wait_ge(s_fg, 16)
            for tt in range(TT):
                ins = dve.scalar_tensor_tensor(out=X[:, tt, :], in0=X[:, tt, :], scalar=ST[:, 5, tt:tt + 1], in1=FG,
                                               op0=ALU.mult, op1=ALU.mult)
            ins.then_inc(s_xf, 1)
            part = lambda T, c: (lambda j: T[:, 2 * j:2 * j + 2, c * SEQ:(c + 1) * SEQ])
            split_features(part(FTH, 0), part(FTL, 0), TMP_B)
            mean_square(6, [(2, D)])
            rstd(6, 2)
            normalized(XN, X, 6)
            split_features(part(FTH, 1), part(FTL, 1), TMP_B)
            dve.memset(ONES, 1.0)

            def conv(n, b):
                dve.wait_ge(s_wused, n(0) * 4 + (UNIT0["lru_in"] + 2))
                dve.wait_ge(s_bv, n(1))
                u = PS[:, b, :].rearrange("p (c s) -> p c s", c=2)
                xc = XC[:, b, :, :]
                taps = BV[:, b, :]
                dve.tensor_scalar(xc, u, taps[:, 2:3], taps[:, 4:5], ALU.mult, ALU.add).then_inc(s_cv, 1)
                for step, (j, first, end) in enumerate(((0, 2, SEQ), (1, 1, SEQ), (3, 0, SEQ - 1))):
                    dve.wait_ge(s_cv, n(0) * 3 + (step + 1))
                    ins = dve.scalar_tensor_tensor(out=xc[:, :, first:end], in0=u[:, :, first + j - 2:end + j - 2], scalar=taps[:, j:j + 1],
                                                   in1=xc[:, :, first:end], op0=ALU.mult, op1=ALU.add)
                    ins.then_inc(s_cv if step < 2 else s_xc, 1)

            def decays(n, b):
                dve.wait_ge(s_ab, n(1))
                dve.tensor_tensor(out=LTMP, in0=LAF, in1=LAF, op=ALU.mult).then_inc(s_w2a, 1)
                dve.wait_ge(s_w2a, n(1))
                dve.scalar_tensor_tensor(out=LWF, in0=LTMP, scalar=1.0, in1=LWF, op0=ALU.add, op1=ALU.mult).then_inc(s_w2, 1)
                dve.tensor_tensor(out=SG, in0=PS[:, 2 + b, :], in1=SG, op=ALU.mult).then_inc(s_gs, 1)

            def recur(n):
                dve.wait_ge(s_sqr, n(1))
                dve.wait_ge(s_ix, n(1))
                dve.tensor_tensor(out=LW[:], in0=LW[:], in1=RI[:, 1::2, :], op=ALU.mult).then_inc(s_b, 1)
                dve.wait_ge(s_b, n(1))
                scan = lambda h, first, end, step, h0: dve.tensor_tensor_scan(
                    out=HSC[:, h, first:end][:, ::step], data0=LA[:, h, first:end][:, ::step], data1=LW[:, h, first:end][:, ::step],
                    initial=h0, op0=ALU.mult, op1=ALU.add)
                scan(0, 0, 2 * SEQ, 1, 0.0)
                scan(1, 0, SEQ, -1, 0.0).then_inc(s_sn, 1)
                dve.wait_ge(s_sn, n(0) * 2 + 1)
                scan(1, SEQ, 2 * SEQ, -1, HSC[:, 1, 0:1]).then_inc(s_sn, 1)
                dve.wait_ge(s_sn, n(0) * 2 + 2)
                dve.tensor_tensor(out=HSC[:, 0, :], in0=HSC[:, 0, :], in1=HSC[:, 1, :], op=ALU.add).then_inc(s_hsum, 1)
                dve.wait_ge(s_hsum, n(1))
                y = YL[:, n(0), :] if isinstance(n(0), int) else YL[:, bass.ds(n(0), 1), :].squeeze(1)
                dve.tensor_tensor(out=y, in0=HSC[:, 0, :], in1=SG, op=ALU.mult).then_inc(s_y, 1)

            def block_n(b, i=None):
                return lambda plus: b + plus if i is None else i * 2 + (b + plus)
            for s, n in ((s_xc, 2), (s_gs, 2), (s_y, 2)):
                dve.sem_inc(s, n)
            conv(block_n(0), 0)
            with dve.Fori(0, KT // 2 - 1) as i:
                for b in range(2):
                    decays(block_n(b, i), b)
                    conv(block_n(b + 1, i), 1 - b)
                    recur(block_n(b, i))
            decays(block_n(KT - 2), 0)
            conv(block_n(KT - 1), 1)
            recur(block_n(KT - 2))
            los("lru_out", range(0, 4))
            decays(block_n(KT - 1), 1)
            recur(block_n(KT - 1))

            def gate_diagonals(j, layer, w):
                if j >= 2:
                    dve.wait_ge(s_gb, j - 1)
                for k in range(4):
                    ins = dve.tensor_scalar(DIAG(j)[:, k, :], ident, MODT[:, layer, 2 * KT + 4 * (j % 4) + k, w:w + 1], None, ALU.mult)
                ins.then_inc(s_dg, 1)

            def y_lo(first, count, dest_hi, dest_lo, src, base):
                for k in range(first, first + count):
                    dve.wait_ge(s_yhi, base + k + 1)
                    dve.tensor_tensor(out=dest_lo[:, k, :], in0=src[:, k, :], in1=dest_hi[:, k, :].bitcast(F32),
                                      op=ALU.subtract).then_inc(s_ylo, 1)

            def gated_residual(stage, c, tiles, gates, bank, rows, scratch):
                cols = slice(c * CHUNK, (c + 1) * CHUNK)
                q = RES0[stage] + c
                dve.wait_ge(s_wused, multiplied(stage, c))
                dve.wait_ge(s_gbe, rows)
                dve.wait_ge(s_re, q)
                for m in range(len(tiles)):
                    ins = dve.tensor_tensor(out=scratch[:, m * CHUNK:(m + 1) * CHUNK], in0=PS[:, bank + m, :], in1=gates[m][:, cols], op=ALU.mult)
                ins.then_inc(s_rh, 1)
                dve.wait_ge(s_rh, q + 1 - RES0["lru_out"])
                for m in range(len(tiles)):
                    x = tiles[m][:, cols]
                    ins = dve.tensor_tensor(out=x, in0=scratch[:, m * CHUNK:(m + 1) * CHUNK], in1=x, op=ALU.add)
                ins.then_inc(s_re, 1)

            for j in range(8):
                gate_diagonals(j, 0, j // 4)
                y_lo(j, 1, FTH, FTL, YL, 0)
            y_lo(8, 8, FTH, FTL, YL, 0)
            dve.wait_ge(s_cx2, 16)

            def lru_residual(c):
                gated_residual("lru_out", c, [CX[:, 0, :], CX[:, 1, :], X[:, 0, :], X[:, 1, :]], [G_CTX, G_CTX, G_LAT, G_LAT], 4 * (c % 2),
                               8, BUF[:, 0:2048])
            los("lru_out", range(4, 8))
            for c in range(1, 4):
                los("lru_out", range(8 * c, 8 * c + 4))
                lru_residual(c - 1)
                los("lru_out", range(8 * c + 4, 8 * c + 8))
            los("att_in", range(0, 4))
            lru_residual(3)

            mean_square(7, [(2, D)])
            rstd(7, 2)
            normalized(CN, CX, 7)
            mean_square(8, [(2, D)])
            rstd(8, 2)
            normalized(XN, X, 8)
            split_features(part(FTH, 0), part(FTL, 0), TMP_B)
            split_features(part(FTH, 1), part(FTL, 1), TMP_B)
            axial = const("axial").rearrange("p (t z a y f) -> p t z a y f", t=TT, z=2, a=2, y=2)
            PER_HEADS, PER_TAIL, PER_PREP = 8 * 3, 5, 12

            def linker(s, i, per):
                done = [0]

                def link(ins):
                    done[0] += 1
                    ins.then_inc(s, 1)
                    dve.wait_ge(s, i * per + done[0])
                return link, done

            def att_lo(i, units):
                for u in units:
                    lo(UNIT0["att_in"] + 32 + u if not isinstance(i, int) else UNIT0["att_in"] + 32 * (i + 1) + u, UNIT,
                       None if isinstance(i, int) else i, 32)

            def maxima(i, s):
                dve.wait_ge(s_e3, i * 8 + (s + 1))
                dve.tensor_reduce(NM[:, s % 2, :], PS[:, 4:6, :], AX, ALU.max, negate=True).then_inc(s_e4, 1)

            def combine(i, s, link):
                a = s % 2
                dve.wait_ge(s_e5, i * 8 + (s + 1))
                link(dve.reciprocal(RL[:, a, :], LS[:, a, :]))
                link(dve.tensor_tensor(out=RL[:, a, 1:2], in0=RL[:, a, 1:2], in1=NLAM, op=ALU.mult))
                link(dve.tensor_scalar(DE[:, a, 1, :], DE[:, a, 1, :], RL[:, a, 1:2], None, ALU.mult))
                dve.scalar_tensor_tensor(out=DE[:, a, 0, :], in0=DE[:, a, 0, :], scalar=RL[:, a, 0:1], in1=DE[:, a, 1, :],
                                         op0=ALU.mult, op1=ALU.add).then_inc(s_e8, 1)

            def output(i, s):
                dve.wait_ge(s_e11, i * 8 + (s + 1))
                dve.tensor_copy(OS[:, s % 2, s // 2 * P:(s // 2 + 1) * P], PS[:, 7, 0:P]).then_inc(s_oe, 1)

            oflat = OS[:].rearrange("p t c -> p (t c)")
            oh = oflat.rearrange("p (g c) -> p g c", c=P)

            def outputs_square(i, link):
                dve.wait_ge(s_oe, i * 8 + 8)
                link(dve.tensor_tensor(out=DSQ[:, 0:1024], in0=oflat, in1=oflat, op=ALU.mult))
                link(dve.tensor_reduce(DS8, DSQ[:, 0:1024].rearrange("p (g c) -> p g c", c=P), AX, ALU.add))
                dve.tensor_scalar(DS8, DS8, 1.0 / P, EPS, ALU.mult, ALU.add).then_inc(s_om, 1)

            def outputs_gate(i, link):
                dve.wait_ge(s_or, i + 1)
                link(dve.reciprocal(DS8, DS8))
                link(dve.tensor_tensor(out=oh, in0=oh, in1=DS8.unsqueeze(2).to_broadcast([P, 8, P]), op=ALU.mult))
                link(dve.tensor_tensor(out=oh, in0=oh, in1=SUBG.unsqueeze(1).to_broadcast([P, 8, P]), op=ALU.mult))
                dve.tensor_tensor(out=oflat, in0=oflat, in1=RG[:].rearrange("p t c -> p (t c)"), op=ALU.mult).then_inc(s_oy, 1)

            flat = RQK[:].rearrange("p t c -> p (t c)")
            by64 = flat.rearrange("p (g c) -> p g c", c=ATT_DH)

            def qk_square(i, link):
                dve.wait_ge(s_dqe, i * 4 + 6)
                link(dve.tensor_tensor(out=DSQ, in0=flat, in1=flat, op=ALU.mult))
                link(dve.tensor_reduce(DS48, DSQ.rearrange("p (g c) -> p g c", c=ATT_DH), AX, ALU.add))
                dve.tensor_scalar(DS48, DS48, 1.0 / ATT_DH, EPS, ALU.mult, ALU.add).then_inc(s_dm, 1)

            def qk_normalize(i, link):
                dve.wait_ge(s_dp0, i + 2)
                link(dve.reciprocal(DS48, DS48))
                link(dve.tensor_tensor(out=by64, in0=by64, in1=DS48.unsqueeze(2).to_broadcast([P, 48, ATT_DH]), op=ALU.mult))

            def qk_gain(link):
                dve.tensor_tensor(out=by64[:, 0:32, :], in0=by64[:, 0:32, :], in1=KG.unsqueeze(1).to_broadcast([P, 32, ATT_DH]), op=ALU.mult)
                link(dve.tensor_tensor(out=by64[:, 32:48, :], in0=by64[:, 32:48, :], in1=QG.unsqueeze(1).to_broadcast([P, 16, ATT_DH]), op=ALU.mult))

            def qk_rotate(tile, link):
                x = RQK[:, tile, :]
                cos = axial[:, tile % 2, 0].rearrange("p a y f -> p (a y f)").unsqueeze(1).to_broadcast([P, 8, ATT_DH])
                parts = lambda v: v.rearrange("p (h a y f) -> p h a y f", h=8, a=2, y=2)
                dve.tensor_tensor(out=DT1.rearrange("p (h c) -> p h c", h=8), in0=x.rearrange("p (h c) -> p h c", h=8), in1=cos, op=ALU.mult)
                for y in range(2):
                    sin = axial[:, tile % 2, 1, :, y, :].unsqueeze(1).to_broadcast([P, 8, 2, 16])
                    ins = dve.tensor_tensor(out=parts(DT2)[:, :, :, y, :], in0=parts(x)[:, :, :, 1 - y, :], in1=sin, op=ALU.mult)
                link(ins)
                ins = dve.tensor_tensor(out=x, in0=DT1, in1=DT2, op=ALU.add)
                if tile < 5:
                    link(ins)
                else:
                    ins.then_inc(s_qn, 1)

            def projections_behind(i, heads):
                att_lo(i, [20])
                if heads:
                    link, done = linker(s_tstep, i, PER_TAIL)
                    outputs_square(i, link)
                att_lo(i, [21])
                if heads:
                    outputs_gate(i, link)
                    assert done[0] == PER_TAIL
                att_lo(i, [22])
                link, done = linker(s_pstep, i + 1, PER_PREP)
                qk_square(i, link)
                att_lo(i, [23])
                qk_normalize(i, link)
                att_lo(i, [24])
                qk_gain(link)
                att_lo(i, [25])
                qk_rotate(2, link)
                qk_rotate(3, link)
                att_lo(i, [26])
                qk_rotate(4, link)
                att_lo(i, [27])
                qk_rotate(5, link)
                assert done[0] == PER_PREP
                att_lo(i, range(28, 36))

            att_lo(-1, range(4, 20))
            projections_behind(-1, False)
            with dve.Fori(0, GROUPS - 1) as i:
                link, done = linker(s_dstep, i, PER_HEADS)
                maxima(i, 0)
                combine(i, 0, link)
                for s in range(8):
                    att_lo(i, [2 * s + 4])
                    if s < 7:
                        maxima(i, s + 1)
                        combine(i, s + 1, link)
                    att_lo(i, [2 * s + 5])
                    output(i, s)
                assert done[0] == PER_HEADS
                projections_behind(i, True)

            last = GROUPS - 1
            link, done = linker(s_dstep, last, PER_HEADS)
            maxima(last, 0)
            combine(last, 0, link)
            y_lo(0, 2, DYH, DYL, DYT, KT)
            for s in range(8):
                if s < OUT_AHEAD:
                    los("att_out", [s + 4])
                if s < 7:
                    maxima(last, s + 1)
                    combine(last, s + 1, link)
                if s < OUT_AHEAD - 1:
                    y_lo(2 * s + 2, 2, DYH, DYL, DYT, KT)
                output(last, s)
                if s == 2:
                    dve.wait_ge(s_e2, 4 * GROUPS)
                if 2 <= s < 6:
                    gate_diagonals(8 + s - 2, 1, 0)
            link, done = linker(s_tstep, last, PER_TAIL)
            outputs_square(last, link)
            outputs_gate(last, link)
            y_lo(2 * OUT_AHEAD, KT - 2 * OUT_AHEAD, DYH, DYL, DYT, KT)

            def att_residual(c):
                gated_residual("att_out", c, [X[:, 0, :], X[:, 1, :]], [G_ATT, G_ATT], 2 * (c % 2), 12, BUF[:, 13312:14336])
            los("att_out", range(OUT_AHEAD + 4, 12))
            att_residual(0)
            los("att_out", range(12, 16))
            for c in range(2, 4):
                los("att_out", range(8 * c, 8 * c + 4))
                att_residual(c - 1)
                los("att_out", range(8 * c + 4, 8 * c + 8))
            att_residual(3)

        @block.gpsimd
        def _(pool):
            def stage_heads(h):
                H = HE if h in EV_LOOPS else HO
                wq = NOPE + ROPE if h.kind == "mla" else P
                wk = NOPE + MLA_DV if h.kind == "mla" else P
                with pool.Fori(0, h.turns) as i:
                    pair = h.kind == "swa"
                    for a in range(1 if pair else 2):
                        pool.wait_ge(s_t1, i * 2 + (h.n0 + (1 if pair else a) + 1))
                        q = H[:, :, bass.ds(i * (P if pair else 2 * wq) + (h.q + a * wq), wq)]
                        pool.tensor_copy(QS[:, a, :, 0:wq], q)
                        if pair:
                            for z in range(2):
                                ins = pool.tensor_copy(KS[:, a, :, 64 * z:64 * z + 64], H[:, :, h.k:h.k + SWA_DH])
                        elif h.mem is not None:
                            ins = pool.tensor_copy(KS[:, a, :, :], MKV[:, h.mem, :, bass.ds(i * 256 + (h.k + a * P), P)])
                        else:
                            ins = pool.tensor_copy(KS[:, a, :, :], H[:, :, bass.ds(i * (2 * wk) + (h.k + a * wk), P)])
                        ins.then_inc(s_stg, 2 if pair else 1)
                    for u in range(8):
                        if LO_BY[UNIT0["mod_" + h.name] + u][0]:
                            weights_lo(UNIT0["mod_" + h.name] + u, i)

            def weights_lo(U, i=None):
                pool.wait_ge(s_hi, at(U + 1, i, 8))
                pool.tensor_tensor(out=WL[:, U % SLOTS, :], in0=RA[:, U % SLOTS, :], in1=WH[:, U % SLOTS, :].bitcast(F32),
                                   op=ALU.subtract).then_inc(s_lop, 1)

            pool.wait_ge(s_ge, CHUNK0["uq"])
            pool.wait_ge(s_kpt, 1)
            pool.wait_ge(s_ms, 3)
            stage_heads(MEM_EV)
            pool.wait_ge(s_rope, 2)
            stage_heads(MOBA)
            pool.wait_ge(s_ge, CHUNK0["od_b"])
            pool.wait_ge(s_rope, 3)
            stage_heads(MLA)
            pool.wait_ge(s_ge, CHUNK0["od_c"] + 1)
            pool.wait_ge(s_rope, 5)
            for h in OD_LOOPS:
                stage_heads(h)

            def block_vectors(b, n):
                pool.tensor_copy(BV[:, b, :], LTAB[:, n, :] if isinstance(n, int) else LTAB[:, bass.ds(n, 1), :].squeeze(1)).then_inc(s_bv, 1)

            def lru_ix(b, i=None):
                pool.wait_ge(s_sg, at(b + 2, i, 2))
                for d in range(2):
                    ins = pool.tensor_tensor(out=RI[:, 2 * d + 1, :], in0=RI[:, 2 * d + 1, :],
                                             in1=XC[:, b % 2, :, :].rearrange("p c s -> p (c s)"), op=ALU.mult)
                ins.then_inc(s_ix, 1)

            pool.wait_ge(s_ltab, 1)
            for b in range(2):
                block_vectors(b, b)
            for b in range(2):
                for u in range(4):
                    weights_lo(UNIT0["lru_in"] + 4 * b + u)
            with pool.Fori(0, KT // 2 - 1) as i:
                for b in range(2):
                    lru_ix(b, i)
                    for u in range(4):
                        weights_lo(UNIT0["lru_in"] + 4 * b + 8 + u, i)
                    pool.wait_ge(s_y, i * 2 + (b + 3))
                    block_vectors(b, i * 2 + (b + 2))
            lru_ix(KT - 2)
            lru_ix(KT - 1)


_INS = ("x", "mem", "ev_norm_g", "ev_w_in", "ev_q_norm_g", "ev_w_uq", "ev_kv_norm_g", "ev_w_ukv", "ev_mem_norm_g",
        "ev_w_mem_kv", "ev_w_out", "od_norm_g", "od_w_in", "od_sinks", "od_mem_norm_g", "od_w_mem_kv", "od_w_out",
        "final_norm_g", "c_2", "ctx_2", "c_ctx_2", "mod_w_2", "mod_b_2", "norm_g_2", "lru_w_in_2", "lru_conv_w_2",
        "lru_conv_b_2", "lru_gate_w_2", "lru_gate_b_2", "lru_lambda_2", "lru_w_out_2", "att_w_in_2", "att_q_norm_2",
        "att_k_norm_2", "att_lambda_2", "att_subln_2", "att_w_out_2")


def kernel(**inputs):
    import concourse.bacc as bacc
    from concourse.bass_utils import run_bass_kernel_spmd

    nc = bacc.Bacc("TRN2", target_bir_lowering=False, num_devices=1)
    arrays, args = {}, {}
    for name in _INS:
        a = np.ascontiguousarray(inputs[name])
        arrays[f"in_{name}"] = a
        args[name] = nc.dram_tensor(f"in_{name}", a.shape, mybir.dt.from_np(a.dtype), kind="ExternalInput").ap()
    arrays["shape_constants"] = shape_constants()
    consts = nc.dram_tensor("shape_constants", (P, NCONST), F32, kind="ExternalInput").ap()
    out = nc.dram_tensor("out", (1, SEQ, D), F32, kind="ExternalOutput").ap()
    build(nc, args, consts, out)
    return run_bass_kernel_spmd(nc, [arrays], core_ids=[0]).results[0]["out"]
```

```python
import math
from contextlib import ExitStack

import numpy as np

import concourse.bass as bass
from concourse import mybir

F32 = mybir.dt.float32
F32R = mybir.dt.float32r
ACT = mybir.ActivationFunctionType
ALU = mybir.AluOpType
AX = mybir.AxisListType.X

P = 128
SEQ = 256
D = 2048
KT = D // P
TT = SEQ // P
EPS = 1e-6
NEG = -1e30

MLA_HEADS, MLA_QR, MLA_KVR, NOPE, ROPE, MLA_DV = 8, 512, 256, 128, 64, 128
MOBA_HEADS, DH = 8, 128
MEM_HEADS = 4
MEMW = MEM_HEADS * DH
EV_VW = MLA_HEADS * MLA_DV + MOBA_HEADS * DH + MEMW
EV_CKV = MLA_QR
EV_KPE = EV_CKV + MLA_KVR
EV_LAT = EV_KPE + ROPE
EV_QKV = 0
EV_QM = EV_QKV + 3 * MOBA_HEADS * DH
EV_GATE = EV_QM + MEMW
EV_W = EV_GATE + EV_VW
SWA_HEADS, SWA_KV, SWA_DH, SWA_WINDOW = 16, 2, 64, 128
DIL_HEADS = 6
DIL_PATTERNS = ((128, 1), (512, 4), (2048, 16))
OD_KC = SWA_HEADS * SWA_DH
OD_VC = OD_KC + SWA_KV * SWA_DH
OD_QD = OD_VC + SWA_KV * SWA_DH
OD_KD = OD_QD + DIL_HEADS * DH
OD_VD = OD_KD + DIL_HEADS * DH
OD_QM = OD_VD + DIL_HEADS * DH
OD_GATE = OD_QM + MEMW
OD_VW = SWA_HEADS * SWA_DH + DIL_HEADS * DH + MEMW
OD_IN = OD_GATE + OD_VW
EV_QA = EV_QKV
EV_KVA = EV_QA + MLA_HEADS * (NOPE + ROPE)
ATT_HEADS, ATT_DH = 16, 64
GROUPS = 4
LRU_C = 8.0
LAM_INIT = 0.8 - 0.6 * math.exp(-0.3 * 1)

CHUNK = 512
SLOTS = 4
UNIT = 2 * CHUNK

CONSTS = {}


def _lay_consts():
    at = 0
    for name, width in (("ident", P), ("axial", TT * 2 * 64), ("mla", TT * 4 * 32), ("r32", TT * 4 * 16),
                        ("r16", TT * 4 * 8), ("causal", 2 * SEQ), ("swa", 2 * SEQ), ("dil", 2 * SEQ)):
        CONSTS[name] = (at, width)
        at += width
    return at


NCONST = _lay_consts()
NCONST_ALL = CONSTS["mla"][0]


def shape_constants():
    out = np.zeros((P, NCONST), np.float32)

    def put(name, a):
        at, width = CONSTS[name]
        out[:, at:at + width] = a.reshape(P, width)

    put("ident", np.eye(P, dtype=np.float32))
    pos = np.arange(SEQ, dtype=np.float32)
    for name, rot in (("mla", ROPE), ("r32", DH // 4), ("r16", SWA_DH // 4)):
        inv = (1.0 / (np.float32(500000.0) ** (np.arange(0, rot, 2, dtype=np.float32) / np.float32(rot)))).astype(np.float32)
        ang = (pos[:, None] * inv[None]).astype(np.float32)
        c, s = np.cos(ang), np.sin(ang)
        table = np.stack([np.concatenate([c, c], 1), np.concatenate([-s, s], 1)], 1)
        put(name, table.reshape(TT, P, 2 * rot).transpose(1, 0, 2))
    nf = ATT_DH // 4
    inv = (np.float32(10000.0) ** (-np.arange(nf, dtype=np.float32) / np.float32(nf))).astype(np.float32)
    t = np.arange(SEQ)
    ang = np.stack([(t // 64).astype(np.float32)[:, None] * inv, (t % 64).astype(np.float32)[:, None] * inv], 1)
    c, s = np.cos(ang).astype(np.float32), np.sin(ang).astype(np.float32)
    table = np.stack([np.stack([c, c], 2).reshape(SEQ, 64), np.stack([-s, s], 2).reshape(SEQ, 64)], 1)
    put("axial", table.reshape(TT, P, 128).transpose(1, 0, 2))
    q, k = np.arange(SEQ)[:, None], np.arange(SEQ)[None]
    dist = q - k

    def mask(times):
        bias = np.where(times > 0, np.log(np.maximum(times, 1).astype(np.float64)), NEG).astype(np.float32)
        return bias.reshape(TT, P, SEQ).transpose(1, 0, 2)

    put("causal", mask((dist >= 0).astype(int)))
    put("swa", mask(((dist >= 0) & (dist <= SWA_WINDOW - 1)).astype(int)))
    put("dil", mask(sum(((dist >= 0) & (dist % dil == 0) & (dist // dil <= window // dil)).astype(int)
                        for window, dil in DIL_PATTERNS)))
    return out


VECTORS = (
    (("ev_norm_g", 0, 16), ("ev_mem_norm_g", 0, 16), ("od_norm_g", 0, 16), ("od_mem_norm_g", 0, 16),
     ("c_2", 0, 16), ("c_ctx_2", None, 16), ("ev_q_norm_g", 0, 4), ("ev_kv_norm_g", 0, 2)),
    (("norm_g_2", None, 32), ("lru_lambda_2", 0, 32), ("lru_conv_b_2", 0, 16)),
    (("lru_conv_w_2", 0, 64), ("lru_gate_b_2", 0, 64)),
    (("mod_b_2", None, 96),),
)
VEC_ROWS = [sum(n for _, _, n in tile) for tile in VECTORS]
VEC_COL = [sum(VEC_ROWS[:t]) for t in range(len(VECTORS) + 1)]
VEC_AT = {}
for _t, _tile in enumerate(VECTORS):
    _row = 0
    for _name, _, _n in _tile:
        VEC_AT[_name] = VEC_COL[_t] + _row
        _row += _n

STAGES = (("mkv0", 16), ("mkv1", 16), ("ev_a", 16), ("ev_b", 96), ("mod_mem_ev", 16), ("mod_moba", 32), ("uq", 6), ("ukv", 4),
          ("mod_mla", 32), ("ev_out", 40), ("od_b", 96), ("od_c", 16), ("mod_swa0", 32), ("mod_swa1", 32), ("mod_dil", 24),
          ("mod_mem_od", 16), ("od_out", 36), ("lru_in", 64), ("lru_out", 32), ("att_in", 128), ("att_out", 32))
UNIT0 = {}
LO_BY = []


def by_gpsimd(stage, u):
    return stage == "lru_in" or (stage.startswith("mod_") and u % 8 in (4, 6))


_made = [0, 0]
for _name, _n in STAGES:
    UNIT0[_name] = len(LO_BY)
    for _u in range(_n):
        _pool = by_gpsimd(_name, _u)
        LO_BY.append((_pool, _made[_pool]))
        _made[_pool] += 1
CHUNK_UNITS = {name: 8 for name, _ in STAGES} | {"uq": 2, "ukv": 1, "od_c": 16, "ev_out": 10, "od_out": 9}


def multiplied(stage, c):
    return UNIT0[stage] + (c + 1) * CHUNK_UNITS[stage]


CHUNK0 = {"mkv0": 0, "mkv1": 2, "ev_a": 4, "ev_b": 6, "uq": 18, "ukv": 21, "od_b": 25, "od_c": 37}
RES0 = {"ev_out": 0, "od_out": 4, "lru_out": 8, "att_out": 13}


class Heads:

    def __init__(self, name, n0, turns, kind, q, k, v, gate, y0, mask, scale, mod_layer, mod_chunk0, mod0, mem=None, sink=None):
        self.name, self.n0, self.turns, self.kind = name, n0, turns, kind
        self.q, self.k, self.v, self.gate, self.y0 = q, k, v, gate, y0
        self.mask, self.scale = mask, scale
        self.mod_layer, self.mod_chunk0, self.mod0 = mod_layer, mod_chunk0, mod0
        self.mem, self.sink = mem, sink


EV_Y_B = MLA_HEADS
EV_Y_M = MLA_HEADS + MOBA_HEADS
OD_Y_D = SWA_HEADS * SWA_DH // P
OD_Y_M = OD_Y_D + DIL_HEADS
SC128, SC64 = DH ** -0.5, SWA_DH ** -0.5
MEM_EV = Heads("mem_ev", 0, 2, "plain", EV_QM, 0, MEMW, EV_GATE + EV_Y_M * P, EV_Y_M, None, SC128, 0, 0, 0, mem=0)
MOBA = Heads("moba", 4, 4, "plain", EV_QKV, EV_QKV + 1024, EV_QKV + 2048, EV_GATE + EV_Y_B * P, EV_Y_B, "causal", SC128, 0, 2, 2)
MLA = Heads("mla", 12, 4, "mla", EV_QA, EV_KVA, EV_KVA + NOPE, EV_GATE, 0, "causal", (NOPE + ROPE) ** -0.5, 0, 6, 6)
SWA = [Heads(f"swa{j}", 20 + 8 * j, 4, "swa", 512 * j, OD_KC + 64 * j, OD_VC + 64 * j, OD_GATE + 512 * j, 4 * j, "swa", SC64,
             1, 4 * j, 11 + 4 * j, sink=8 * j) for j in range(2)]
DIL = Heads("dil", 36, 3, "plain", OD_QD, OD_KD, OD_VD, OD_GATE + OD_Y_D * P, OD_Y_D, "dil", SC128, 1, 8, 19)
MEM_OD = Heads("mem_od", 42, 2, "plain", OD_QM, 0, MEMW, OD_GATE + OD_Y_M * P, OD_Y_M, None, SC128, 0, 10, 22, mem=1)
EV_LOOPS = (MEM_EV, MOBA, MLA)
OD_LOOPS = (*SWA, DIL, MEM_OD)
N_HEADS = 46
MOD_ALONE = 10
N_MOD = 24


def build(nc, t, consts, out):
    ctx = ExitStack()
    with ctx:
        def sb(name, shape, dtype=F32, owner=ctx):
            return owner.enter_context(nc.sbuf_tensor(name, shape, dtype))

        def sem(name):
            return ctx.enter_context(nc.semaphore(name))

        PS = ctx.enter_context(nc.psum_tensor("ps", [P, 8, CHUNK], F32))
        X = sb("x_res", [P, TT, D])
        CST = sb("consts", [P, NCONST_ALL])
        GT = sb("vectors_t", [P, VEC_COL[-1]])
        CS = sb("cond_t", [P, 4 * KT + P], F32R)
        MODT = sb("mod_t", [P, 2, 48, 2])
        BC = sb("bcast", [P, 272])
        ST = sb("stats", [P, 9, 4])
        HS = sb("head_stats", [P, 2, 16])
        SC = sb("scalars", [P, 512])
        RA = sb("ring", [P, SLOTS, UNIT])
        WH = sb("ring_hi", [P, SLOTS, UNIT], F32R)
        WL = sb("ring_lo", [P, SLOTS, UNIT], F32R)
        with ExitStack() as first:
            MKVB = sb("mem_kv", [P, 2 * TT * 2 * MEMW], owner=first)
            with ExitStack() as start:
                MEMB = sb("mem_rows", [P, TT * D], owner=start)
                M1H = sb("mem_hi", [P, KT * SEQ], F32R, owner=start)
                M1L = sb("mem_lo", [P, KT * SEQ], F32R, owner=start)
                GRB = sb("vector_rows", [P, 4 * P], owner=start)
            HB = sb("proj", [P, 12800], owner=first)
            ATH = sb("act_hi", [P, 20 * SEQ], F32R, owner=first)
            ATL = sb("act_lo", [P, 20 * SEQ], F32R, owner=first)
            AR = sb("arena", [P, 5632], owner=first)
            CSTA = sb("consts_first", [P, NCONST - NCONST_ALL], owner=first)
        BUF = sb("second_block", [P, 17536])
        FTH = sb("features_hi", [P, KT, 2 * SEQ], F32R)
        FTL = sb("features_lo", [P, KT, 2 * SEQ], F32R)

        def const(name):
            at, width = CONSTS[name]
            if at < NCONST_ALL:
                return CST[:, at:at + width]
            return CSTA[:, at - NCONST_ALL:at - NCONST_ALL + width]

        def vec(name, k=0, n=1):
            return GT[:, VEC_AT[name] + k:VEC_AT[name] + k + n]

        def at(v, i=None, per=0):
            return v if i is None else i * per + v

        def carve(buf, first, parts):
            views = []
            for n in parts:
                views.append(buf[:, first:first + n])
                first += n
            return views

        ident = const("ident")
        SUBG, QG, KG, SINK = BC[:, 0:128], BC[:, 128:192], BC[:, 192:256], BC[:, 256:272]

        MKV = MKVB[:].rearrange("p (l t c) -> p l t c", l=2, t=TT)
        HE = HB[:, 0:TT * EV_W].rearrange("p (t c) -> p t c", c=EV_W)
        HO = HB[:, 0:TT * OD_IN].rearrange("p (t c) -> p t c", c=OD_IN)
        MEMX = MEMB[:].rearrange("p (t d) -> p t d", t=TT)
        GR = GRB[:].rearrange("p (v c) -> p v c", c=P)
        HQ = AR[:, 0:TT * EV_LAT].rearrange("p (t c) -> p t c", c=EV_LAT)
        LV, LVP = AR[:, 2048:2304], AR[:, 2304:2432]
        COND = AR[:, 2432:2464].rearrange("p (k v) -> p k v", v=2)
        CSV = CS[:, 0:4 * KT].rearrange("p (k v) -> p k v", v=4)
        JUNK_A = AR[:, 3072:3072 + D]
        TMP_X = AR[:, 0:2048].rearrange("p (j c) -> p j c", j=4)
        JUNK_LAT = AR[:, 1664:2176]
        TMP_LAT = AR[:, 3072:5120].rearrange("p (j c) -> p j c", j=4)

        a_qs, a_ks, a_qkt, a_qrt, KPT, a_s, a_pt, a_ys = carve(AR, 0, (768, 512, 1024, 512, 256, 1024, 1024, 512))
        QS = a_qs.rearrange("p (a t c) -> p a t c", a=2, t=TT)
        KS = a_ks.rearrange("p (a t c) -> p a t c", a=2, t=TT)
        QKT = a_qkt.rearrange("p (a c) -> p a c", a=2)
        QRT = a_qrt.rearrange("p (a c) -> p a c", a=2)
        S = a_s.rearrange("p (a t c) -> p a t c", a=2, t=TT)
        PT = a_pt.rearrange("p (a c) -> p a c", a=2)
        YS = a_ys.rearrange("p (a t c) -> p a t c", a=2, t=TT)
        ROT_A, ROT_B = AR[:, 4608:5120], AR[:, 5120:5632]
        MODS_EV, MODS_OD = HB[:, TT * EV_W:TT * EV_W + CHUNK], a_qrt
        NM, LS, RL, ES, SN = (HS[:, :, j:j + 2] for j in (0, 2, 4, 6, 8))

        XN, CN, CX = (BUF[:, j * TT * D:(j + 1) * TT * D].rearrange("p (t d) -> p t d", t=TT) for j in range(3))
        FG = BUF[:, 12288:12288 + D]
        TMP_B = BUF[:, 14336:16384].rearrange("p (j c) -> p j c", j=4)
        YL = BUF[:, 0:KT * 2 * SEQ].rearrange("p (k s) -> p k s", s=2 * SEQ)
        l_xc, l_gw, l_ri, SG, l_hs, LAF, LWF = carve(BUF, 8192, (1024, 1024, 2048, 512, 1024, 1024, 1024))
        XC = l_xc.rearrange("p (b c s) -> p b c s", b=2, c=2)
        GW = l_gw.rearrange("p (b j d) -> p b j d", b=2, j=4)
        RI = l_ri.rearrange("p (j s) -> p j s", j=4)
        HSC = l_hs.rearrange("p (d s) -> p d s", d=2)
        LTMP = l_hs
        LA = LAF.rearrange("p (d s) -> p d s", d=2)
        LW = LWF.rearrange("p (d s) -> p d s", d=2)
        LTAB = SC[:, 164:164 + 18 * 12].rearrange("p (k j) -> p k j", j=12)
        BV = SC[:, 380:404].rearrange("p (b j) -> p b j", b=2)
        NSINK = SC[:, 404:436].rearrange("p (h t) -> p h t", t=TT)
        NLAM = SC[:, 436:437]
        SQX, SQL, SQC = (SC[:, j:j + 8].rearrange("p (t c) -> p t c", t=TT) for j in (72, 56, 64))
        MSC = SC[:, 440:504]
        G_LAT, G_CTX, G_ATT = BUF[:, 12288:14336], BUF[:, 14336:16384], BUF[:, 0:D]
        ONES = BUF[:, 17408:17536]

        def DIAG(j):
            first = (16384 if j < 8 else D) + (j % 2) * 512
            return BUF[:, first:first + 512].rearrange("p (k d) -> p k d", k=4)

        d_qk, d_v, d_g, d_y, d_qkt, d_e, d_pt, d_os = carve(BUF, 0, (3072, 2048, 1024, 4096, 3072, 2048, 1024, 1024))
        RQK = d_qk.rearrange("p (t c) -> p t c", t=6)
        RV = d_v.rearrange("p (t c) -> p t c", t=4)
        RG = d_g.rearrange("p (t c) -> p t c", t=2)
        DYT = d_y.rearrange("p (k s) -> p k s", s=SEQ)
        DQK = d_qkt.rearrange("p (h c) -> p h c", h=4)
        DE = d_e.rearrange("p (a c s) -> p a c s", a=2, c=2)
        DPT = d_pt.rearrange("p (a c) -> p a c", a=2)
        OS = d_os.rearrange("p (t c) -> p t c", t=TT)
        DSQ = BUF[:, 13312:16384]
        DT1, DT2 = d_qkt[:, 0:512], d_qkt[:, 512:1024]
        DS48, DS8 = SC[:, 0:48], SC[:, 48:56]
        DYH, DYL = FTH[:, :, 0:SEQ], FTL[:, :, 0:SEQ]

        s_const, s_consta, s_rows, s_mem, s_x, s_bc, s_ctx, s_fg, s_cx2, s_out = map(sem, (
            "const_loaded", "first_const_loaded", "vector_rows_loaded", "mem_loaded", "x_loaded", "bcast_loaded",
            "ctx_loaded", "final_g_loaded", "ctx_loaded_again", "out_stored"))
        s_w = [sem(f"weights_landed{j}") for j in range(SLOTS)]
        s_hi, s_lo, s_lop, s_wused = map(sem, ("weights_hi", "weights_lo_by_vector", "weights_lo_by_gpsimd", "weight_units_used"))
        s_vt, s_vec, s_cond, s_cs = map(sem, ("vectors_transposed", "vectors_ready", "cond_hi", "cond_ready"))
        s_sq, s_sqc, s_ms, s_rt, s_rs = map(sem, ("squares_summed", "chunk_squares_summed", "mean_square", "root_taken", "rstd_ready"))
        s_xn, s_xt, s_tmp, s_xh, s_xl = map(sem, ("rows_normalized", "rows_transposed", "features_scaled", "features_hi", "features_lo"))
        s_ge, s_rh, s_re = map(sem, ("chunk_evicted", "residual_gated", "residual_added"))
        s_rope, s_kpe, s_kpt = map(sem, ("rope_done", "kpe_transposed", "kpe_ready"))
        s_stg, s_t1, s_qk, s_sc, s_sm, s_mx, s_ex, s_pt, s_pe, s_o, s_rl, s_ys, s_yt, s_yh, s_ye = map(sem, (
            "head_staged", "head_qk_transposed", "head_qk_ready", "head_scores", "head_masked", "head_max",
            "head_exp", "head_p_transposed", "head_p_ready", "head_out", "head_recip", "head_y", "head_y_transposed",
            "head_y_hi", "head_y_lo"))
        s_sk, s_sk2, s_l2 = map(sem, ("sink_shifted", "sink_max", "sink_added"))
        s_mods, s_modt, s_modb, s_modd, s_msc = map(sem, ("mod_rows_ready", "mod_transposed", "mod_biased", "mod_ready", "mod_scale_ready"))
        s_dve = sem("vector_step")
        s_lam, s_exl, s_ltab, s_xf = map(sem, ("lru_decay_ready", "lru_exp_ready", "lru_table_ready", "x_final"))
        SQUARED = np.cumsum([2, 2, 4, 2, 2, 0, 2]).tolist()
        s_gw = [sem(f"gate_weights_landed{b}") for b in range(2)]
        s_cv, s_xc, s_gt, s_sg, s_gs, s_ab, s_w2a, s_w2, s_sqr, s_ix, s_b, s_sn, s_hsum, s_y, s_bv = map(sem, (
            "lru_conv_tap", "lru_conv", "lru_gates", "lru_sigmoids", "lru_silu", "lru_a", "lru_a2", "lru_1ma2", "lru_sqrt",
            "lru_ix", "lru_b", "lru_scan", "lru_sum", "lru_y", "lru_block_vectors"))
        s_yhi, s_ylo = map(sem, ("y_hi", "y_lo"))
        s_dg, s_gb, s_gbe = map(sem, ("gate_diag", "gate_bcast", "gate_bcast_ready"))
        s_dqe, s_dstep, s_tstep, s_pstep, s_dm, s_dp0, s_qn = map(sem, (
            "diff_chunk_evicted", "diff_head_step", "diff_tail_step", "diff_prep_step", "diff_qk_ms", "diff_qk_root", "diff_qk_normal"))
        s_e1, s_e2, s_e3, s_e4, s_e5, s_e8, s_e9, s_e10, s_e11, s_oe = map(sem, (
            "diff_qk_transposed", "diff_qk_ready", "diff_scores", "diff_max", "diff_exp", "diff_weights",
            "diff_w_transposed", "diff_w_ready", "diff_o", "diff_o_ready"))
        s_om, s_or, s_oy, s_dyt, s_dye = map(sem, ("diff_o_ms", "diff_o_root", "diff_y", "diff_y_transposed", "diff_y_ready"))

        N_CONST_BC = 5
        S_ROWS = 16 * sum(len(tile) for tile in VECTORS)
        OUT_AHEAD = 6
        OUT_UNITS = ([(c, u) for c in range(2) for u in range(OUT_AHEAD)] + [(c, u) for c in range(2) for u in range(OUT_AHEAD, 8)]
                     + [(c, u) for c in range(2, 4) for u in range(8)])
        OUT_DONE = [max(j for j, unit in enumerate(OUT_UNITS) if unit[0] == c) + 1 for c in range(4)]
        OUT_FILL = ((0, 1), (2,), (3, 4), (5,), (6, 7), (8,), (9, 10), (11,))
        block = ctx.enter_context(nc.Block())

        def landed(U, i=None, per=0):
            return at(16 * (U // SLOTS + 1), i, 16 * per // SLOTS)

        def lo_made(U, i=None, per=0, turns=0):
            pool, before = LO_BY[U]
            stage0 = max(u0 for u0 in UNIT0.values() if u0 <= U)
            a_turn = sum(LO_BY[u][0] == pool for u in range(stage0, stage0 + per))
            return s_lop if pool else s_lo, at(before + 1 - turns * a_turn, i, a_turn)

        @block.sync
        def _(sp):
            sp.dma_start(CST[:], consts[:, 0:NCONST_ALL]).then_inc(s_const, 16)
            sp.dma_start(MEMX, t["mem"].rearrange("b (t p) d -> p (b t) d", p=P)).then_inc(s_mem, 16)
            for v, tile in enumerate(VECTORS):
                row = 0
                for name, layer, n in tile:
                    src = t[name] if layer is None else t[name][layer]
                    while len(src.shape) > 1:
                        src = src.rearrange("a b -> (a b)") if len(src.shape) == 2 else src.rearrange("a b c -> (a b) c") \
                            if len(src.shape) == 3 else src.rearrange("a b c d -> (a b) c d")
                    sp.dma_start(GR[row:row + n, v, :], src.rearrange("(r c) -> r c", c=P)).then_inc(s_rows, 16)
                    row += n

            def unit(U, w, k0, nk, col, n, i=None, per=0):
                dst = RA[:, U % SLOTS, 0:nk * n].rearrange("p (k n) -> p k n", k=nk)
                cols = col if i is None else sp.snap(col)
                if U + per >= SLOTS:
                    sp.wait_ge(*lo_made(U + per - SLOTS, i, per, 1 if per else 0))
                src = w.rearrange("(k p) n -> p k n", p=P)[:, k0:k0 + nk, bass.ds(cols, n)]
                sp.dma_start(dst, src).then_inc(s_w[U % SLOTS], 16)

            def chunks(stage, w, col0, count, n=CHUNK, kt=KT, behind=None):
                per = -(-kt // 2)
                for c in range(count):
                    for u in range(per):
                        unit(UNIT0[stage] + c * per + u, w, u * 2, min(2, kt - u * 2), col0 + c * CHUNK, n)
                        if behind is not None and c * per + u == SLOTS - 1:
                            behind()

            def chunk_loop(stage, w, col0, count):
                chunks(stage, w, col0, 1)
                with sp.Fori(1, count) as i:
                    for u in range(KT // 2):
                        unit(UNIT0[stage] + u, w, u * 2, 2, i * CHUNK + col0, CHUNK, i, KT // 2)

            def mod_loop(h):
                chunk_loop("mod_" + h.name, t["mod_w_2"][h.mod_layer], h.mod_chunk0 * CHUNK, h.turns)

            def rest_of_inputs():
                sp.dma_start(X[:], t["x"].rearrange("b (t p) d -> p (b t) d", p=P)).then_inc(s_x, 16)
                sp.dma_start(CSTA[:], consts[:, NCONST_ALL:NCONST]).then_inc(s_consta, 16)
            chunks("mkv0", t["ev_w_mem_kv"][0], 0, 2, behind=rest_of_inputs)
            chunks("mkv1", t["od_w_mem_kv"][0], 0, 2)
            chunks("ev_a", t["ev_w_in"][0], 0, 1)
            for u in range(8):
                unit(UNIT0["ev_a"] + 8 + u, t["ev_w_in"][0], 2 * u, 2, EV_CKV, EV_LAT - EV_CKV)
            chunk_loop("ev_b", t["ev_w_in"][0], EV_LAT, EV_W // CHUNK)
            mod_loop(MEM_EV)
            mod_loop(MOBA)
            chunks("uq", t["ev_w_uq"][0], 0, 3, kt=4)
            chunks("ukv", t["ev_w_ukv"][0], 0, 4, kt=2)
            mod_loop(MLA)
            chunks("ev_out", t["ev_w_out"][0], 0, 4, kt=EV_VW // P)
            chunk_loop("od_b", t["od_w_in"][0], 0, OD_IN // CHUNK)
            for u in range(KT // 2):
                unit(UNIT0["od_c"] + 2 * u, t["od_w_in"][0], 2 * u, 2, OD_IN // CHUNK * CHUNK, OD_IN % CHUNK)
                unit(UNIT0["od_c"] + 2 * u + 1, t["mod_w_2"][1], 2 * u, 2, 11 * CHUNK, CHUNK)
            for h in OD_LOOPS:
                mod_loop(h)
            chunks("od_out", t["od_w_out"][0], 0, 4, kt=OD_VW // P)

            gwv = t["lru_gate_w_2"][0].rearrange("d g n c e -> c d g n e")
            lw = t["lru_w_in_2"][0]

            def lru_units(i):
                loop = i is not None
                for b in range(2):
                    n = sp.snap(i * 2 + b) if loop else b
                    for part in range(2):
                        for half in range(2):
                            U = UNIT0["lru_in"] + b * 4 + part * 2 + half
                            unit(U, lw, half * 8, 8, i * 256 + (part * D + b * P) if loop else part * D + b * P, P, i, 8 if loop else 0)
                    if loop:
                        sp.wait_ge(s_gt, i * 2 + b - 1)
                    else:
                        sp.wait_ge(s_xn, 1)
                    for d in range(2):
                        for g in range(2):
                            sp.dma_start(GW[:, b, d * 2 + g, :], gwv[:, d, g, bass.ds(n, 1), :]).then_inc(s_gw[b], 16)
            lru_units(None)
            with sp.Fori(1, KT // 2) as i:
                lru_units(i)
            chunk_loop("lru_out", t["lru_w_out_2"][0], 0, 4)

            def att_units(i=None):
                for j in range(4):
                    for u in range(8):
                        unit(UNIT0["att_in"] + j * 8 + u, t["att_w_in_2"][0], u * 2, 2, j * D if i is None else i * CHUNK + j * D,
                             CHUNK, i, 32)
            att_units()
            with sp.Fori(1, GROUPS) as i:
                att_units(i)
            for j, (c, u) in enumerate(OUT_UNITS[:16]):
                unit(UNIT0["att_out"] + j, t["att_w_out_2"][0], u * 2, 2, c * CHUNK, CHUNK)
            with sp.Fori(2, 4) as i:
                for u in range(8):
                    unit(UNIT0["att_out"] + u, t["att_w_out_2"][0], u * 2, 2, i * CHUNK, CHUNK, i, 8)
            ov = out.rearrange("b (t p) d -> p (b t) d", p=P)
            for c in range(4):
                sp.wait_ge(s_re, RES0["att_out"] + c + 1)
                sp.dma_start(ov[:, :, c * CHUNK:(c + 1) * CHUNK], X[:, :, c * CHUNK:(c + 1) * CHUNK]).then_inc(s_out, 16)
            sp.wait_ge(s_out, 64)

        @block.tensor
        def _(pe):
            def split_ready(U, i=None, per=0):
                pe.wait_ge(*lo_made(U, i, per))

            def multiply(U, k0, nk, kt, n, tiles, x, i=None, per=0, hold=None):
                split_ready(U, i, per)
                wh, wl = (W[:, U % SLOTS, 0:nk * n].rearrange("p (k n) -> p k n", k=nk) for W in (WH, WL))
                for k in range(k0, k0 + nk):
                    for m, bank in tiles:
                        if hold is not None and k == k0 and m == hold[0]:
                            pe.wait_ge(*hold[1])
                        xh, xl = x(k, m)
                        for j, (a, w) in enumerate(((xh, wh), (xh, wl), (xl, wh))):
                            mm = pe.matmul(PS[:, bank, 0:n], a, w[:, k - k0, :], start=(k == 0 and j == 0), stop=(k == kt - 1 and j == 2))
                mm.then_inc(s_wused, 1)

            def product(stage, c, kt, n, tiles, x, i=None, per=0):
                units = -(-kt // 2)
                for u in range(units):
                    multiply(UNIT0[stage] + c * units + u, 2 * u, min(2, kt - 2 * u), kt, n, tiles, x, i, per)

            def chunk(stage, c, kt, n, x, i=None, per=0, step=0):
                g = CHUNK0[stage] + c
                if g >= 2:
                    pe.wait_ge(s_ge, at(g - 1, i, step))
                product(stage, c, kt, n, [(m, 2 * (g % 2) + m) for m in range(TT)], x, i, per)

            def residual(stage, kt):
                for c in range(4):
                    if c >= 2:
                        pe.wait_ge(s_re, RES0[stage] + c - 1)
                    product(stage, c, kt, CHUNK, [(m, 2 * (c % 2) + m) for m in range(TT)], xt)

            def xt(k, m):
                cols = slice(k * SEQ + m * P, k * SEQ + (m + 1) * P)
                return ATH[:, cols], ATL[:, cols]

            fills = [0]

            def to_features(rows, first=0, count=8, before=None):
                for j in range(first, first + count):
                    q = fills[0]
                    if q >= 4:
                        pe.wait_ge(s_tmp, q - 3)
                    if before is not None:
                        before(j)
                    for k in range(2):
                        for tt in range(TT):
                            col = (k * TT + tt) * P
                            mm = pe.transpose(PS[:, 4 + q % 4, col:col + P], rows(tt, 2 * j + k), ident)
                    mm.then_inc(s_xt, 1)
                    fills[0] += 1

            def tiles_of(rows):
                return lambda tt, k: rows[:, tt, k * P:(k + 1) * P]

            def features_ready(ahead=0):
                pe.wait_ge(s_xl, fills[0] - ahead)

            def fill_mod(stage, units, i=None, step=1, bank=0):
                for u in units:
                    U = UNIT0[stage] + step * u + step - 1
                    split_ready(U, i, 0 if i is None else 8)
                    for k in range(2 * u, 2 * u + 2):
                        for W in (WH, WL):
                            mm = pe.matmul(PS[:, bank, :], CS[:, 4 * k:4 * k + P], W[:, U % SLOTS, k % 2 * CHUNK:(k % 2 + 1) * CHUNK],
                                           start=(k == 0 and W is WH), stop=(k == KT - 1 and W is WL))
                    mm.then_inc(s_wused, 1)

            def turn_mod(m, rows, i=None, bank=1):
                pe.wait_ge(s_mods, at(m + 1, i, 1))
                pe.wait_ge(s_modd, at(m + 1, i, 1))
                for j in range(4):
                    mm = pe.transpose(PS[:, bank, j * P:(j + 1) * P], rows[:, j * P:(j + 1) * P], ident)
                mm.then_inc(s_modt, 1)

            def head_loop(h):
                H = HE if h in EV_LOOPS else HO
                mod = "mod_" + h.name
                with pe.Fori(0, h.turns) as i:
                    n = lambda a, plus: i * 2 + (h.n0 + a + plus)
                    pair = h.kind == "swa"
                    for a in range(1 if pair else 2):
                        pe.wait_ge(s_stg, n(1 if pair else a, 1))
                        for tt in range(TT):
                            pe.transpose(PS[:, 2 + a, tt * P:(tt + 1) * P], QS[:, a, tt, 0:P], ident)
                        for tt in range(TT):
                            mm = pe.transpose(PS[:, 2 + a, SEQ + tt * P:SEQ + (tt + 1) * P], KS[:, a, tt, :], ident)
                        if h.kind == "mla":
                            for tt in range(TT):
                                mm = pe.transpose(PS[0:ROPE, 6 + a, tt * P:(tt + 1) * P], QS[:, a, tt, NOPE:NOPE + ROPE], ident)
                        mm.then_inc(s_t1, 2 if pair else 1)
                    fill_mod(mod, range(0, 2), i)
                    for a in range(2):
                        pe.wait_ge(s_qk, n(1 if pair else a, 1))
                        if pair:
                            qk = QKT[64 * a:64 * a + 64, 0, :]
                        else:
                            qk = QKT[:, a, :]
                        for tt in range(TT):
                            mla = h.kind == "mla"
                            mm = pe.matmul(PS[:, 6 + a, tt * SEQ:(tt + 1) * SEQ], qk[:, tt * P:(tt + 1) * P], qk[:, SEQ:2 * SEQ],
                                           start=True, stop=not mla)
                            if mla:
                                mm = pe.matmul(PS[:, 6 + a, tt * SEQ:(tt + 1) * SEQ], QRT[0:ROPE, a, tt * P:(tt + 1) * P],
                                               KPT[0:ROPE, :], start=False, stop=True)
                        mm.then_inc(s_sc, 1)
                    fill_mod(mod, range(2, 4), i)
                    for a in range(2):
                        pe.wait_ge(s_ex, n(a, 1))
                        pe.wait_ge(s_ye, n(a, 1))
                        for tt in range(TT):
                            for kt in range(TT):
                                mm = pe.transpose(PS[:, 4 + a, kt * SEQ + tt * P:kt * SEQ + (tt + 1) * P],
                                                  S[:, a, tt, kt * P:(kt + 1) * P], ident)
                        mm.then_inc(s_pt, 1)
                    fill_mod(mod, range(4, 6), i)
                    for a in range(2):
                        pe.wait_ge(s_pe, n(a, 1))
                        for tt in range(TT):
                            for kt in range(TT):
                                if pair:
                                    v = H[:, kt, h.v:h.v + SWA_DH]
                                elif h.mem is not None:
                                    v = MKV[:, h.mem, kt, bass.ds(i * 256 + (h.v + a * P), P)]
                                else:
                                    width = NOPE + MLA_DV if h.kind == "mla" else P
                                    v = H[:, kt, bass.ds(i * (2 * width) + (h.v + a * width), P)]
                                w = SWA_DH if pair else P
                                mm = pe.matmul(PS[:, 6 + a, tt * P:tt * P + w],
                                               PT[:, a, kt * SEQ + tt * P:kt * SEQ + (tt + 1) * P], v,
                                               start=(kt == 0), stop=(kt == TT - 1))
                        mm.then_inc(s_o, 1)
                    fill_mod(mod, range(6, 8), i)
                    for a in range(1 if pair else 2):
                        pe.wait_ge(s_ys, n(1 if pair else a, 1))
                        for tt in range(TT):
                            mm = pe.transpose(PS[:, 4 + a, tt * P:(tt + 1) * P], YS[:, a, tt, :], ident)
                        mm.then_inc(s_yt, 2 if pair else 1)
                    turn_mod(h.mod0, MODS_EV if h in EV_LOOPS else MODS_OD, i)

            pe.sem_inc(s_t1, 2)
            pe.wait_ge(s_const, 16)
            pe.wait_ge(s_rows, S_ROWS)
            for v, rows in enumerate(VEC_ROWS):
                mm = pe.transpose(PS[:, 0, v * P:v * P + rows], GR[0:rows, v, :], ident[0:rows, 0:rows])
            mm.then_inc(s_vt, 1)
            def mem0(k, m):
                return xt(k, m)

            def mem1(k, m):
                cols = slice(k * SEQ + m * P, k * SEQ + (m + 1) * P)
                return M1H[:, cols], M1L[:, cols]
            pe.wait_ge(s_mem, 16)
            to_features(tiles_of(MEMX))
            to_features(tiles_of(MEMX), 0, 4)
            pe.wait_ge(s_vec, 4)
            features_ready(4)
            chunk("mkv0", 0, KT, CHUNK, mem0)
            to_features(tiles_of(MEMX), 4, 4)
            chunk("mkv0", 1, KT, CHUNK, mem0)
            pe.wait_ge(s_x, 16)
            to_features(tiles_of(X), 0, 4)
            features_ready(4)
            chunk("mkv1", 0, KT, CHUNK, mem1)
            to_features(tiles_of(X), 4, 4)
            chunk("mkv1", 1, KT, CHUNK, mem1)
            features_ready()
            chunk("ev_a", 0, KT, CHUNK, xt)
            chunk("ev_a", 1, KT, EV_LAT - EV_CKV, xt)
            for c in range(2):
                chunk("ev_b", c, KT, CHUNK, xt)
            pe.wait_ge(s_ge, CHUNK0["ev_b"])
            to_features(tiles_of(HQ), 0, 3)
            pe.wait_ge(s_rope, 1)
            pe.wait_ge(s_xl, fills[0] - 3)
            for tt in range(TT):
                mm = pe.transpose(PS[0:ROPE, 7, tt * P:(tt + 1) * P], HQ[:, tt, EV_KPE:EV_KPE + ROPE], ident)
            mm.then_inc(s_kpe, 1)
            with pe.Fori(0, 5) as i:
                for c in range(2, 4):
                    chunk("ev_b", c, KT, CHUNK, xt, i, 16, 2)
            pe.wait_ge(s_ge, CHUNK0["uq"])
            pe.wait_ge(s_kpt, 1)
            pe.wait_ge(s_tmp, fills[0])
            pe.wait_ge(s_cs, 1)
            head_loop(MEM_EV)
            head_loop(MOBA)
            pe.wait_ge(s_modd, MLA.mod0 + 1)
            features_ready()
            for c in range(3):
                chunk("uq", c, 4, CHUNK, xt)
            for c in range(4):
                chunk("ukv", c, 2, CHUNK, lambda k, m: xt(k + 4, m))
            pe.wait_ge(s_ge, CHUNK0["od_b"])
            head_loop(MLA)
            pe.wait_ge(s_ye, 20 + 2)
            pe.wait_ge(s_modd, MOD_ALONE + 1)
            residual("ev_out", EV_VW // P)

            def x_complete(stage):
                return lambda j: pe.wait_ge(s_re, RES0[stage] + j // 2 + 1)
            to_features(tiles_of(X), before=x_complete("ev_out"))
            features_ready()
            with pe.Fori(0, 6) as i:
                for c in range(2):
                    chunk("od_b", c, KT, CHUNK, xt, i, 16, 2)
            pe.wait_ge(s_ge, CHUNK0["od_c"] - 1)
            for u in range(KT // 2):
                multiply(UNIT0["od_c"] + 2 * u, 2 * u, 2, KT, OD_IN % CHUNK, [(m, 2 + m) for m in range(TT)], xt)
                fill_mod("od_c", [u], None, 2, 4)
            turn_mod(MOD_ALONE, MODS_OD, None, 5)
            pe.wait_ge(s_ge, CHUNK0["od_c"] + 1)
            pe.wait_ge(s_modd, MOD_ALONE + 2)
            for h in OD_LOOPS:
                head_loop(h)
            pe.wait_ge(s_ye, N_HEADS + 2)
            pe.wait_ge(s_modd, N_MOD + 1)
            residual("od_out", OD_VW // P)

            pe.wait_ge(s_re, RES0["lru_out"])
            pe.wait_ge(s_xn, 1)
            to_features(tiles_of(CN))
            pe.wait_ge(s_xn, 2)
            to_features(tiles_of(XN))

            with pe.Fori(0, KT // 2) as i:
                for b in range(2):
                    n = lambda plus: i * 2 + (b + plus)
                    pe.wait_ge(s_xc, n(1))
                    for part in range(2):
                        if part:
                            pe.wait_ge(s_gs, n(1))
                        for half in range(2):
                            U = UNIT0["lru_in"] + b * 4 + part * 2 + half
                            split_ready(U, i, 8)
                            features_ready(0 if half else 4)
                            for k in range(8):
                                w = slice(k * P, (k + 1) * P)
                                kk = half * 8 + k
                                for j, (W, x) in enumerate(((WH, FTH), (WH, FTL), (WL, FTH))):
                                    mm = pe.matmul(PS[:, part * 2 + b, :], W[:, U % SLOTS, w], x[:, kk, :],
                                                   start=(kk == 0 and j == 0), stop=(kk == KT - 1 and j == 2))
                            mm.then_inc(s_wused, 1)
                    pe.wait_ge(s_xc, n(3))
                    pe.wait_ge(s_gw[b], i * 64 + 64)
                    pe.wait_ge(s_sg, n(1))
                    for j in range(4):
                        mm = pe.matmul(PS[:, 4 + j, :], GW[:, b, j, :], XC[:, b, :, :].rearrange("p c s -> p (c s)"),
                                       start=True, stop=True)
                    mm.then_inc(s_gt, 1)

            def gate_row(j, bank, held):
                if held:
                    pe.wait_ge(s_gbe, held)
                pe.wait_ge(s_dg, j + 1)
                for k in range(4):
                    mm = pe.matmul(PS[:, bank, k * P:(k + 1) * P], ONES, DIAG(j)[:, k, :], start=True, stop=True)
                mm.then_inc(s_gb, 1)

            def ft(k, m):
                return FTH[:, k, m * P:(m + 1) * P], FTL[:, k, m * P:(m + 1) * P]

            def lru_y(k, m):
                if m == 0:
                    pe.wait_ge(s_ylo, k + 1)
                return ft(k, m)
            all_tiles = lambda c: [(m, 4 * ((c + 1) % 2) + m) for m in range(4)]
            pe.wait_ge(s_sg, KT + 1)
            product("lru_out", 0, KT, CHUNK, all_tiles(0), lru_y)
            pe.wait_ge(s_gs, KT + 2)
            for j in range(8):
                gate_row(j, j % 4, j - 3 if j >= 4 else 0)
            pe.wait_ge(s_gbe, 8)
            product("lru_out", 1, KT, CHUNK, all_tiles(1), ft)
            for c in range(2, 4):
                pe.wait_ge(s_re, RES0["lru_out"] + c - 1)
                product("lru_out", c, KT, CHUNK, all_tiles(c), ft)

            pe.wait_ge(s_re, RES0["att_out"])
            def wait(s, value):
                if not isinstance(value, int) or value > 0:
                    pe.wait_ge(s, value)

            def att_unit(i, u):
                part, v = divmod(u, 8)
                hold = None
                if part == 0:
                    tiles = [(2, 0), (3, 1)]
                    if v == 0:
                        wait(s_dqe, i * 4 + 4)
                elif part == 1:
                    tiles = [(2, 2), (3, 3), (0, 0), (1, 1)]
                    if v == 0:
                        hold = (0, (s_dqe, i * 4 + 5))
                elif part == 2:
                    tiles = [(m, 4 + m) for m in range(4)]
                    if v == 0:
                        wait(s_oe, i * 8 + 8)
                else:
                    tiles = [(2, 0), (3, 1)]
                    if v == 0:
                        pe.wait_ge(s_dqe, i * 4 + 6)
                multiply(UNIT0["att_in"] + 32 + u, 2 * v, 2, KT, CHUNK, tiles, ft, i, 32, hold)

            def qk_transposes(i, j):
                if j == 0:
                    pe.wait_ge(s_qn, i + 2)
                    wait(s_dye, i + 1)
                else:
                    pe.wait_ge(s_e2, i * 4 + (4 + j))
                for kt in range(4):
                    pe.transpose(PS[:, 2, kt * P:(kt + 1) * P], RQK[:, kt, j * P:(j + 1) * P], ident)
                for tt in range(TT):
                    mm = pe.transpose(PS[:, 3, tt * P:(tt + 1) * P], RQK[:, 4 + tt, j * P:(j + 1) * P], ident)
                mm.then_inc(s_e1, 1)

            def scores(i, s):
                j, tt = divmod(s, 2)
                if s == 0:
                    pe.wait_ge(s_dqe, i * 4 + 3)
                else:
                    pe.wait_ge(s_e5, i * 8 + s)
                if tt == 0:
                    pe.wait_ge(s_e2, i * 4 + (j + 1))
                for c in range(2):
                    mm = pe.matmul(PS[:, 4 + c, :], DQK[64 * c:64 * c + 64, j, CHUNK + tt * P:CHUNK + (tt + 1) * P],
                                   DQK[64 * c:64 * c + 64, j, 0:CHUNK], start=True, stop=True)
                mm.then_inc(s_e3, 1)

            def weights_transposes(i, s):
                pe.wait_ge(s_e8, i * 8 + (s + 1))
                if s >= 1:
                    pe.wait_ge(s_e10, i * 8 + s)
                for kt in range(4):
                    mm = pe.transpose(PS[:, 6, kt * P:(kt + 1) * P], DE[:, s % 2, 0, kt * P:(kt + 1) * P], ident)
                mm.then_inc(s_e9, 1)

            def weights_values(i, s):
                pe.wait_ge(s_e10, i * 8 + (s + 1))
                if s >= 1:
                    pe.wait_ge(s_oe, i * 8 + s)
                j = s // 2
                for kt in range(4):
                    mm = pe.matmul(PS[:, 7, 0:P], DPT[:, s % 2, kt * P:(kt + 1) * P], RV[:, kt, j * P:(j + 1) * P],
                                   start=(kt == 0), stop=(kt == 3))
                mm.then_inc(s_e11, 1)

            def y_transposes(i, bank):
                pe.wait_ge(s_oy, i + 1)
                for j in range(4):
                    for tt in range(TT):
                        col = (j % 2 * TT + tt) * P
                        mm = pe.transpose(PS[:, bank + j // 2, col:col + P], OS[:, tt, j * P:(j + 1) * P], ident)
                mm.then_inc(s_dyt, 1)

            def projections_behind(i, heads):
                for u in range(16, 24):
                    att_unit(i, u)
                if heads:
                    pe.wait_ge(s_dqe, i * 4 + 6)
                    y_transposes(i, 2)
                for u in range(24, 28):
                    att_unit(i, u)
                for j in range(4):
                    att_unit(i, 28 + j)
                    qk_transposes(i, j)

            pe.wait_ge(s_xn, 3)
            to_features(tiles_of(XN), 0, 4)
            lat = fills[0] - 4
            for u in range(8):
                if u < 4:
                    to_features(tiles_of(XN), 4 + u, 1)
                if u == 0:
                    pe.wait_ge(s_re, RES0["att_out"])
                pe.wait_ge(s_xl, lat + u + 1)
                att_unit(-1, u)
                if u == 4:
                    pe.wait_ge(s_xn, 4)
                if u >= 4:
                    to_features(tiles_of(CN), 2 * (u - 4), 2)
            features_ready()
            for u in range(8, 16):
                att_unit(-1, u)
            projections_behind(-1, False)
            with pe.Fori(0, GROUPS - 1) as i:
                scores(i, 0)
                for s in range(8):
                    att_unit(i, 2 * s)
                    weights_transposes(i, s)
                    if s < 7:
                        scores(i, s + 1)
                    att_unit(i, 2 * s + 1)
                    weights_values(i, s)
                projections_behind(i, True)

            def att_y(k, m):
                return DYH[:, k, m * P:(m + 1) * P], DYL[:, k, m * P:(m + 1) * P]

            def out_unit(j):
                c, u = OUT_UNITS[j]
                if c == 0:
                    pe.wait_ge(s_ylo, KT + 2 * u + 2)
                multiply(UNIT0["att_out"] + j, 2 * u, 2, KT, CHUNK, [(m, 2 * (c % 2) + m) for m in range(TT)], att_y)
            last = GROUPS - 1
            scores(last, 0)
            pe.wait_ge(s_dqe, 4 * GROUPS)
            pe.wait_ge(s_e2, 4 * GROUPS)
            for s in range(8):
                out_unit(OUT_FILL[s][0])
                weights_transposes(last, s)
                if s < 7:
                    scores(last, s + 1)
                for j in OUT_FILL[s][1:]:
                    out_unit(j)
                weights_values(last, s)
            for j in range(8, 12):
                gate_row(j, 4 + j % 2, j - 1 if j >= 10 else 0)
            pe.wait_ge(s_oe, 8 * GROUPS)
            y_transposes(last, 6)
            for j in range(2 * OUT_AHEAD, len(OUT_UNITS)):
                c, u = OUT_UNITS[j]
                if c >= 2 and u == 0:
                    pe.wait_ge(s_re, RES0["att_out"] + c - 1)
                out_unit(j)

        @block.scalar
        def _(act):
            act.dma_start(SUBG, t["att_subln_2"][0].unsqueeze(0).to_broadcast([P, 128])).then_inc(s_bc, 16)
            act.dma_start(QG, t["att_q_norm_2"][0].unsqueeze(0).to_broadcast([P, 64])).then_inc(s_bc, 16)
            act.dma_start(KG, t["att_k_norm_2"][0].unsqueeze(0).to_broadcast([P, 64])).then_inc(s_bc, 16)
            act.dma_start(LV, t["att_lambda_2"][0].rearrange("a b -> (a b)").unsqueeze(0).to_broadcast([P, 256])).then_inc(s_bc, 16)
            act.dma_start(SINK, t["od_sinks"][0].unsqueeze(0).to_broadcast([P, 16])).then_inc(s_bc, 16)

            def hi(U, n=UNIT, i=None, per=0):
                act.wait_ge(s_w[U % SLOTS], landed(U, i, per))
                if U >= SLOTS:
                    act.wait_ge(s_wused, at(U - SLOTS + 1, i, per))
                act.copy(WH[:, U % SLOTS, 0:n], RA[:, U % SLOTS, 0:n]).then_inc(s_hi, 1)

            def his(stage, units, n=UNIT, i=None, per=0):
                for u in units:
                    hi(UNIT0[stage] + u, n, i, per)

            def squares(r, rows, junk):
                for j, row in enumerate(rows):
                    if SQUARED[r] - len(rows) + j:
                        act.wait_ge(s_sq, SQUARED[r] - len(rows) + j)
                    act.activation(junk[:, 0:row.shape[-1]], row, ACT.Square, accum_out=ST[:, r, j:j + 1]).then_inc(s_sq, 1)

            sums = [0]

            def chunk_squares(tiles, sums_of, c, junk):
                for tt in range(TT):
                    if sums[0]:
                        act.wait_ge(s_sqc, sums[0])
                    act.activation(junk, tiles[:, tt, c * CHUNK:(c + 1) * CHUNK], ACT.Square, accum_out=sums_of[:, tt, c:c + 1]).then_inc(s_sqc, 1)
                    sums[0] += 1

            def root(r, n):
                act.wait_ge(s_ms, r + 1)
                act.activation(ST[:, r, 0:n], ST[:, r, 0:n], ACT.Sqrt).then_inc(s_rt, 1)

            fills = [0]

            def scale_features(scale, shift, tmp, first=0, count=8):
                for j in range(first, first + count):
                    q = fills[0]
                    fills[0] += 1
                    act.wait_ge(s_xt, q + 1)
                    if q >= 4:
                        act.wait_ge(s_xl, q - 3)
                    for k in range(2):
                        ins = act.activation(tmp[:, q % 4, k * SEQ:(k + 1) * SEQ], PS[:, 4 + q % 4, k * SEQ:(k + 1) * SEQ], ACT.Identity,
                                             scale=scale(2 * j + k), bias=0.0 if shift is None else shift(2 * j + k))
                    ins.then_inc(s_tmp, 1)

            def evict(stage, c, dest, r, j0=0, n=CHUNK, silu=False, i=None, step=0):
                g = CHUNK0[stage] + c
                act.wait_ge(s_wused, at(multiplied(stage, c), i, 8 * step))
                for m in range(TT):
                    ins = act.activation(dest(m), PS[:, 2 * (g % 2) + m, 0:n], ACT.Silu if silu else ACT.Copy,
                                         scale=ST[:, r, j0 + m:j0 + m + 1])
                ins.then_inc(s_ge, 1)

            def head_loop(h):
                def modulation_hi(i, units):
                    for u in units:
                        U = UNIT0["mod_" + h.name] + u
                        if isinstance(i, int):
                            hi(U + 8 * i)
                        else:
                            hi(U, UNIT, i, 8)

                def turn(i):
                    n = lambda a, plus: i * 2 + (h.n0 + a + plus)
                    pair = h.kind == "swa"
                    for a in range(1 if pair else 2):
                        act.wait_ge(s_t1, n(1 if pair else a, 3))
                        ins = act.copy(QKT[:, a, :], PS[:, 2 + a, :])
                        if h.kind == "mla":
                            ins = act.copy(QRT[0:ROPE, a, :], PS[0:ROPE, 6 + a, 0:SEQ])
                        ins.then_inc(s_qk, 2 if pair else 1)
                    modulation_hi(i, [4, 5])
                    for a in range(2):
                        act.wait_ge(s_mx, n(a, 1))
                        for tt in range(TT):
                            ins = act.activation(S[:, a, tt, :], S[:, a, tt, :], ACT.Exp, bias=NM[:, a, tt:tt + 1],
                                                 accum_out=LS[:, a, tt:tt + 1])
                        if pair:
                            ins = act.activation(ES[:, a, :], SN[:, a, :], ACT.Exp)
                        ins.then_inc(s_ex, 1)
                    modulation_hi(i, range(6, 11))
                    for a in range(1 if pair else 2):
                        act.wait_ge(s_yt, n(1 if pair else a, 1))
                        y = i * SEQ + h.y0 * SEQ if pair else i * (2 * SEQ) + (h.y0 + a) * SEQ
                        act.copy(ATH[:, bass.ds(y, SEQ)], PS[:, 4 + a, 0:SEQ]).then_inc(s_yh, 2 if pair else 1)
                    modulation_hi(i, [11])
                with act.Fori(0, h.turns - 1) as i:
                    turn(i)
                turn(h.turns - 1)

            def token_tiles(rows):
                return [rows[:, tt, :] for tt in range(TT)]

            his("mkv0", range(0, 4))
            act.wait_ge(s_vec, 4)
            gvec = lambda name: (lambda k: vec(name, k))
            scale_features(gvec("ev_mem_norm_g"), None, TMP_X)
            scale_features(gvec("od_mem_norm_g"), None, TMP_X, 0, 4)
            his("mkv0", range(4, 8))
            act.wait_ge(s_mem, 16)
            squares(0, token_tiles(MEMX), JUNK_A)
            act.wait_ge(s_x, 16)
            squares(1, token_tiles(X), JUNK_A)
            root(0, 2)
            root(1, 2)
            act.activation(COND, GT[:, VEC_AT["c_2"]:VEC_AT["c_2"] + 32].rearrange("p (v k) -> p k v", v=2), ACT.Silu).then_inc(s_cond, 1)
            act.wait_ge(s_cond, 1)
            act.copy(CSV[:, :, 0:2], COND).then_inc(s_cond, 1)
            act.wait_ge(s_lam, 1)
            act.activation(SC[:, 0:32], SC[:, 0:32], ACT.Exp, scale=-1.0)
            act.activation(SC[:, 64:66], SC[:, 64:66], ACT.Exp).then_inc(s_exl, 1)
            his("mkv0", range(8, 12))
            scale_features(gvec("od_mem_norm_g"), None, TMP_X, 4, 4)
            act.wait_ge(s_rs, 2)
            kv = lambda l, c: (lambda m: MKV[:, l, m, c * CHUNK:(c + 1) * CHUNK])
            evict("mkv0", 0, kv(0, 0), 0)
            his("mkv0", range(12, 16))
            his("mkv1", range(0, 4))
            scale_features(gvec("ev_norm_g"), None, TMP_X, 0, 4)
            evict("mkv0", 1, kv(0, 1), 0)
            his("mkv1", range(4, 12))
            scale_features(gvec("ev_norm_g"), None, TMP_X, 4, 4)
            evict("mkv1", 0, kv(1, 0), 0)
            his("mkv1", range(12, 16))
            his("ev_a", range(0, 4))
            evict("mkv1", 1, kv(1, 1), 0)
            his("ev_a", range(4, 8))
            narrow = 2 * (EV_LAT - EV_CKV)
            his("ev_a", range(8, 12), narrow)
            evict("ev_a", 0, lambda m: HQ[:, m, 0:MLA_QR], 1)
            his("ev_a", range(12, 16), narrow)
            his("ev_b", range(0, 4))
            evict("ev_a", 1, lambda m: HQ[:, m, EV_CKV:EV_LAT], 1, n=EV_LAT - EV_CKV)
            his("ev_b", range(4, 8))

            def to_rows(H, c, i=None):
                return lambda m: H[:, m, c * CHUNK:(c + 1) * CHUNK] if i is None else H[:, m, bass.ds(i * 1024 + c * CHUNK, CHUNK)]

            def split_and_evict(stage, H, c, r, silu, i=None):
                his(stage, range(8 * c + 8, 8 * c + 12), i=i, per=16)
                evict(stage, c, to_rows(H, c, i), r, silu=silu, i=i, step=2)
                his(stage, range(8 * c + 12, 8 * c + 16), i=i, per=16)

            split_and_evict("ev_b", HE, 0, 1, False)
            his("ev_b", range(16, 20))
            act.wait_ge(s_ge, CHUNK0["ev_b"])
            for j, (first, end) in enumerate(((0, MLA_QR), (0, MLA_QR), (EV_CKV, EV_KPE), (EV_CKV, EV_KPE))):
                act.wait_ge(s_sq, SQUARED[1] + j)
                act.activation(JUNK_LAT[:, 0:end - first], HQ[:, j % 2, first:end], ACT.Square, accum_out=ST[:, 2, j:j + 1]).then_inc(s_sq, 1)
            evict("ev_b", 1, to_rows(HE, 1), 1)
            scale_features(lambda k: vec("ev_q_norm_g", k) if k < 4 else vec("ev_kv_norm_g", k - 4), None, TMP_LAT, 0, 3)
            his("ev_b", range(20, 24))
            root(2, 4)
            with act.Fori(0, 2) as i:
                for c in range(2, 4):
                    split_and_evict("ev_b", HE, c, 1, False, i)
            split_and_evict("ev_b", HE, 6, 1, False)
            with act.Fori(0, 2) as i:
                for c in range(7, 9):
                    split_and_evict("ev_b", HE, c, 1, True, i)
            his("mod_mem_ev", range(0, 4))
            evict("ev_b", 11, to_rows(HE, 11), 1, silu=True)
            head_loop(MEM_EV)
            head_loop(MOBA)
            act.wait_ge(s_rs, 3)
            uq = lambda c: (lambda m: HE[:, m, EV_QA + c * CHUNK:EV_QA + (c + 1) * CHUNK])
            ukv = lambda c: (lambda m: HE[:, m, EV_KVA + c * CHUNK:EV_KVA + (c + 1) * CHUNK])
            his("uq", range(4, 6))
            evict("uq", 0, uq(0), 2, 0)
            his("ukv", range(0, 2))
            evict("uq", 1, uq(1), 2, 0)
            his("ukv", range(2, 4))
            evict("uq", 2, uq(2), 2, 0)
            for c in range(4):
                evict("ukv", c, ukv(c), 2, 2)
                his("mod_mla", [c])
            head_loop(MLA)
            his("ev_out", range(4, 40))

            his("od_b", range(0, 4))
            scale_features(gvec("od_norm_g"), None, TMP_X)
            act.wait_ge(s_re, RES0["od_out"])
            squares(3, token_tiles(X), JUNK_A)
            root(3, 2)
            his("od_b", range(4, 8))
            act.wait_ge(s_rs, 4)
            with act.Fori(0, 4) as i:
                for c in range(2):
                    split_and_evict("od_b", HO, c, 3, False, i)
            with act.Fori(0, 1) as i:
                for c in range(8, 10):
                    split_and_evict("od_b", HO, c, 3, True, i)
            split_and_evict("od_b", HO, 10, 3, True)

            def od_c_his(units):
                for u in units:
                    his("od_c", [u], UNIT if u % 2 else 2 * (OD_IN % CHUNK))
            od_c_his(range(0, 4))
            evict("od_b", 11, to_rows(HO, 11), 3, silu=True)
            od_c_his(range(4, 16))
            his("mod_swa0", range(0, 4))
            evict("od_c", 0, lambda m: HO[:, m, OD_IN // CHUNK * CHUNK:OD_IN], 3, n=OD_IN % CHUNK, silu=True)
            for h in OD_LOOPS:
                head_loop(h)
            act.wait_ge(s_ys, N_HEADS)
            act.dma_start(CX, t["ctx_2"].rearrange("b (t p) d -> p (b t) d", p=P)).then_inc(s_ctx, 16)
            act.dma_start(FG, t["final_norm_g"].unsqueeze(0).to_broadcast([P, D])).then_inc(s_fg, 16)
            his("od_out", range(4, 13))
            act.wait_ge(s_ctx, 16)
            squares(4, token_tiles(CX), BUF[:, 0:D])
            his("od_out", range(13, 18))
            root(4, 2)
            act.wait_ge(s_sq, SQUARED[4])
            for c, units in enumerate((range(18, 22), range(22, 31), range(31, 36))):
                his("od_out", units)
                act.wait_ge(s_re, RES0["od_out"] + c + 1)
                chunk_squares(X, SQX, c, BUF[:, 0:CHUNK])

            his("lru_in", range(0, 4))
            act.wait_ge(s_re, RES0["lru_out"])
            chunk_squares(X, SQX, 3, BUF[:, 0:CHUNK])
            root(5, 2)
            mod_scale = lambda j: (lambda k: MSC[:, 16 * j + k:16 * j + k + 1])
            mod_shift = lambda l, w: (lambda k: MODT[:, l, k, w:w + 1])
            act.wait_ge(s_msc, 4)
            scale_features(mod_scale(1), mod_shift(0, 1), TMP_B)
            act.wait_ge(s_sqc, sums[0])
            for tt in range(TT):
                act.wait_ge(s_xf, tt + 1)
                if tt:
                    act.wait_ge(s_sq, SQUARED[6] - 1)
                act.activation(BUF[:, 0:D], X[:, tt, :], ACT.Square, accum_out=ST[:, 6, tt:tt + 1]).then_inc(s_sq, 1)
            root(6, 2)
            scale_features(mod_scale(0), mod_shift(0, 0), TMP_B)
            his("lru_in", range(4, 8))
            act.sem_inc(s_sg, 1)

            def y_hi(first, count, dest, src):
                for k in range(first, first + count):
                    act.copy(dest[:, k, :], src[:, k, :]).then_inc(s_yhi, 1)

            def lru_block(b, ahead, i=None):
                n = lambda plus: b + plus if i is None else i * 2 + (b + plus)
                act.wait_ge(s_gt, n(1))
                act.wait_ge(s_y, n(2))
                for j in range(4):
                    act.activation(RI[:, j, :], PS[:, 4 + j, :], ACT.Sigmoid, bias=BV[:, b % 2, 5 + j:6 + j])
                act.activation(SG, PS[:, 2 + b % 2, :], ACT.Sigmoid).then_inc(s_sg, 1)
                if ahead is None:
                    y_hi(0, 4, FTH, YL)
                act.wait_ge(s_sg, n(2))
                for d in range(2):
                    act.activation(LA[:, d, :], RI[:, 2 * d, :], ACT.Exp, scale=BV[:, b % 2, 9 + d:10 + d])
                for d in range(2):
                    ins = act.activation(LW[:, d, :], RI[:, 2 * d, :], ACT.Tanh, scale=BV[:, b % 2, 9 + d:10 + d])
                ins.then_inc(s_ab, 1)
                if ahead is not None:
                    hi(ahead, UNIT, i, 8)
                act.wait_ge(s_w2, n(1))
                act.activation(LWF, LWF, ACT.Sqrt, scale=-1.0).then_inc(s_sqr, 1)
                if ahead is not None:
                    for u in range(1, 4):
                        hi(ahead + u, UNIT, i, 8)

            with act.Fori(0, KT // 2 - 1) as i:
                for b in range(2):
                    lru_block(b, UNIT0["lru_in"] + 8 + 4 * b, i)
            lru_block(KT - 2, UNIT0["lru_out"])
            lru_block(KT - 1, None)

            def gate_rows_out(dest, j, bank):
                act.wait_ge(s_gb, j + 1)
                act.copy(dest[:, j % 4 * CHUNK:(j % 4 + 1) * CHUNK], PS[:, bank, :]).then_inc(s_gbe, 1)

            y_hi(4, KT - 5, FTH, YL)
            his("lru_out", range(4, 6))
            act.wait_ge(s_y, KT + 2)
            y_hi(KT - 1, 1, FTH, YL)
            act.dma_start(CX, t["ctx_2"].rearrange("b (t p) d -> p (b t) d", p=P)).then_inc(s_cx2, 16)
            his("lru_out", range(6, 12))
            for j in range(8):
                gate_rows_out(G_LAT if j < 4 else G_CTX, j, j % 4)
            his("lru_out", range(12, 16))

            def lru_squares(c):
                act.wait_ge(s_re, RES0["lru_out"] + c + 1)
                chunk_squares(X, SQL, c, BUF[:, 7680:8192])
                chunk_squares(CX, SQC, c, BUF[:, 7680:8192])
            for c in range(2, 4):
                his("lru_out", range(8 * c, 8 * c + 8))
                lru_squares(c - 2)
            his("att_in", range(0, 4))
            lru_squares(2)
            act.wait_ge(s_re, RES0["lru_out"] + 4)
            chunk_squares(X, SQL, 3, BUF[:, 7680:8192])

            root(7, 2)
            act.wait_ge(s_re, RES0["lru_out"] + 5)
            chunk_squares(CX, SQC, 3, BUF[:, 7680:8192])
            scale_features(mod_scale(2), mod_shift(1, 0), TMP_B)
            root(8, 2)

            def att_hi(i, units):
                for u in units:
                    hi(UNIT0["att_in"] + 32 + u if not isinstance(i, int) else UNIT0["att_in"] + 32 * (i + 1) + u, UNIT,
                       None if isinstance(i, int) else i, 32)

            def take_chunk(i, part, dest, tiles, bank, silu=False):
                act.wait_ge(s_wused, i * 32 + (UNIT0["att_in"] + 32 + 8 * part + 8))
                for m in range(tiles):
                    ins = act.activation(dest[:, m, :], PS[:, bank + m, :], ACT.Silu) if silu else act.copy(dest[:, m, :], PS[:, bank + m, :])
                ins.then_inc(s_dqe, 1)

            def exponentials(i, s):
                act.wait_ge(s_e4, i * 8 + (s + 1))
                for c in range(2):
                    ins = act.activation(DE[:, s % 2, c, :], PS[:, 4 + c, :], ACT.Exp, bias=NM[:, s % 2, c:c + 1],
                                         accum_out=LS[:, s % 2, c:c + 1])
                ins.then_inc(s_e5, 1)

            def weights_out(i, s):
                act.wait_ge(s_e9, i * 8 + (s + 1))
                act.copy(DPT[:, s % 2, :], PS[:, 6, :]).then_inc(s_e10, 1)

            def outputs_root(i):
                act.wait_ge(s_om, i + 1)
                act.activation(DS8, DS8, ACT.Sqrt).then_inc(s_or, 1)

            def outputs_out(i, bank):
                act.wait_ge(s_dyt, i + 1)
                for j in range(2):
                    y = DYT[:, 4 * i + 2 * j:4 * i + 2 * j + 2, :] if isinstance(i, int) else DYT[:, bass.ds(i * 4 + 2 * j, 2), :]
                    ins = act.copy(y, PS[:, bank + j, :].rearrange("p (k s) -> p k s", k=2))
                ins.then_inc(s_dye, 1)

            def qk_out(i, j):
                act.wait_ge(s_e1, i * 4 + (j + 5))
                act.copy(DQK[:, j, 0:CHUNK], PS[:, 2, :])
                act.copy(DQK[:, j, CHUNK:CHUNK + SEQ], PS[:, 3, 0:SEQ]).then_inc(s_e2, 1)

            def projections_behind(i, heads):
                take_chunk(i, 1, RQK[:, 0:4, :], 4, 0)
                att_hi(i, [20])
                if heads:
                    outputs_root(i)
                att_hi(i, [21, 22, 23])
                act.wait_ge(s_dm, i + 2)
                act.activation(DS48, DS48, ACT.Sqrt).then_inc(s_dp0, 1)
                att_hi(i, range(24, 28))
                if heads:
                    outputs_out(i, 2)
                take_chunk(i, 2, RV, 4, 4)
                att_hi(i, range(28, 32))
                for j in range(4):
                    att_hi(i, [32 + j])
                    qk_out(i, j)
                take_chunk(i, 3, RG, 2, 0, silu=True)

            att_hi(-1, range(4, 8))
            for j in range(4):
                att_hi(-1, [8 + j])
                scale_features(mod_scale(3), mod_shift(1, 1), TMP_B, 2 * j, 2)
            take_chunk(-1, 0, RQK[:, 4:6, :], 2, 0)
            att_hi(-1, range(12, 20))
            projections_behind(-1, False)
            with act.Fori(0, GROUPS - 1) as i:
                exponentials(i, 0)
                for s in range(8):
                    att_hi(i, [2 * s + 4])
                    weights_out(i, s)
                    if s < 7:
                        exponentials(i, s + 1)
                    att_hi(i, [2 * s + 5])
                    if s == 3:
                        take_chunk(i, 0, RQK[:, 4:6, :], 2, 0)
                projections_behind(i, True)

            last = GROUPS - 1
            y_hi(0, 2, DYH, DYT)
            exponentials(last, 0)
            y_hi(2, 2, DYH, DYT)
            for s in range(8):
                his("att_out", [OUT_FILL[s][0] + 4])
                weights_out(last, s)
                if s < 7:
                    exponentials(last, s + 1)
                his("att_out", [j + 4 for j in OUT_FILL[s][1:]])
                if s < OUT_AHEAD // 2 - 1:
                    y_hi(4 * s + 4, 4, DYH, DYT)
            for j in range(8, 10):
                gate_rows_out(G_ATT, j, 4 + j % 2)
            outputs_root(last)
            for j in range(10, 12):
                gate_rows_out(G_ATT, j, 4 + j % 2)
            outputs_out(last, 6)
            act.wait_ge(s_dye, GROUPS)
            y_hi(2 * OUT_AHEAD, KT - 2 * OUT_AHEAD, DYH, DYT)
            with act.Fori(2, 4) as i:
                his("att_out", range(8), i=i, per=8)

        @block.vector
        def _(dve):
            steps = [0]

            def link(ins):
                steps[0] += 1
                ins.then_inc(s_dve, 1)
                dve.wait_ge(s_dve, steps[0])

            def lo(U, n=UNIT, i=None, per=0):
                dve.wait_ge(s_hi, at(U + 1, i, per))
                dve.tensor_tensor(out=WL[:, U % SLOTS, 0:n], in0=RA[:, U % SLOTS, 0:n], in1=WH[:, U % SLOTS, 0:n].bitcast(F32),
                                  op=ALU.subtract).then_inc(s_lo, 1)

            def los(stage, units, n=UNIT, i=None, per=0):
                for u in units:
                    lo(UNIT0[stage] + u, n, i, per)

            def mean_square(r, widths):
                dve.wait_ge(s_sq, SQUARED[r])
                first = 0
                for n, width in widths:
                    ins = dve.tensor_scalar(ST[:, r, first:first + n], ST[:, r, first:first + n], 1.0 / width, EPS, ALU.mult, ALU.add)
                    first += n
                ins.then_inc(s_ms, 1)

            def mean_square_of_chunks(r, sums_of, summed):
                dve.wait_ge(s_sqc, summed)
                link(dve.tensor_reduce(ST[:, r, 0:TT], sums_of, AX, ALU.add))
                dve.tensor_scalar(ST[:, r, 0:TT], ST[:, r, 0:TT], 1.0 / D, EPS, ALU.mult, ALU.add).then_inc(s_ms, 1)

            def rstd(r, n):
                dve.wait_ge(s_rt, r + 1)
                dve.reciprocal(ST[:, r, 0:n], ST[:, r, 0:n]).then_inc(s_rs, 1)

            fills = [0]

            def split_features(dest_hi, dest_lo, tmp, first=0, count=8):
                for j in range(first, first + count):
                    q = fills[0]
                    fills[0] += 1
                    dve.wait_ge(s_tmp, q + 1)
                    src, h = tmp[:, q % 4, :], dest_hi(j)
                    if len(h.shape) == 3:
                        src = src.rearrange("p (k s) -> p k s", k=2)
                    dve.tensor_copy(h, src).then_inc(s_xh, 1)
                    dve.wait_ge(s_xh, q + 1)
                    dve.tensor_tensor(out=dest_lo(j), in0=src, in1=h.bitcast(F32), op=ALU.subtract).then_inc(s_xl, 1)

            def rope(x, table, rot, heads):
                tab = const(table).rearrange("p (t z c) -> p t z c", t=TT, z=2)
                half = rot // 2
                ra = ROT_A[:, 0:heads * rot].rearrange("p (h c) -> p h c", h=heads)
                rb = ROT_B[:, 0:heads * rot].rearrange("p (h c) -> p h c", h=heads)

                def wide(z, tt, first, end):
                    return tab[:, tt, z, first:end].unsqueeze(1).to_broadcast([P, heads, end - first])
                for tt in range(TT):
                    v = x(tt)
                    dve.tensor_tensor(out=ra, in0=v, in1=wide(0, tt, 0, rot), op=ALU.mult)
                    dve.tensor_tensor(out=rb[:, :, 0:half], in0=v[:, :, half:rot], in1=wide(1, tt, 0, half), op=ALU.mult)
                    link(dve.tensor_tensor(out=rb[:, :, half:rot], in0=v[:, :, 0:half], in1=wide(1, tt, half, rot), op=ALU.mult))
                    link(dve.tensor_tensor(out=v, in0=ra, in1=rb, op=ALU.add))
                dve.sem_inc(s_rope, 1)

            def residual_add(stage, c):
                dve.wait_ge(s_wused, multiplied(stage, c))
                for m in range(TT):
                    x = X[:, m, c * CHUNK:(c + 1) * CHUNK]
                    ins = dve.tensor_tensor(out=x, in0=PS[:, 2 * (c % 2) + m, :], in1=x, op=ALU.add)
                ins.then_inc(s_re, 1)

            def mod_rows(stage, rows, i=None, units=8, bank=0):
                dve.wait_ge(s_wused, at(UNIT0[stage] + units, i, 8))
                dve.tensor_copy(rows[0:4, :], PS[0:4, bank, :]).then_inc(s_mods, 1)

            def mod_columns(m, layer, c, i=None, bank=1):
                dve.wait_ge(s_modt, at(m + 1, i, 1))
                first = at(4 * c, i, 4)
                bias = GT[:, bass.ds(first + (VEC_AT["mod_b_2"] + 48 * layer), 4)]
                to = MODT[:, layer, bass.ds(first, 4), :]
                rows = PS[:, bank, :].rearrange("p (k w) -> p k w", w=P)
                dve.tensor_tensor(out=to, in0=rows[:, :, 0:2], in1=bias.unsqueeze(2).to_broadcast([P, 4, 2]), op=ALU.add).then_inc(s_modb, 1)
                dve.wait_ge(s_modb, at(m + 1, i, 1))
                dve.tensor_tensor(out=to, in0=rows[:, :, 2:4], in1=to, op=ALU.add).then_inc(s_modd, 1)

            def head_loop(h):
                H = HE if h in EV_LOOPS else HO

                def modulation_lo(i, units):
                    for u in units:
                        U = UNIT0["mod_" + h.name] + u
                        if u < 8 and LO_BY[U][0]:
                            continue
                        if isinstance(i, int):
                            lo(U + 8 * i)
                        else:
                            lo(U, UNIT, i, 8)

                def turn(i):
                    n = lambda a, plus: i * 2 + (h.n0 + a + plus)
                    pair = h.kind == "swa"
                    for a in range(2):
                        dve.wait_ge(s_sc, n(a, 1))
                        flat = S[:, a, :, :].rearrange("p t c -> p (t c)")
                        if h.mask is None:
                            ins = dve.tensor_scalar(flat, PS[:, 6 + a, :], h.scale, None, ALU.mult)
                        else:
                            ins = dve.scalar_tensor_tensor(out=flat, in0=PS[:, 6 + a, :], scalar=h.scale, in1=const(h.mask),
                                                           op0=ALU.mult, op1=ALU.add)
                        ins.then_inc(s_sm, 1)
                        dve.wait_ge(s_sm, n(a, 1))
                        ins = dve.tensor_reduce(NM[:, a, :], S[:, a, :, :], AX, ALU.max, negate=True)
                        if pair:
                            ins.then_inc(s_sk, 1)
                            w = i * 2 + (h.sink + a + 1)
                            dve.wait_ge(s_sk, w)
                            nsink = NSINK[:, bass.ds(i * 2 + (h.sink + a), 1), :].squeeze(1)
                            dve.tensor_tensor(out=NM[:, a, :], in0=NM[:, a, :], in1=nsink, op=ALU.min).then_inc(s_sk2, 1)
                            dve.wait_ge(s_sk2, w)
                            ins = dve.tensor_tensor(out=SN[:, a, :], in0=NM[:, a, :], in1=nsink, op=ALU.subtract)
                        ins.then_inc(s_mx, 1)
                    modulation_lo(i, range(4, 6))
                    for a in range(2):
                        dve.wait_ge(s_pt, n(a, 1))
                        dve.tensor_copy(PT[:, a, :], PS[:, 4 + a, :]).then_inc(s_pe, 1)
                    modulation_lo(i, range(6, 9))
                    for a in range(2):
                        dve.wait_ge(s_o, n(a, 1))
                        if pair:
                            dve.tensor_tensor(out=LS[:, a, :], in0=LS[:, a, :], in1=ES[:, a, :], op=ALU.add).then_inc(s_l2, 1)
                            dve.wait_ge(s_l2, i * 2 + (h.sink + a + 1))
                        dve.reciprocal(RL[:, a, :], LS[:, a, :]).then_inc(s_rl, 1)
                        dve.wait_ge(s_rl, n(a, 1))
                        w = SWA_DH if pair else P
                        for tt in range(TT):
                            y = YS[:, 0, tt, a * w:(a + 1) * w] if pair else YS[:, a, tt, :]
                            gate = H[:, tt, bass.ds(i * (2 * w) + (h.gate + a * w), w)]
                            ins = dve.scalar_tensor_tensor(out=y, in0=PS[:, 6 + a, tt * P:tt * P + w], scalar=RL[:, a, tt:tt + 1],
                                                           in1=gate, op0=ALU.mult, op1=ALU.mult)
                        ins.then_inc(s_ys, 1)
                    mod_rows("mod_" + h.name, MODS_EV if h in EV_LOOPS else MODS_OD, i)
                    modulation_lo(i, range(9, 11))
                    for a in range(1 if pair else 2):
                        dve.wait_ge(s_yh, n(1 if pair else a, 1))
                        y = bass.ds(i * SEQ + h.y0 * SEQ if pair else i * (2 * SEQ) + (h.y0 + a) * SEQ, SEQ)
                        dve.tensor_tensor(out=ATL[:, y], in0=PS[:, 4 + a, 0:SEQ], in1=ATH[:, y].bitcast(F32),
                                          op=ALU.subtract).then_inc(s_ye, 2 if pair else 1)
                    mod_columns(h.mod0, h.mod_layer, h.mod_chunk0, i)
                    modulation_lo(i, [11])
                with dve.Fori(0, h.turns - 1) as i:
                    turn(i)
                turn(h.turns - 1)

            dve.wait_ge(s_vt, 1)
            for v, rows in enumerate(VEC_ROWS):
                dve.tensor_copy(GT[:, VEC_COL[v]:VEC_COL[v] + rows], PS[:, 0, v * P:v * P + rows]).then_inc(s_vec, 1)
            dve.sem_inc(s_modd, 1)
            link(dve.memset(MODS_EV, 0.0))
            dve.sem_inc(s_ye, 2)
            dve.wait_ge(s_vec, 4)
            los("mkv0", range(0, 4))
            x_hi = lambda j: ATH[:, j * 2 * SEQ:(j + 1) * 2 * SEQ]
            x_lo = lambda j: ATL[:, j * 2 * SEQ:(j + 1) * 2 * SEQ]
            mem_hi = lambda j: M1H[:, j * 2 * SEQ:(j + 1) * 2 * SEQ]
            mem_lo = lambda j: M1L[:, j * 2 * SEQ:(j + 1) * 2 * SEQ]
            split_features(x_hi, x_lo, TMP_X)
            split_features(mem_hi, mem_lo, TMP_X, 0, 4)
            los("mkv0", range(4, 8))
            mean_square(0, [(2, D)])
            mean_square(1, [(2, D)])
            rstd(0, 2)
            rstd(1, 2)
            dve.memset(CS[:, 4 * KT:].bitcast(F32), 0.0)
            dve.wait_ge(s_cond, 2)
            dve.tensor_tensor(out=CSV[:, :, 2:4], in0=COND, in1=CSV[:, :, 0:2].bitcast(F32), op=ALU.subtract).then_inc(s_cs, 1)

            lam = vec("lru_lambda_2", 0, 32)
            dve.wait_ge(s_bc, 16 * N_CONST_BC)
            link(dve.tensor_scalar(SC[:, 32:64], lam, -1.0, None, ALU.mult))
            dve.tensor_tensor(out=SC[:, 0:32], in0=lam, in1=SC[:, 32:64], op=ALU.max)
            dve.tensor_tensor(out=LVP[:, 0:64], in0=LV[:, 0:64], in1=LV[:, 64:128], op=ALU.mult)
            link(dve.tensor_tensor(out=LVP[:, 64:128], in0=LV[:, 128:192], in1=LV[:, 192:256], op=ALU.mult))
            dve.tensor_reduce(SC[:, 64:66], LVP.rearrange("p (z c) -> p z c", z=2), AX, ALU.add).then_inc(s_lam, 1)
            los("mkv0", range(8, 12))
            split_features(mem_hi, mem_lo, TMP_X, 4, 4)
            los("mkv0", range(12, 16))
            los("mkv1", range(0, 4))
            split_features(x_hi, x_lo, TMP_X, 0, 4)
            los("mkv1", range(4, 8))
            dve.wait_ge(s_exl, 1)
            link(dve.tensor_tensor(out=SC[:, 66:67], in0=SC[:, 65:66], in1=SC[:, 64:65], op=ALU.subtract))
            link(dve.tensor_scalar(NLAM, SC[:, 66:67], -LAM_INIT, None, ALU.add))
            dve.tensor_scalar(SUBG, SUBG, 1.0 - LAM_INIT, None, ALU.mult)
            dve.tensor_scalar(QG, QG, ATT_DH ** -0.5, None, ALU.mult)
            dve.tensor_scalar(NSINK, SINK.unsqueeze(2).to_broadcast([P, SWA_HEADS, 2]), -1.0, None, ALU.mult)
            y, z, z2, acc = SC[:, 0:32], SC[:, 68:100], SC[:, 100:132], SC[:, 132:164]
            link(dve.tensor_scalar(z, y, 2.0, None, ALU.add))
            link(dve.reciprocal(z, z))
            link(dve.tensor_tensor(out=z, in0=z, in1=y, op=ALU.mult))
            link(dve.tensor_tensor(out=z2, in0=z, in1=z, op=ALU.mult))
            link(dve.tensor_scalar(acc, z2, 1.0 / 19, 1.0 / 17, ALU.mult, ALU.add))
            for k in range(15, 0, -2):
                link(dve.tensor_tensor(out=acc, in0=acc, in1=z2, op=ALU.mult))
                link(dve.tensor_scalar(acc, acc, 1.0 / k, None, ALU.add))
            link(dve.tensor_tensor(out=acc, in0=acc, in1=z, op=ALU.mult))
            link(dve.tensor_scalar(z, SC[:, 32:64], 0.0, None, ALU.max))
            link(dve.scalar_tensor_tensor(out=acc, in0=acc, scalar=2.0, in1=z, op0=ALU.mult, op1=ALU.add))
            link(dve.memset(LTAB[:], 0.0))
            for first, n, src in ((0, 4, vec("lru_conv_w_2", 0, 64)), (4, 1, vec("lru_conv_b_2", 0, 16)), (5, 4, vec("lru_gate_b_2", 0, 64))):
                dve.tensor_copy(LTAB[:, 0:KT, first:first + n], src.rearrange("p (j k) -> p k j", j=n))
            link(dve.tensor_scalar(LTAB[:, 0:KT, 9:11], acc.rearrange("p (d k) -> p k d", d=2), -LRU_C, None, ALU.mult))
            dve.sem_inc(s_ltab, 1)

            los("mkv1", range(8, 12))
            split_features(x_hi, x_lo, TMP_X, 4, 4)
            los("mkv1", range(12, 16))
            los("ev_a", range(8))
            los("ev_a", range(8, 16), 2 * (EV_LAT - EV_CKV))
            los("ev_b", range(8))
            dve.wait_ge(s_consta, 16)
            dve.wait_ge(s_ge, CHUNK0["ev_b"])
            rope(lambda tt: HQ[:, tt, EV_KPE:EV_KPE + ROPE].unsqueeze(1), "mla", ROPE, 1)
            los("ev_b", range(8, 20))
            mean_square(2, [(2, MLA_QR), (2, MLA_KVR)])
            dve.wait_ge(s_kpe, 1)
            dve.tensor_copy(KPT[0:ROPE, :], PS[0:ROPE, 7, 0:SEQ]).then_inc(s_kpt, 1)
            los("ev_b", range(20, 24))
            rstd(2, 4)
            with dve.Fori(3, 6) as i:
                los("ev_b", range(8), i=i, per=8)
            dve.wait_ge(s_ge, CHUNK0["ev_b"] + 4)
            rope(lambda tt: HE[:, tt, EV_QKV:EV_QKV + 2048].rearrange("p (h c) -> p h c", c=DH)[:, :, 0:32], "r32", 32, 16)
            with dve.Fori(6, 12) as i:
                los("ev_b", range(8), i=i, per=8)
            los("mod_mem_ev", range(0, 4))
            dve.wait_ge(s_wused, multiplied("ev_b", 11))
            split_features(x_hi, x_lo, TMP_LAT, 0, 3)
            dve.wait_ge(s_ge, CHUNK0["uq"])
            head_loop(MEM_EV)
            head_loop(MOBA)
            los("uq", range(4, 6))
            los("ukv", range(4))
            dve.wait_ge(s_ge, CHUNK0["ukv"])
            rope(lambda tt: HE[:, tt, EV_QA:EV_KVA].rearrange("p (h c) -> p h c", c=NOPE + ROPE)[:, :, NOPE:NOPE + ROPE],
                 "mla", ROPE, MLA_HEADS)
            los("mod_mla", range(4))
            head_loop(MLA)
            link(dve.memset(MODS_OD, 0.0))
            for c in range(4):
                if c:
                    los("ev_out", range(10 * c, 10 * c + 4))
                    residual_add("ev_out", c - 1)
                los("ev_out", range(10 * c + 4, 10 * c + 10))

            los("od_b", range(0, 4))
            residual_add("ev_out", 3)
            split_features(x_hi, x_lo, TMP_X)
            mean_square(3, [(2, D)])
            rstd(3, 2)
            los("od_b", range(4, 8))
            with dve.Fori(1, 8) as i:
                los("od_b", range(8), i=i, per=8)
            dve.wait_ge(s_ge, CHUNK0["od_b"] + 6)
            rope(lambda tt: HO[:, tt, 0:OD_VC].rearrange("p (h c) -> p h c", c=SWA_DH)[:, :, 0:16], "r16", 16, 18)
            rope(lambda tt: HO[:, tt, OD_QD:OD_VD].rearrange("p (h c) -> p h c", c=DH)[:, :, 0:32], "r32", 32, 12)
            with dve.Fori(8, 12) as i:
                los("od_b", range(8), i=i, per=8)
            for u in range(16):
                los("od_c", [u], UNIT if u % 2 else 2 * (OD_IN % CHUNK))
            mod_rows("od_c", MODS_OD, None, 16, 4)
            mod_columns(MOD_ALONE, 1, 11, None, 5)
            los("mod_swa0", range(4))
            dve.wait_ge(s_ge, CHUNK0["od_c"] + 1)
            for h in OD_LOOPS:
                head_loop(h)
            dve.wait_ge(s_modd, N_MOD + 1)
            for l in range(2):
                for w in range(2):
                    j = 2 * l + w
                    dve.scalar_tensor_tensor(out=MSC[:, 16 * j:16 * j + 16], in0=MODT[:, l, KT:2 * KT, w], scalar=1.0,
                                             in1=vec("norm_g_2", 16 * l, 16), op0=ALU.add, op1=ALU.mult).then_inc(s_msc, 1)

            def normalized(dest, rows, r):
                dve.wait_ge(s_rs, r + 1)
                for tt in range(TT):
                    ins = dve.tensor_scalar(dest[:, tt, :], rows[:, tt, :], ST[:, r, tt:tt + 1], None, ALU.mult)
                ins.then_inc(s_xn, 1)

            los("od_out", range(4, 13))
            residual_add("od_out", 0)
            los("od_out", range(13, 18))
            mean_square(4, [(2, D)])
            los("od_out", range(18, 22))
            residual_add("od_out", 1)
            rstd(4, 2)
            normalized(CN, CX, 4)
            los("od_out", range(22, 31))
            residual_add("od_out", 2)
            los("od_out", range(31, 36))
            residual_add("od_out", 3)

            mean_square_of_chunks(5, SQX, 4 * TT)
            rstd(5, 2)
            dve.wait_ge(s_rs, 6)
            dve.wait_ge(s_fg, 16)
            for tt in range(TT):
                ins = dve.scalar_tensor_tensor(out=X[:, tt, :], in0=X[:, tt, :], scalar=ST[:, 5, tt:tt + 1], in1=FG,
                                               op0=ALU.mult, op1=ALU.mult)
                ins.then_inc(s_xf, 1)
            part = lambda T, c: (lambda j: T[:, 2 * j:2 * j + 2, c * SEQ:(c + 1) * SEQ])
            split_features(part(FTH, 0), part(FTL, 0), TMP_B)
            mean_square(6, [(2, D)])
            rstd(6, 2)
            normalized(XN, X, 6)
            split_features(part(FTH, 1), part(FTL, 1), TMP_B)
            dve.memset(ONES, 1.0)

            def conv(n, b):
                dve.wait_ge(s_wused, n(0) * 4 + (UNIT0["lru_in"] + 2))
                dve.wait_ge(s_bv, n(1))
                u = PS[:, b, :].rearrange("p (c s) -> p c s", c=2)
                xc = XC[:, b, :, :]
                taps = BV[:, b, :]
                dve.tensor_scalar(xc, u, taps[:, 2:3], taps[:, 4:5], ALU.mult, ALU.add).then_inc(s_cv, 1)
                for step, (j, first, end) in enumerate(((0, 2, SEQ), (1, 1, SEQ), (3, 0, SEQ - 1))):
                    dve.wait_ge(s_cv, n(0) * 3 + (step + 1))
                    ins = dve.scalar_tensor_tensor(out=xc[:, :, first:end], in0=u[:, :, first + j - 2:end + j - 2], scalar=taps[:, j:j + 1],
                                                   in1=xc[:, :, first:end], op0=ALU.mult, op1=ALU.add)
                    ins.then_inc(s_cv if step < 2 else s_xc, 1)

            def decays(n, b):
                dve.wait_ge(s_ab, n(1))
                dve.tensor_tensor(out=LTMP, in0=LAF, in1=LAF, op=ALU.mult).then_inc(s_w2a, 1)
                dve.wait_ge(s_w2a, n(1))
                dve.scalar_tensor_tensor(out=LWF, in0=LTMP, scalar=1.0, in1=LWF, op0=ALU.add, op1=ALU.mult).then_inc(s_w2, 1)
                dve.tensor_tensor(out=SG, in0=PS[:, 2 + b, :], in1=SG, op=ALU.mult).then_inc(s_gs, 1)

            def recur(n):
                dve.wait_ge(s_sqr, n(1))
                dve.wait_ge(s_ix, n(1))
                dve.tensor_tensor(out=LW[:], in0=LW[:], in1=RI[:, 1::2, :], op=ALU.mult).then_inc(s_b, 1)
                dve.wait_ge(s_b, n(1))
                scan = lambda h, first, end, step, h0: dve.tensor_tensor_scan(
                    out=HSC[:, h, first:end][:, ::step], data0=LA[:, h, first:end][:, ::step], data1=LW[:, h, first:end][:, ::step],
                    initial=h0, op0=ALU.mult, op1=ALU.add)
                scan(0, 0, 2 * SEQ, 1, 0.0)
                scan(1, 0, SEQ, -1, 0.0).then_inc(s_sn, 1)
                dve.wait_ge(s_sn, n(0) * 2 + 1)
                scan(1, SEQ, 2 * SEQ, -1, HSC[:, 1, 0:1]).then_inc(s_sn, 1)
                dve.wait_ge(s_sn, n(0) * 2 + 2)
                dve.tensor_tensor(out=HSC[:, 0, :], in0=HSC[:, 0, :], in1=HSC[:, 1, :], op=ALU.add).then_inc(s_hsum, 1)
                dve.wait_ge(s_hsum, n(1))
                y = YL[:, n(0), :] if isinstance(n(0), int) else YL[:, bass.ds(n(0), 1), :].squeeze(1)
                dve.tensor_tensor(out=y, in0=HSC[:, 0, :], in1=SG, op=ALU.mult).then_inc(s_y, 1)

            def y_lo(first, count, dest_hi, dest_lo, src, base):
                for k in range(first, first + count):
                    dve.wait_ge(s_yhi, base + k + 1)
                    dve.tensor_tensor(out=dest_lo[:, k, :], in0=src[:, k, :], in1=dest_hi[:, k, :].bitcast(F32),
                                      op=ALU.subtract).then_inc(s_ylo, 1)

            def block_n(b, i=None):
                return lambda plus: b + plus if i is None else i * 2 + (b + plus)
            for s, n in ((s_xc, 2), (s_gs, 2), (s_y, 2)):
                dve.sem_inc(s, n)
            conv(block_n(0), 0)
            with dve.Fori(0, KT // 2 - 1) as i:
                for b in range(2):
                    decays(block_n(b, i), b)
                    conv(block_n(b + 1, i), 1 - b)
                    recur(block_n(b, i))
            decays(block_n(KT - 2), 0)
            conv(block_n(KT - 1), 1)
            recur(block_n(KT - 2))
            los("lru_out", range(0, 4))
            y_lo(0, 4, FTH, FTL, YL, 0)
            decays(block_n(KT - 1), 1)
            recur(block_n(KT - 1))
            y_lo(4, KT - 5, FTH, FTL, YL, 0)
            los("lru_out", range(4, 6))
            y_lo(KT - 1, 1, FTH, FTL, YL, 0)

            def gate_diagonals(j, layer, w):
                if j >= 2:
                    dve.wait_ge(s_gb, j - 1)
                for k in range(4):
                    ins = dve.tensor_scalar(DIAG(j)[:, k, :], ident, MODT[:, layer, 2 * KT + 4 * (j % 4) + k, w:w + 1], None, ALU.mult)
                ins.then_inc(s_dg, 1)

            def gated_residual(stage, c, used, tiles, gates, bank, rows, scratch, again=0):
                cols = slice(c * CHUNK, (c + 1) * CHUNK)
                q = RES0[stage] + c + again
                dve.wait_ge(s_wused, used)
                dve.wait_ge(s_gbe, rows)
                dve.wait_ge(s_re, q)
                for m in range(len(tiles)):
                    ins = dve.tensor_tensor(out=scratch[:, m * CHUNK:(m + 1) * CHUNK], in0=PS[:, bank + m, :], in1=gates[m][:, cols], op=ALU.mult)
                ins.then_inc(s_rh, 1)
                dve.wait_ge(s_rh, q + 1 - RES0["lru_out"])
                for m in range(len(tiles)):
                    x = tiles[m][:, cols]
                    ins = dve.tensor_tensor(out=x, in0=scratch[:, m * CHUNK:(m + 1) * CHUNK], in1=x, op=ALU.add)
                ins.then_inc(s_re, 1)

            def lru_residual(c, first=0, count=4, again=0):
                tiles = [CX[:, 0, :], CX[:, 1, :], X[:, 0, :], X[:, 1, :]][first:first + count]
                gated_residual("lru_out", c, multiplied("lru_out", c), tiles, [G_CTX, G_CTX, G_LAT, G_LAT][first:first + count],
                               4 * ((c + 1) % 2) + first, 8, BUF[:, 0:2048], again)
            for j in range(2):
                gate_diagonals(j, 0, 0)
            los("lru_out", range(6, 12))
            for j in range(2, 8):
                gate_diagonals(j, 0, j // 4)
            dve.wait_ge(s_cx2, 16)
            lru_residual(0)
            los("lru_out", range(12, 16))
            for c in range(2, 4):
                los("lru_out", range(8 * c, 8 * c + 4))
                lru_residual(c - 1)
                los("lru_out", range(8 * c + 4, 8 * c + 8))
            los("att_in", range(0, 4))
            lru_residual(3, 2, 2)

            mean_square_of_chunks(7, SQL, 8 * TT + 3 * TT)
            lru_residual(3, 0, 2, 1)
            rstd(7, 2)
            normalized(XN, X, 7)
            mean_square_of_chunks(8, SQC, 12 * TT)
            split_features(part(FTH, 1), part(FTL, 1), TMP_B)
            rstd(8, 2)
            normalized(CN, CX, 8)
            axial = const("axial").rearrange("p (t z a y f) -> p t z a y f", t=TT, z=2, a=2, y=2)
            PER_HEADS, PER_TAIL, PER_PREP = 8 * 3, 5, 12

            def linker(s, i, per):
                done = [0]

                def link(ins):
                    done[0] += 1
                    ins.then_inc(s, 1)
                    dve.wait_ge(s, i * per + done[0])
                return link, done

            def att_lo(i, units):
                for u in units:
                    lo(UNIT0["att_in"] + 32 + u if not isinstance(i, int) else UNIT0["att_in"] + 32 * (i + 1) + u, UNIT,
                       None if isinstance(i, int) else i, 32)

            def maxima(i, s):
                dve.wait_ge(s_e3, i * 8 + (s + 1))
                dve.tensor_reduce(NM[:, s % 2, :], PS[:, 4:6, :], AX, ALU.max, negate=True).then_inc(s_e4, 1)

            def combine(i, s, link):
                a = s % 2
                dve.wait_ge(s_e5, i * 8 + (s + 1))
                link(dve.reciprocal(RL[:, a, :], LS[:, a, :]))
                link(dve.tensor_tensor(out=RL[:, a, 1:2], in0=RL[:, a, 1:2], in1=NLAM, op=ALU.mult))
                link(dve.tensor_scalar(DE[:, a, 1, :], DE[:, a, 1, :], RL[:, a, 1:2], None, ALU.mult))
                dve.scalar_tensor_tensor(out=DE[:, a, 0, :], in0=DE[:, a, 0, :], scalar=RL[:, a, 0:1], in1=DE[:, a, 1, :],
                                         op0=ALU.mult, op1=ALU.add).then_inc(s_e8, 1)

            def output(i, s):
                dve.wait_ge(s_e11, i * 8 + (s + 1))
                dve.tensor_copy(OS[:, s % 2, s // 2 * P:(s // 2 + 1) * P], PS[:, 7, 0:P]).then_inc(s_oe, 1)

            oflat = OS[:].rearrange("p t c -> p (t c)")
            oh = oflat.rearrange("p (g c) -> p g c", c=P)

            def outputs_square(i, link):
                dve.wait_ge(s_oe, i * 8 + 8)
                link(dve.tensor_tensor(out=DSQ[:, 0:1024], in0=oflat, in1=oflat, op=ALU.mult))
                link(dve.tensor_reduce(DS8, DSQ[:, 0:1024].rearrange("p (g c) -> p g c", c=P), AX, ALU.add))
                dve.tensor_scalar(DS8, DS8, 1.0 / P, EPS, ALU.mult, ALU.add).then_inc(s_om, 1)

            def outputs_gate(i, link):
                dve.wait_ge(s_or, i + 1)
                link(dve.reciprocal(DS8, DS8))
                link(dve.tensor_tensor(out=oh, in0=oh, in1=DS8.unsqueeze(2).to_broadcast([P, 8, P]), op=ALU.mult))
                link(dve.tensor_tensor(out=oh, in0=oh, in1=SUBG.unsqueeze(1).to_broadcast([P, 8, P]), op=ALU.mult))
                dve.tensor_tensor(out=oflat, in0=oflat, in1=RG[:].rearrange("p t c -> p (t c)"), op=ALU.mult).then_inc(s_oy, 1)

            flat = RQK[:].rearrange("p t c -> p (t c)")
            by64 = flat.rearrange("p (g c) -> p g c", c=ATT_DH)

            def qk_square(i, link):
                dve.wait_ge(s_dqe, i * 4 + 6)
                link(dve.tensor_tensor(out=DSQ, in0=flat, in1=flat, op=ALU.mult))
                link(dve.tensor_reduce(DS48, DSQ.rearrange("p (g c) -> p g c", c=ATT_DH), AX, ALU.add))
                dve.tensor_scalar(DS48, DS48, 1.0 / ATT_DH, EPS, ALU.mult, ALU.add).then_inc(s_dm, 1)

            def qk_normalize(i, link):
                dve.wait_ge(s_dp0, i + 2)
                link(dve.reciprocal(DS48, DS48))
                link(dve.tensor_tensor(out=by64, in0=by64, in1=DS48.unsqueeze(2).to_broadcast([P, 48, ATT_DH]), op=ALU.mult))

            def qk_gain(link):
                dve.tensor_tensor(out=by64[:, 0:32, :], in0=by64[:, 0:32, :], in1=KG.unsqueeze(1).to_broadcast([P, 32, ATT_DH]), op=ALU.mult)
                link(dve.tensor_tensor(out=by64[:, 32:48, :], in0=by64[:, 32:48, :], in1=QG.unsqueeze(1).to_broadcast([P, 16, ATT_DH]), op=ALU.mult))

            def qk_rotate(tile, link):
                x = RQK[:, tile, :]
                cos = axial[:, tile % 2, 0].rearrange("p a y f -> p (a y f)").unsqueeze(1).to_broadcast([P, 8, ATT_DH])
                parts = lambda v: v.rearrange("p (h a y f) -> p h a y f", h=8, a=2, y=2)
                dve.tensor_tensor(out=DT1.rearrange("p (h c) -> p h c", h=8), in0=x.rearrange("p (h c) -> p h c", h=8), in1=cos, op=ALU.mult)
                for y in range(2):
                    sin = axial[:, tile % 2, 1, :, y, :].unsqueeze(1).to_broadcast([P, 8, 2, 16])
                    ins = dve.tensor_tensor(out=parts(DT2)[:, :, :, y, :], in0=parts(x)[:, :, :, 1 - y, :], in1=sin, op=ALU.mult)
                link(ins)
                ins = dve.tensor_tensor(out=x, in0=DT1, in1=DT2, op=ALU.add)
                if tile < 5:
                    link(ins)
                else:
                    ins.then_inc(s_qn, 1)

            def projections_behind(i, heads):
                att_lo(i, [20])
                if heads:
                    link, done = linker(s_tstep, i, PER_TAIL)
                    outputs_square(i, link)
                att_lo(i, [21])
                if heads:
                    outputs_gate(i, link)
                    assert done[0] == PER_TAIL
                att_lo(i, [22])
                link, done = linker(s_pstep, i + 1, PER_PREP)
                qk_square(i, link)
                att_lo(i, [23])
                qk_normalize(i, link)
                att_lo(i, [24])
                qk_gain(link)
                att_lo(i, [25])
                qk_rotate(2, link)
                qk_rotate(3, link)
                att_lo(i, [26])
                qk_rotate(4, link)
                att_lo(i, [27])
                qk_rotate(5, link)
                assert done[0] == PER_PREP
                att_lo(i, range(28, 36))

            att_lo(-1, range(4, 8))
            for j in range(4):
                att_lo(-1, [8 + j])
                split_features(part(FTH, 0), part(FTL, 0), TMP_B, 2 * j, 2)
            att_lo(-1, range(12, 20))
            projections_behind(-1, False)
            with dve.Fori(0, GROUPS - 1) as i:
                link, done = linker(s_dstep, i, PER_HEADS)
                maxima(i, 0)
                combine(i, 0, link)
                for s in range(8):
                    att_lo(i, [2 * s + 4])
                    if s < 7:
                        maxima(i, s + 1)
                        combine(i, s + 1, link)
                    att_lo(i, [2 * s + 5])
                    output(i, s)
                assert done[0] == PER_HEADS
                projections_behind(i, True)

            last = GROUPS - 1
            link, done = linker(s_dstep, last, PER_HEADS)
            maxima(last, 0)
            y_lo(0, 2, DYH, DYL, DYT, KT)
            combine(last, 0, link)
            y_lo(2, 2, DYH, DYL, DYT, KT)
            for s in range(8):
                los("att_out", [OUT_FILL[s][0] + 4])
                if s < 7:
                    maxima(last, s + 1)
                    combine(last, s + 1, link)
                los("att_out", [j + 4 for j in OUT_FILL[s][1:]])
                if s < OUT_AHEAD // 2 - 1:
                    y_lo(4 * s + 4, 4, DYH, DYL, DYT, KT)
                output(last, s)
                if s == 2:
                    dve.wait_ge(s_e2, 4 * GROUPS)
                if s in (2, 3):
                    gate_diagonals(8 + s - 2, 1, 0)
            link, done = linker(s_tstep, last, PER_TAIL)
            outputs_square(last, link)
            for j in range(10, 12):
                gate_diagonals(j, 1, 0)
            outputs_gate(last, link)
            y_lo(2 * OUT_AHEAD, KT - 2 * OUT_AHEAD, DYH, DYL, DYT, KT)

            def att_residual(c):
                gated_residual("att_out", c, UNIT0["att_out"] + OUT_DONE[c], [X[:, 0, :], X[:, 1, :]], [G_ATT, G_ATT], 2 * (c % 2), 12,
                               BUF[:, 13312:14336])
            los("att_out", range(16, 18))
            att_residual(0)
            los("att_out", range(18, 20))
            att_residual(1)
            los("att_out", range(20, 28))
            att_residual(2)
            los("att_out", range(28, 32))
            att_residual(3)

        @block.gpsimd
        def _(pool):
            def stage_heads(h):
                H = HE if h in EV_LOOPS else HO
                wq = NOPE + ROPE if h.kind == "mla" else P
                wk = NOPE + MLA_DV if h.kind == "mla" else P
                with pool.Fori(0, h.turns) as i:
                    pair = h.kind == "swa"
                    for a in range(1 if pair else 2):
                        pool.wait_ge(s_t1, i * 2 + (h.n0 + (1 if pair else a) + 1))
                        q = H[:, :, bass.ds(i * (P if pair else 2 * wq) + (h.q + a * wq), wq)]
                        pool.tensor_copy(QS[:, a, :, 0:wq], q)
                        if pair:
                            for z in range(2):
                                ins = pool.tensor_copy(KS[:, a, :, 64 * z:64 * z + 64], H[:, :, h.k:h.k + SWA_DH])
                        elif h.mem is not None:
                            ins = pool.tensor_copy(KS[:, a, :, :], MKV[:, h.mem, :, bass.ds(i * 256 + (h.k + a * P), P)])
                        else:
                            ins = pool.tensor_copy(KS[:, a, :, :], H[:, :, bass.ds(i * (2 * wk) + (h.k + a * wk), P)])
                        ins.then_inc(s_stg, 2 if pair else 1)
                    for u in range(8):
                        if LO_BY[UNIT0["mod_" + h.name] + u][0]:
                            weights_lo(UNIT0["mod_" + h.name] + u, i)

            def weights_lo(U, i=None):
                pool.wait_ge(s_hi, at(U + 1, i, 8))
                pool.tensor_tensor(out=WL[:, U % SLOTS, :], in0=RA[:, U % SLOTS, :], in1=WH[:, U % SLOTS, :].bitcast(F32),
                                   op=ALU.subtract).then_inc(s_lop, 1)

            pool.wait_ge(s_ge, CHUNK0["ev_b"] + 7)
            pool.wait_ge(s_kpt, 1)
            pool.wait_ge(s_ms, 3)
            stage_heads(MEM_EV)
            pool.wait_ge(s_rope, 2)
            stage_heads(MOBA)
            pool.wait_ge(s_ge, CHUNK0["ukv"] + 1)
            pool.wait_ge(s_rope, 3)
            stage_heads(MLA)
            pool.wait_ge(s_ge, CHUNK0["od_b"] + 6)
            pool.wait_ge(s_rope, 5)
            for h in OD_LOOPS:
                stage_heads(h)

            def block_vectors(b, n):
                pool.tensor_copy(BV[:, b, :], LTAB[:, n, :] if isinstance(n, int) else LTAB[:, bass.ds(n, 1), :].squeeze(1)).then_inc(s_bv, 1)

            def lru_ix(b, i=None):
                pool.wait_ge(s_sg, at(b + 2, i, 2))
                for d in range(2):
                    ins = pool.tensor_tensor(out=RI[:, 2 * d + 1, :], in0=RI[:, 2 * d + 1, :],
                                             in1=XC[:, b % 2, :, :].rearrange("p c s -> p (c s)"), op=ALU.mult)
                ins.then_inc(s_ix, 1)

            pool.wait_ge(s_ltab, 1)
            for b in range(2):
                block_vectors(b, b)
            for b in range(2):
                for u in range(4):
                    weights_lo(UNIT0["lru_in"] + 4 * b + u)
            with pool.Fori(0, KT // 2 - 1) as i:
                for b in range(2):
                    lru_ix(b, i)
                    for u in range(4):
                        weights_lo(UNIT0["lru_in"] + 4 * b + 8 + u, i)
                    pool.wait_ge(s_y, i * 2 + (b + 3))
                    block_vectors(b, i * 2 + (b + 2))
            lru_ix(KT - 2)
            lru_ix(KT - 1)


_INS = ("x", "mem", "ev_norm_g", "ev_w_in", "ev_q_norm_g", "ev_w_uq", "ev_kv_norm_g", "ev_w_ukv", "ev_mem_norm_g",
        "ev_w_mem_kv", "ev_w_out", "od_norm_g", "od_w_in", "od_sinks", "od_mem_norm_g", "od_w_mem_kv", "od_w_out",
        "final_norm_g", "c_2", "ctx_2", "c_ctx_2", "mod_w_2", "mod_b_2", "norm_g_2", "lru_w_in_2", "lru_conv_w_2",
        "lru_conv_b_2", "lru_gate_w_2", "lru_gate_b_2", "lru_lambda_2", "lru_w_out_2", "att_w_in_2", "att_q_norm_2",
        "att_k_norm_2", "att_lambda_2", "att_subln_2", "att_w_out_2")


def kernel(**inputs):
    import concourse.bacc as bacc
    from concourse.bass_utils import run_bass_kernel_spmd

    nc = bacc.Bacc("TRN2", target_bir_lowering=False, num_devices=1)
    arrays, args = {}, {}
    for name in _INS:
        a = np.ascontiguousarray(inputs[name])
        arrays[f"in_{name}"] = a
        args[name] = nc.dram_tensor(f"in_{name}", a.shape, mybir.dt.from_np(a.dtype), kind="ExternalInput").ap()
    arrays["shape_constants"] = shape_constants()
    consts = nc.dram_tensor("shape_constants", (P, NCONST), F32, kind="ExternalInput").ap()
    out = nc.dram_tensor("out", (1, SEQ, D), F32, kind="ExternalOutput").ap()
    build(nc, args, consts, out)
    return run_bass_kernel_spmd(nc, [arrays], core_ids=[0]).results[0]["out"]
```
